# Optimizing a Trainium2 kernel written in Bass

```python
import math
import jax, jax.numpy as jnp
from jax import lax
import numpy as np

D_MODEL = 2048
BATCH = 1
SEQ = 256
DEPTH = 2

EPS = 1e-6
NEG = -1e30
F32 = jnp.float32

A_HEADS = 8
A_HEAD_DIM = 128
A_BLOCK = 256
A_TOPK = 3
A_QCHUNK = 64
T5_BUCKETS = 32
T5_MAX_DIST = 128
B_HEADS = 4
B_QK_DIM = 128
B_V_DIM = 256
B_CONV = 4
B_CHUNK = 64
C_HEADS = 8
C_Q_RANK = 512
C_KV_RANK = 256
C_NOPE = 128
C_ROPE = 64
C_V_DIM = 128
C_QBLOCK = 128
ROPE_THETA = 10000.0

A_W = A_HEADS * A_HEAD_DIM
B_QK_W = B_HEADS * B_QK_DIM
B_V_W = B_HEADS * B_V_DIM
C_W = C_HEADS * C_V_DIM
BRANCH_WIDTH = 1024
N_BRANCH = 3

SPLIT_SIZES = (A_W, A_W, A_W, A_W,
               B_QK_W, B_QK_W, B_V_W, B_HEADS, B_HEADS,
               B_V_W, B_V_W,
               C_Q_RANK, C_KV_RANK, C_ROPE, C_W,
               N_BRANCH * D_MODEL)
D_IN = int(sum(SPLIT_SIZES))
SPLIT_POINTS = tuple(int(v) for v in np.cumsum(SPLIT_SIZES)[:-1])

kernel_name = 'hybrid_moba_mlstm_mla_block'

def rmsnorm(x, g):
    xf = x.astype(F32)
    y = xf * lax.rsqrt(jnp.mean(xf * xf, axis=-1, keepdims=True) + EPS)
    return (y * g.astype(F32)).astype(x.dtype)

def to_heads(t, n_heads):
    b, s, w = t.shape
    return t.reshape(b, s, n_heads, w // n_heads).transpose(0, 2, 1, 3)

def from_heads(t):
    b, h, s, d = t.shape
    return t.transpose(0, 2, 1, 3).reshape(b, s, h * d)

def t5_bucket(dist):
    max_exact = T5_BUCKETS // 2
    d = jnp.maximum(dist, 0)
    large = max_exact + (jnp.log(jnp.maximum(d, 1).astype(F32) / max_exact)
                         / math.log(T5_MAX_DIST / max_exact) * (T5_BUCKETS - max_exact)).astype(jnp.int32)
    large = jnp.minimum(large, T5_BUCKETS - 1)
    return jnp.where(d < max_exact, d, large)

def rope(x, pos):
    half = x.shape[-1] // 2
    inv = ROPE_THETA ** (-jnp.arange(half, dtype=F32) / half)
    ang = pos.astype(F32)[:, None] * inv[None, :]
    cos, sin = jnp.cos(ang), jnp.sin(ang)
    x1 = x[..., :half].astype(F32)
    x2 = x[..., half:].astype(F32)
    return jnp.concatenate([x1 * cos - x2 * sin, x1 * sin + x2 * cos], axis=-1).astype(x.dtype)

def causal_conv(x, w, b):
    k = w.shape[0]
    s = x.shape[1]
    xp = jnp.pad(x, ((0, 0), (k - 1, 0), (0, 0)))
    return sum(xp[:, j:j + s] * w[j] for j in range(k)) + b

def moba_attention(q, k, v, t5_table):
    bsz, h, s, hd = q.shape
    nb = -(-s // A_BLOCK)
    pad = nb * A_BLOCK - s
    padw = ((0, 0), (0, 0), (0, pad), (0, 0))
    kb = jnp.pad(k, padw).reshape(bsz, h, nb, A_BLOCK, hd)
    vb = jnp.pad(v, padw).reshape(bsz, h, nb, A_BLOCK, hd)
    k_mean = jnp.mean(kb.astype(F32), axis=3)
    q_block = jnp.arange(s) // A_BLOCK
    gate = jnp.einsum('bhsd,bhnd->bhsn', q.astype(F32), k_mean)
    is_past = jnp.arange(nb)[None, :] < q_block[:, None]
    gate = jnp.where(is_past, gate, NEG)
    n_sel = min(A_TOPK, nb)
    _, sel = lax.top_k(gate, n_sel)
    nc = s // A_QCHUNK
    q_c = q.reshape(bsz, h, nc, A_QCHUNK, hd).transpose(2, 0, 1, 3, 4)
    sel_c = sel.reshape(bsz, h, nc, A_QCHUNK, n_sel).transpose(2, 0, 1, 3, 4)
    bias_table = t5_table.T.astype(F32)
    b_idx = jnp.arange(bsz)[:, None, None, None]
    h_idx = jnp.arange(h)[None, :, None, None]
    offs = jnp.arange(A_BLOCK)
    scale = hd ** -0.5

    def one_chunk(args):
        ci, qq, ss = args
        qpos = ci * A_QCHUNK + jnp.arange(A_QCHUNK)
        own = (ci * A_QCHUNK) // A_BLOCK
        k_sel = kb[b_idx, h_idx, ss]
        v_sel = vb[b_idx, h_idx, ss]
        kpos_sel = ss[..., None] * A_BLOCK + offs
        bias_sel = bias_table[h_idx[..., None], t5_bucket(qpos[:, None, None] - kpos_sel)]
        valid = (jnp.arange(n_sel)[None, :] < (qpos // A_BLOCK)[:, None])[:, :, None]
        s_sel = jnp.einsum('bhqd,bhqnkd->bhqnk', qq, k_sel, preferred_element_type=F32) * scale + bias_sel
        s_sel = jnp.where(valid, s_sel, NEG)
        k_own = lax.dynamic_index_in_dim(kb, own, axis=2, keepdims=False)
        v_own = lax.dynamic_index_in_dim(vb, own, axis=2, keepdims=False)
        dist_own = qpos[:, None] - (own * A_BLOCK + offs)[None, :]
        s_own = (jnp.einsum('bhqd,bhkd->bhqk', qq, k_own, preferred_element_type=F32) * scale
                 + bias_table[:, t5_bucket(dist_own)])
        s_own = jnp.where(dist_own >= 0, s_own, NEG)
        s_all = jnp.concatenate([s_sel.reshape(bsz, h, A_QCHUNK, n_sel * A_BLOCK), s_own], axis=-1)
        p = jax.nn.softmax(s_all, axis=-1)
        p_sel = p[..., :n_sel * A_BLOCK].reshape(bsz, h, A_QCHUNK, n_sel, A_BLOCK).astype(v.dtype)
        p_own = p[..., n_sel * A_BLOCK:].astype(v.dtype)
        return (jnp.einsum('bhqnk,bhqnkd->bhqd', p_sel, v_sel, preferred_element_type=F32)
                + jnp.einsum('bhqk,bhkd->bhqd', p_own, v_own, preferred_element_type=F32))

    out = lax.map(one_chunk, (jnp.arange(nc), q_c, sel_c))
    return out.transpose(1, 2, 0, 3, 4).reshape(bsz, h, s, hd)

def mlstm_chunkwise(q, k, v, i_pre, f_pre):
    bsz, h, s, dk = q.shape
    dv = v.shape[-1]
    L = B_CHUNK
    nc = s // L

    def chunks(t):
        return jnp.moveaxis(t.reshape(bsz, h, nc, L, *t.shape[3:]), 2, 0)

    qc = chunks(q.astype(F32))
    kc = chunks(k.astype(F32) * (dk ** -0.5))
    vc = chunks(v.astype(F32))
    lic = chunks(i_pre.astype(F32))
    lfc = chunks(jax.nn.log_sigmoid(f_pre.astype(F32)))
    causal = jnp.tril(jnp.ones((L, L), dtype=bool))

    def step(carry, xs):
        C, n, m = carry
        qq, kk, vv, li, lf = xs
        b = jnp.cumsum(lf, axis=-1)
        a = b + m[..., None]
        D = jnp.where(causal, b[..., :, None] - b[..., None, :] + li[..., None, :], -jnp.inf)
        m_t = jnp.maximum(a, jnp.max(D, axis=-1))
        w_inter = jnp.exp(a - m_t)
        sc = jnp.einsum('bhld,bhsd->bhls', qq, kk) * jnp.exp(D - m_t[..., None])
        num = (w_inter[..., None] * jnp.einsum('bhld,bhde->bhle', qq, C)
               + jnp.einsum('bhls,bhse->bhle', sc, vv))
        den = w_inter * jnp.einsum('bhld,bhd->bhl', qq, n) + jnp.sum(sc, axis=-1)
        hh = num / jnp.maximum(jnp.abs(den), jnp.exp(-m_t))[..., None]
        b_last = b[..., -1]
        g = b_last[..., None] - b + li
        m_new = jnp.maximum(b_last + m, jnp.max(g, axis=-1))
        decay = jnp.exp(b_last + m - m_new)
        wk = jnp.exp(g - m_new[..., None])[..., None] * kk
        C_new = decay[..., None, None] * C + jnp.einsum('bhsd,bhse->bhde', wk, vv)
        n_new = decay[..., None] * n + jnp.sum(wk, axis=-2)
        return (C_new, n_new, m_new), hh

    init = (jnp.zeros((bsz, h, dk, dv), F32), jnp.zeros((bsz, h, dk), F32), jnp.zeros((bsz, h), F32))
    _, hs = lax.scan(step, init, (qc, kc, vc, lic, lfc))
    return jnp.moveaxis(hs, 0, 2).reshape(bsz, h, s, dv)

def head_layernorm(hh, g):
    t = hh.transpose(0, 2, 1, 3).astype(F32)
    mu = jnp.mean(t, axis=-1, keepdims=True)
    var = jnp.mean(jnp.square(t - mu), axis=-1, keepdims=True)
    t = (t - mu) * lax.rsqrt(var + EPS)
    b, s, h, d = t.shape
    return t.reshape(b, s, h * d) * g.astype(F32)

def causal_block_attention(q, k, v):
    bsz, h, s, dq = q.shape
    nq = s // C_QBLOCK
    qb = q.reshape(bsz, h, nq, C_QBLOCK, dq).transpose(2, 0, 1, 3, 4)
    kpos = jnp.arange(s)
    scale = dq ** -0.5

    def blk(args):
        bi, q_b = args
        qpos = bi * C_QBLOCK + jnp.arange(C_QBLOCK)
        logits = jnp.einsum('bhqd,bhkd->bhqk', q_b, k, preferred_element_type=F32) * scale
        logits = jnp.where(kpos[None, :] <= qpos[:, None], logits, NEG)
        p = jax.nn.softmax(logits, axis=-1).astype(v.dtype)
        return jnp.einsum('bhqk,bhkd->bhqd', p, v, preferred_element_type=F32)

    out = lax.map(blk, (jnp.arange(nq), qb))
    return out.transpose(1, 2, 0, 3, 4).reshape(bsz, h, s, -1)

def mla_attention(cq, ckv, kr, q_norm, kv_norm, w_uq, w_ukv, pos):
    bsz, s, _ = cq.shape
    q = jnp.einsum('bsr,re->bse', rmsnorm(cq, q_norm), w_uq)
    q = q.reshape(bsz, s, C_HEADS, C_NOPE + C_ROPE).transpose(0, 2, 1, 3)
    kv = jnp.einsum('bsr,re->bse', rmsnorm(ckv, kv_norm), w_ukv)
    kv = kv.reshape(bsz, s, C_HEADS, C_NOPE + C_V_DIM).transpose(0, 2, 1, 3)
    q = jnp.concatenate([q[..., :C_NOPE], rope(q[..., C_NOPE:], pos)], axis=-1)
    k_rope = rope(kr[:, None], pos)
    k = jnp.concatenate([kv[..., :C_NOPE], jnp.broadcast_to(k_rope, (bsz, C_HEADS, s, C_ROPE))], axis=-1)
    v = kv[..., C_NOPE:]
    return causal_block_attention(q, k, v)

def setup_inputs(seed: int = 0) -> dict:
    key = jax.random.key(seed)
    ks = jax.random.split(key, 17)
    nrm = jax.random.normal
    return {
        'x': nrm(ks[0], (BATCH, SEQ, D_MODEL), F32),
        'norm_gain': 1.0 + 0.02 * nrm(ks[1], (DEPTH, D_MODEL), F32),
        'w_in': nrm(ks[2], (DEPTH, D_MODEL, D_IN), F32) * D_MODEL ** -0.5,
        't5_table': 0.5 * nrm(ks[3], (T5_BUCKETS, A_HEADS), F32),
        'mlstm_conv_w': nrm(ks[4], (DEPTH, B_CONV, 2 * B_QK_W), F32) * B_CONV ** -0.5,
        'mlstm_conv_b': 0.01 * nrm(ks[5], (DEPTH, 2 * B_QK_W), F32),
        'mlstm_i_bias': 0.1 * nrm(ks[6], (DEPTH, B_HEADS), F32),
        'mlstm_f_bias': jnp.linspace(3.0, 6.0, B_HEADS, dtype=F32)[None, :] + 0.1 * nrm(ks[7], (DEPTH, B_HEADS), F32),
        'mlstm_out_norm': 1.0 + 0.02 * nrm(ks[8], (DEPTH, B_V_W), F32),
        'mla_q_norm': 1.0 + 0.02 * nrm(ks[9], (DEPTH, C_Q_RANK), F32),
        'mla_kv_norm': 1.0 + 0.02 * nrm(ks[10], (DEPTH, C_KV_RANK), F32),
        'mla_w_uq': nrm(ks[11], (DEPTH, C_Q_RANK, C_HEADS * (C_NOPE + C_ROPE)), F32) * C_Q_RANK ** -0.5,
        'mla_w_ukv': nrm(ks[12], (DEPTH, C_KV_RANK, C_HEADS * (C_NOPE + C_V_DIM)), F32) * C_KV_RANK ** -0.5,
        'w_branch': nrm(ks[13], (DEPTH, N_BRANCH, BRANCH_WIDTH, D_MODEL), F32) * BRANCH_WIDTH ** -0.5,
        'w_out': nrm(ks[14], (DEPTH, D_MODEL, D_MODEL), F32) * D_MODEL ** -0.5,
        'final_norm': 1.0 + 0.02 * nrm(ks[15], (D_MODEL,), F32),
    }

def reference(x, norm_gain, w_in, t5_table, mlstm_conv_w, mlstm_conv_b, mlstm_i_bias, mlstm_f_bias,
              mlstm_out_norm, mla_q_norm, mla_kv_norm, mla_w_uq, mla_w_ukv, w_branch, w_out, final_norm):
    bsz, s, _ = x.shape
    pos = jnp.arange(s, dtype=jnp.int32)
    for l in range(DEPTH):
        h = rmsnorm(x, norm_gain[l])
        proj = jnp.einsum('bsd,de->bse', h, w_in[l])
        (qa, ka, va, za, qb, kb, vb, ib, fb, ob, zb, cq, ckv, kr, zc, gt) = jnp.split(proj, SPLIT_POINTS, axis=-1)
        ya = moba_attention(to_heads(qa, A_HEADS), to_heads(ka, A_HEADS), to_heads(va, A_HEADS), t5_table)
        ya = from_heads(ya) * jax.nn.silu(za.astype(F32))
        qk = jax.nn.silu(causal_conv(jnp.concatenate([qb, kb], axis=-1), mlstm_conv_w[l], mlstm_conv_b[l]))
        qb2, kb2 = jnp.split(qk, 2, axis=-1)
        i_pre = (ib + mlstm_i_bias[l]).transpose(0, 2, 1)
        f_pre = (fb + mlstm_f_bias[l]).transpose(0, 2, 1)
        hb = mlstm_chunkwise(to_heads(qb2, B_HEADS), to_heads(kb2, B_HEADS), to_heads(vb, B_HEADS), i_pre, f_pre)
        yb = (head_layernorm(hb, mlstm_out_norm[l]) * jax.nn.sigmoid(ob.astype(F32))
              * jax.nn.silu(zb.astype(F32)))
        hc = mla_attention(cq, ckv, kr, mla_q_norm[l], mla_kv_norm[l], mla_w_uq[l], mla_w_ukv[l], pos)
        yc = from_heads(hc) * jax.nn.silu(zc.astype(F32))
        ys = jnp.stack([ya, yb, yc], axis=2).astype(h.dtype)
        branch = jnp.einsum('bsnw,nwd->bsnd', ys, w_branch[l])
        gates = jax.nn.sigmoid(gt.reshape(bsz, s, N_BRANCH, D_MODEL))
        merged = jnp.sum(gates * branch, axis=2)
        x = (x + jnp.einsum('bsd,de->bse', merged, w_out[l])).astype(x.dtype)
    return rmsnorm(x, final_norm)


_drawn_inputs = setup_inputs


def setup_inputs(seed=0):
    import zlib

    import numpy as np

    out = dict(_drawn_inputs(seed))
    spreads = {}
    factors = {'norm_gain': 4.736,
     'mlstm_conv_b': 39.9,
     'mlstm_i_bias': 200.0,
     'mlstm_out_norm': 8.0,
     'mla_q_norm': 8.0,
     'mla_kv_norm': 8.0,
     'final_norm': 20.748}
    for name, (base, spread) in spreads.items():
        noise = np.random.default_rng([zlib.crc32(name.encode()), seed]).standard_normal(out[name].shape)
        drawn = base * np.exp(spread * noise) if base else spread * noise
        out[name] = __import__('jax').numpy.asarray(drawn.astype(out[name].dtype))
    for name, factor in factors.items():
        out[name] = (out[name] * factor).astype(out[name].dtype)
    return out
```

```python
import numpy as np
import concourse.bass as bass
from concourse import mybir

F32, F32R = mybir.dt.float32, mybir.dt.float32r
ALU, ACT, AX = mybir.AluOpType, mybir.ActivationFunctionType, mybir.AxisListType

P = 128
L = 2
S = 256
D = 2048
DT = D // P
EPS = 1e-6
NEG = -1e30
RING = 4
AHEAD = 3
C_A, C_B, C_H, C_U, C_C, C_G, C_M, C_O = 0, 16, 48, 80, 108, 172, 268, 316
CHUNKS = 348
G_A, G_B, G_H, G_U, G_C, G_G, G_M, G_O = 0, 2, 6, 10, 20, 28, 44, 52
GROUPS = 56
TOTAL = L * CHUNKS + RING
FREE = 1
PIECES = 16
Q_NG, Q_CONV, Q_ON, Q_QN, Q_KVN, Q_IB, Q_FB, NPAR = 0, 16, 56, 64, 68, 70, 71, 72
A_SCALE = 128 ** -0.5
C_SCALE = 192 ** -0.5
B_SCALE = 128 ** -0.5 / 4
LOG1P = [1 / 15, 1 / 13, 1 / 11, 1 / 9, 1 / 7, 1 / 5, 1 / 3]


def build(nc, w, xin, consts, params, table, onehot, out):
    bias_scratch = nc.dram_tensor("bias_scratch", (8, P * 384), F32).ap()
    x_saved_dram = nc.dram_tensor("x_saved_dram", (P, DT * S), F32).ap()

    base = 16512
    offset = [base]

    def at(name, shape, dtype, where):
        return nc.alloc_sbuf_tensor_at(name, [P, *shape] if isinstance(shape, tuple) else shape, dtype, offset=where)

    def new(name, shape, dtype=F32):
        size = 4 * int(np.prod(shape))
        t = at(name, shape, dtype, offset[0])
        offset[0] += (size + 31) // 32 * 32
        return t

    def region(size):
        where = offset[0]
        offset[0] += size
        return where

    act = new("act", (DT, 512), F32R)
    raw = new("raw", (RING, 2, 512))
    w_hi = new("w_hi", (RING, 2, 512), F32R)
    w_lo = new("w_lo", (RING, 2, 512), F32R)
    r1 = region(32768)
    first = at("first", (24, S), F32, r1)
    hb = at("hb", (4, 2, S), F32, r1 + 24576)
    moba = at("moba", (8, 4, S), F32, r1)
    table_bc = at("table_bc", (8, P), F32, r1)
    bias_wide = at("bias_wide", (8, 384), F32, r1 + 4096)
    r2 = region(32768)
    lat = at("lat", (4, 7, S), F32, r2)
    y_act = at("y_act", (8, 512), F32R, r2)
    x = at("x", (DT, S), F32, r2)
    merged = at("merged", (DT, S), F32, r2 + 16384)
    x_sq = at("x_sq", (DT, S), F32, r2 + 16384)
    c_sq = at("c_sq", (6, S), F32, r2 + 16384)
    g_diag = at("g_diag", (4, S), F32, r2 + 16384 + 8192)
    y_bc = new("y_bc", (2, 8, S))
    bias = new("bias", (8, S))
    r3 = region(12288)
    gi = [at(f"gi{n}", (S,), F32, r3 + 1024 * n) for n in range(12)]
    qk_conv = at("qk_conv", (2, S), F32, r3)
    qk_tanh = at("qk_tanh", (2, S), F32, r3 + 2048)
    qk = at("qk", (2, S), F32, r3 + 4096)
    b_v = at("b_v", (2, S), F32, r3 + 6144)
    b_h = at("b_h", (2, S), F32, r3 + 8192)
    b_vt = at("b_vt", (2, S), F32, r3 + 10240)
    cq_act = at("cq_act", (4, 512), F32R, r3)
    ckv_act = at("ckv_act", (2, 512), F32R, r3 + 8192)
    c_in = at("c_in", (7, S), F32, r3)
    c_rot = at("c_rot", (2, S), F32, r3 + 7168)
    c_qr = at("c_qr", (S,), F32, r3 + 9216)
    a_in = at("a_in", (4, S), F32, r3)
    sq_sum = at("sq_sum", (2, S), F32, r3)
    sq_new = at("sq_new", (2, S), F32, r3 + 2048)
    onehot_sb = at("onehot_sb", (384,), F32, r3 + 4096)
    table_sb = at("table_sb", (8,), F32, r3 + 8192)
    carry = new("carry", (4, S))
    ev = new("ev", (4, S))
    th = new("th", (4, S))
    tp = region(3072)
    t_log = at("t_log", (384,), F32, tp)
    probs = at("probs", (384,), F32, tp + 1536)
    b_norm = at("b_norm", (2, S), F32, tp)
    probs_t = new("probs_t", (384,))
    v_t = new("v_t", (S,))
    z_tanh = new("z_tanh", (S,))
    z_gate = new("z_gate", (S,))
    kr = new("kr", (S,))
    rstd = new("rstd", (S,))
    const = new("const", (1024,))
    ones = new("ones", (P,))
    par_all = new("par_all", (L * NPAR + DT,))
    par = new("par", (NPAR,))
    b_cols = new("b_cols", (4, 4))
    b_mv = new("b_mv", (4, 2, 2))
    b_var = new("b_var", (8,))
    small = new("small", (32,))
    stats = new("stats", (2, 6))
    mean_var = new("mean_var", (2, 2))
    assert offset[0] <= nc.sbuf_usable_end, offset[0]
    ident, perm = const[:, 0:128], const[:, 128:256]
    mask, cos, sin = const[:, 256:512], const[:, 512:768], const[:, 768:1024]
    row_max, den, den_inv = small[:, 0:2], small[:, 8:10], small[:, 16:18]

    acc = nc.alloc_psum_tensor("acc", [P, 4, 512], F32)
    ps_s = nc.alloc_psum_tensor("ps_s", [P, 512], F32)
    ps_t = nc.alloc_psum_tensor("ps_t", [P, 512], F32)
    ps_o = nc.alloc_psum_tensor("ps_o", [P, 512], F32)
    ps_g = nc.alloc_psum_tensor("ps_g", [P, 512], F32)

    sem = nc.alloc_semaphore
    consts_in, table_in, x_in = sem("consts_in"), sem("table_in"), sem("x_in")
    raw_in = [sem(f"raw_in{r}") for r in range(RING)]
    hi_ready, split_ready, chunk_used = sem("hi_ready"), sem("split_ready"), sem("chunk_used")
    pair_done, carry_ready, acc_free = sem("pair_done"), sem("carry_ready"), sem("acc_free")
    piece_src, piece_hi, piece_lo = sem("piece_src"), sem("piece_hi"), sem("piece_lo")
    ones_ready, table_ready, bias_mm, bias_sb = sem("ones_ready"), sem("table_ready"), sem("bias_mm"), sem("bias_sb")
    bias_out, bias_ready = sem("bias_out"), sem("bias_ready")
    sq_ready, sq_cleared, sums_ready, var_ready, std_ready = (
        sem("sq_ready"), sem("sq_cleared"), sem("sums_ready"), sem("var_ready"), sem("std_ready"))
    par_ready, x_saved, x_back, x_added, sq_pair = (
        sem("par_ready"), sem("x_saved"), sem("x_back"), sem("x_added"), sem("sq_pair"))
    th_ready, prod_ready, merged_done = sem("th_ready"), sem("prod_ready"), sem("merged_done")
    f_abs, f_exp, m_sum, m_exp, g_ready, g_cols = (
        sem("f_abs"), sem("f_exp"), sem("m_sum"), sem("m_exp"), sem("g_ready"), sem("g_cols"))
    b_conv, b_tanh, b_vs, b_vg, b_log, b_exp, b_s, b_sc, b_pt, b_ptc, b_pv, b_out, b_kept = (
        sem(f"b_{n}") for n in ("conv", "tanh", "vs", "vg", "log", "exp", "s", "sc", "pt", "ptc", "pv", "out", "kept"))
    c_squares, l_sums, l_var, l_std, n_in, n_t, n_out = (
        sem(n) for n in ("c_squares", "l_sums", "l_var", "l_std", "n_in", "n_t", "n_out"))
    c_q_in, c_kv_in, c_swap, c_rope = sem("c_q_in"), sem("c_kv_in"), sem("c_swap"), sem("c_rope")
    a_staged = sem("a_staged")
    h_scores, h_vt, h_max, h_exp, h_probs, h_pt, h_ptc, h_pv, h_out = (
        sem(f"h_{n}") for n in ("scores", "vt", "max", "exp", "probs", "pt", "ptc", "pv", "out"))
    stored, final_ready = sem("stored"), sem("final_ready")

    block_cm = nc.Block()
    block = block_cm.__enter__()

    @block.sync
    def _(sp):
        sp.dma_start(const[:], consts).then_inc(consts_in, 16)
        sp.dma_start(par_all[:], params).then_inc(consts_in, 16)
        sp.dma_start(onehot_sb[0:33, :], onehot).then_inc(table_in, 16)
        sp.dma_start(table_sb[0:32, :], table).then_inc(table_in, 16)
        sp.dma_start(x[:], xin).then_inc(x_in, 16)
        for r in range(RING):
            sp.dma_start(raw[:, r], w[r]).then_inc(raw_in[r], 16)
        sp.wait_ge(x_in, 16)
        sp.dma_start(x_saved_dram, x[:].rearrange("p t s -> p (t s)")).then_inc(x_saved, 16)
        with sp.Fori(1, TOTAL // RING) as turn:
            for r in range(RING):
                sp.wait_ge(split_ready, RING * turn + (r - RING + 1))
                sp.dma_start(raw[:, r], w[RING * turn + r]).then_inc(raw_in[r], 16)
        for r in range(RING):
            sp.wait_ge(raw_in[r], 16 * (TOTAL // RING))
        sp.wait_ge(final_ready, 4)
        sp.dma_start(out, merged[:]).then_inc(stored, 16)
        sp.wait_ge(x_saved, 16 * (L + 1))
        sp.wait_ge(stored, 16)

    @block.tensor
    def _(pe):
        mm = nc.tensor.matmul

        def chunk(c, g2, j, operand, k0, begin, end, strips=4, group=0):
            slot = j % RING
            pe.wait_ge(split_ready, c + (j + 1))
            for s in range(strips):
                if begin and s % 2 == 0:
                    pe.wait_ge(acc_free, g2 + (2 * group + s // 2 + 1))
                for kk in range(2):
                    mm(acc[:, s, :], w_hi[:, slot, kk, s * P:(s + 1) * P], operand[:, k0 + kk, :],
                       start=begin and kk == 0, stop=False)
                    last = mm(acc[:, s, 0:S], w_lo[:, slot, kk, s * P:(s + 1) * P], operand[:, k0 + kk, 0:S],
                              start=False, stop=end and kk == 1)
                if end and s == 1:
                    last.then_inc(pair_done, 1)
            last.then_inc(chunk_used, 1)

        def causal_scores(q, k):
            n = len(q)
            for cols, qs, ks in ((slice(0, 256), slice(128, 256), slice(0, 256)),
                                 (slice(256, 384), slice(0, 128), slice(0, 128))):
                for t in range(n):
                    last = mm(ps_s[:, cols], q[t][:, qs], k[t][:, ks], start=t == 0, stop=t == n - 1)
            return last

        def transpose_probs():
            nc.tensor.transpose(ps_t[:, 0:128], probs[:, 256:384], ident)
            nc.tensor.transpose(ps_t[:, 128:256], probs[:, 0:128], ident)
            return nc.tensor.transpose(ps_t[:, 256:384], probs[:, 128:256], ident)

        def head_scores(q, k, v):
            causal_scores(q, k)
            nc.tensor.transpose(ps_g[:, 0:128], v[:, 0:128], ident)
            nc.tensor.transpose(ps_g[:, 128:256], v[:, 128:256], ident).then_inc(h_scores, 1)

        def head_transposes(count):
            pe.wait_ge(h_probs, count)
            transpose_probs().then_inc(h_pt, 1)

        def head_values(count):
            pe.wait_ge(h_ptc, count)
            mm(ps_o[:, 0:256], v_t[:, 0:128], probs_t[:, 0:256], start=True, stop=False)
            mm(ps_o[:, 128:256], v_t[:, 128:256], probs_t[:, 256:384], start=False, stop=True).then_inc(h_pv, 1)

        def sum_squares(squares, count):
            pe.wait_ge(squares, count)
            mm(ps_g[:, 0:S], ones[:], sq_sum[:, 0], start=True, stop=False)
            mm(ps_g[:, 0:S], ones[:], sq_sum[:, 1], start=False, stop=True).then_inc(sums_ready, 1)

        pe.wait_ge(consts_in, 32)
        pe.wait_ge(table_ready, 1)
        for h in range(8):
            bank = acc[:, h, 0:384] if h < 4 else (ps_s, ps_t, ps_o, ps_g)[h - 4][:, 0:384]
            last = mm(bank, table_bc[0:33, h, :], onehot_sb[0:33, :], start=True, stop=True)
            if h < 2:
                last.then_inc((chunk_used, b_pv)[h], FREE)
        last.then_inc(bias_mm, 1)
        pe.wait_ge(bias_sb, 1)
        sum_squares(sq_ready, 1)

        with pe.Fori(0, L) as l:
            pieces = pe.snap(l * PIECES)
            c = pe.snap(l * CHUNKS + C_A)
            g2 = pe.snap(2 * (l * GROUPS + G_A))
            for j in range(16):
                if j % 2 == 0 and j < 8:
                    pe.wait_ge(piece_lo, pieces + (j // 2 + 1) + FREE)
                if j == 15:
                    pe.wait_ge(g_ready, l + 1)
                chunk(c, g2, j, act, 2 * (j % 8), j % 8 == 0, j % 8 == 7, group=j // 8)
                if j == 15:
                    for n, rows in enumerate((gi[8], gi[10])):
                        for t in range(2):
                            last = nc.tensor.transpose(ps_t[:, 8 * n + 4 * t:8 * n + 4 * t + 4],
                                                       rows[0:4, t * P:(t + 1) * P], ident[0:4, 0:4])
                    last.then_inc(g_cols, 1)
            with pe.Fori(0, 4) as i:
                c = pe.snap(l * CHUNKS + C_B + i * 8)
                g2 = pe.snap(2 * (l * GROUPS + G_B + i))
                for j in range(8):
                    chunk(c, g2, j, act, 2 * j, j == 0, j == 7)
            with pe.Fori(0, 4) as i:
                c = pe.snap(l * CHUNKS + C_H + i * 8)
                g2 = pe.snap(2 * (l * GROUPS + G_H + i))
                n = pe.snap(l * 4 + i)
                for j in range(8):
                    chunk(c, g2, j, act, 2 * j, j == 0, j == 7)
                    if j == 1:
                        pe.wait_ge(b_vs, n + 1)
                        for t in range(2):
                            for s in range(2):
                                nc.tensor.transpose(ps_t[:, t * S + s * P:t * S + (s + 1) * P],
                                                    b_v[:, s, t * P:(t + 1) * P], ident)
                        mm(ps_g[:, 0:S], ones[0:4, :], g_diag[0:4, i, :], start=True, stop=True).then_inc(b_vg, 1)
                    if j == 3:
                        pe.wait_ge(b_log, n + 1)
                        causal_scores([qk[:, 0]], [qk[:, 1]]).then_inc(b_s, 1)
                    if j == 5:
                        pe.wait_ge(b_sc, n + 1)
                        transpose_probs().then_inc(b_pt, 1)
                    if j == 6:
                        pe.wait_ge(b_ptc, n + 1)
                        mm(ps_o[:, 0:256], probs_t[:, 0:128], b_vt[:, 0], start=True, stop=True)
                        mm(ps_o[:, 256:512], probs_t[:, 128:256], b_vt[:, 0], start=True, stop=False)
                        mm(ps_o[:, 256:512], probs_t[:, 256:384], b_vt[:, 1], start=False, stop=True).then_inc(b_pv, 1)
            c = pe.snap(l * CHUNKS + C_U)
            g2 = pe.snap(2 * (l * GROUPS + G_U))
            for j in range(28):
                if j < 16:
                    chunk(c, g2, j, act, 2 * (j % 8), j % 8 == 0, j % 8 == 7, group=j // 8)
                elif j < 24:
                    if j == 16:
                        pe.wait_ge(piece_lo, pieces + 6 + FREE)
                    chunk(c, g2, j, cq_act, 2 * (j % 2), j % 2 == 0, j % 2 == 1, strips=3, group=2 + (j - 16) // 2)
                else:
                    chunk(c, g2, j, ckv_act, 0, True, True, group=6 + j - 24)
                if j == 0:
                    pe.wait_ge(c_squares, l + 1)
                    mm(ps_g[:, 0:S], ones[:], c_sq[:, 2], start=True, stop=True)
                    mm(ps_g[:, S:2 * S], ones[:], c_sq[:, 0], start=True, stop=True)
                    mm(ps_s[:, 0:S], perm, first[:, 0], start=True, stop=True).then_inc(l_sums, 1)
                if j in (7, 9, 11, 13):
                    b = (j - 7) // 2
                    pe.wait_ge(n_in, l * 4 + (b + 1))
                    for s in range(2):
                        for t in range(2):
                            last = nc.tensor.transpose(ps_t[:, s * S + t * P:s * S + (t + 1) * P],
                                                       b_norm[:, t, s * P:(s + 1) * P], ident)
                    last.then_inc(n_t, 1)
            with pe.Fori(0, 4) as i:
                c = pe.snap(l * CHUNKS + C_C + i * 16)
                g2 = pe.snap(2 * (l * GROUPS + G_C + 2 * i))
                n = pe.snap(l * 4 + i)
                h = pe.snap(l * 16 + 2 * i)
                for j in range(16):
                    chunk(c, g2, j, act, 2 * (j % 8), j % 8 == 0, j % 8 == 7, group=j // 8)
                    if j == 2:
                        pe.wait_ge(c_q_in, n + 1)
                        mm(ps_g[:, S:2 * S], perm, c_in[:, 2], start=True, stop=True).then_inc(c_swap, 1)
                    if j in (4, 10):
                        u = j // 10
                        if u == 0:
                            pe.wait_ge(c_rope, n + 1)
                            pe.wait_ge(c_kv_in, n + 1)
                        rot = slice(64 * u, 64 * u + 64)
                        head_scores([c_in[:, u], c_qr[rot]], [c_in[:, 3 + u], kr[rot]], c_in[:, 5 + u])
                    if j in (7, 13):
                        head_transposes(h + ((j - 7) // 6 + 1))
                    if j in (8, 14):
                        head_values(h + ((j - 8) // 6 + 1))
            with pe.Fori(0, 2) as n:
                with pe.Fori(0, 4) as i:
                    c = pe.snap(l * CHUNKS + C_G + n * 48 + i * 12)
                    g2 = pe.snap(2 * (l * GROUPS + G_G + n * 8 + i * 2))
                    h = pe.snap(l * 16 + 8 + n * 4 + i)
                    for j in range(12):
                        if j < 8:
                            chunk(c, g2, j, act, 2 * j, j == 0, j == 7)
                        else:
                            if j == 8:
                                pe.wait_ge(piece_lo, pieces + n * 2 + 8 + FREE)
                            chunk(c, g2, j, y_act, 2 * (j - 8), j == 8, j == 11, group=1)
                        if j == 1:
                            pe.wait_ge(a_staged, l * 8 + n * 4 + i + 1)
                            head_scores([a_in[:, 0]], [a_in[:, 1]], a_in[:, 2])
                        if j == 4:
                            head_transposes(h + 1)
                        if j == 5:
                            head_values(h + 1)
            with pe.Fori(0, 4) as i:
                c = pe.snap(l * CHUNKS + C_M + i * 12)
                g2 = pe.snap(2 * (l * GROUPS + G_M + i * 2))
                for j in range(12):
                    if j < 8:
                        chunk(c, g2, j, act, 2 * j, j == 0, j == 7)
                    else:
                        if j == 8:
                            pe.wait_ge(piece_lo, pieces + 12 + FREE)
                        chunk(c, g2, j, y_act, 2 * (j - 8), j == 8, j == 11, group=1)
            with pe.Fori(0, 4) as i:
                c = pe.snap(l * CHUNKS + C_O + i * 8)
                g2 = pe.snap(2 * (l * GROUPS + G_O + i))
                for j in range(8):
                    if j % 2 == 0:
                        pe.wait_ge(piece_lo, pieces + (12 + j // 2 + 1) + FREE)
                    chunk(c, g2, j, act, 2 * j, j == 0, j == 7)
            sum_squares(sq_pair, l * 4 + 5)

    @block.scalar
    def _(a):
        def split_ahead(c, j):
            m = j + AHEAD
            a.wait_ge(raw_in[m % RING], 4 * c + (16 * (m // RING) + 16))
            a.wait_ge(chunk_used, c + j + FREE)
            nc.scalar.activation(w_hi[:, m % RING], raw[:, m % RING], ACT.Copy).then_inc(hi_ready, 1)

        def empty(c, g, j, strips=4, group=0):
            a.wait_ge(pair_done, g + (group + 1))
            nc.scalar.copy(carry[:, 0:2], acc[:, 0:2, S:2 * S]).then_inc(carry_ready, 1)
            a.wait_ge(chunk_used, c + (j + 1) + FREE)
            nc.scalar.copy(carry[:, 2:strips], acc[:, 2:strips, S:2 * S]).then_inc(carry_ready, 1)

        def gate_tanh(g2, group=0):
            a.wait_ge(acc_free, g2 + (2 * group + 4))
            nc.scalar.activation(th[:], ev[:], ACT.Tanh, scale=0.5).then_inc(th_ready, 1)

        def piece(dst, src, scale=1.0):
            nc.scalar.activation(dst, src, ACT.Copy, scale=scale).then_inc(piece_hi, 1)

        def head_vt(count, z=None):
            a.wait_ge(h_scores, count)
            if z is not None:
                nc.scalar.activation(z_tanh[:], z, ACT.Tanh, scale=0.5)
            nc.scalar.copy(v_t[:], ps_g[:, 0:S])

        def exps(bias0, bias1, scale, done, sums):
            kw = ({}, {}) if not sums else (dict(accum_out=den[:, 1:2]), dict(accum_out=den[:, 0:1]))
            nc.scalar.activation(probs[:, 0:256], t_log[:, 0:256], ACT.Exp, bias=bias1, scale=scale, **kw[0])
            nc.scalar.activation(probs[:, 256:384], t_log[:, 256:384], ACT.Exp, bias=bias0, scale=scale,
                                 **kw[1]).then_inc(done, 1)

        def head_exp(count):
            a.wait_ge(h_max, count)
            exps(row_max[:, 0:1], row_max[:, 1:2], 1.0, h_exp, True)

        def head_pt(count):
            a.wait_ge(h_pt, count)
            nc.scalar.copy(probs_t[:], ps_t[:, 0:384]).then_inc(h_ptc, 1)

        a.wait_ge(x_in, 16)
        nc.scalar.activation(x_sq[:], x[:], ACT.Square).then_inc(sq_pair, 1)
        for n in range(AHEAD):
            a.wait_ge(raw_in[n], 16)
            nc.scalar.activation(w_hi[:, n], raw[:, n], ACT.Copy).then_inc(hi_ready, 1)
        a.wait_ge(var_ready, 1)
        nc.scalar.activation(rstd[:], rstd[:], ACT.Sqrt).then_inc(std_ready, 1)

        with a.Fori(0, L) as l:
            g = a.snap(l * GROUPS)
            for q in range(4):
                a.wait_ge(piece_src, l * 6 + (q + 1))
                piece(act[:, 4 * q:4 * q + 4, 0:S], (ev, th)[q % 2][:])
            c = a.snap(l * CHUNKS + C_A)
            for j in range(16):
                split_ahead(c, j)
                if j % 8 == 7:
                    empty(c, g, j, group=j // 8)
                if j == 9:
                    a.wait_ge(f_abs, l + 1)
                    nc.scalar.activation(gi[2][0:4], gi[2][0:4], ACT.Exp, scale=-1.0).then_inc(f_exp, 1)
                if j == 13:
                    a.wait_ge(m_sum, l + 1)
                    nc.scalar.activation(gi[10][0:4], gi[9][0:4], ACT.Exp, scale=-1.0).then_inc(m_exp, 1)
            with a.Fori(0, 4) as i:
                c = a.snap(l * CHUNKS + C_B + i * 8)
                g = a.snap(l * GROUPS + G_B + i)
                for j in range(8):
                    split_ahead(c, j)
                empty(c, g, 7)
            with a.Fori(0, 4) as i:
                c = a.snap(l * CHUNKS + C_H + i * 8)
                g = a.snap(l * GROUPS + G_H + i)
                n = a.snap(l * 4 + i)
                for j in range(8):
                    split_ahead(c, j)
                    if j == 1:
                        a.wait_ge(b_conv, n + 1)
                        nc.scalar.activation(qk_tanh[:], qk_conv[:], ACT.Tanh, scale=0.5).then_inc(b_tanh, 1)
                    if j == 2:
                        a.wait_ge(b_vg, n + 1)
                        nc.scalar.copy(b_vt[:], ps_t[:].rearrange("p (t s) -> p t s", t=2))
                        a.wait_ge(b_log, n + 1)
                        exps(b_cols[:, 0, bass.ds(i, 1)], b_cols[:, 1, bass.ds(i, 1)], 1.0, b_exp, False)
                    if j == 6:
                        a.wait_ge(b_pt, n + 1)
                        nc.scalar.copy(probs_t[:], ps_t[:, 0:384]).then_inc(b_ptc, 1)
                empty(c, g, 7)
                gate_tanh(a.snap(2 * g))
            c = a.snap(l * CHUNKS + C_U)
            g = a.snap(l * GROUPS + G_U)
            g2 = a.snap(2 * g)
            for j in range(28):
                split_ahead(c, j)
                if j < 16 and j % 8 == 7:
                    empty(c, g, j, group=j // 8)
                    gate_tanh(g2, group=j // 8)
                if 16 <= j < 24 and j % 2 == 1:
                    empty(c, g, j, strips=3, group=2 + (j - 16) // 2)
                if j >= 24:
                    empty(c, g, j, group=6 + j - 24)
                if j == 1:
                    a.wait_ge(l_var, l + 1)
                    nc.scalar.activation(th[:, 2:4], th[:, 2:4], ACT.Sqrt)
                    nc.scalar.activation(b_var[:], b_var[:], ACT.Sqrt).then_inc(l_std, 1)
                if j == 4:
                    a.wait_ge(piece_src, l * 6 + 5)
                    piece(cq_act[:, :, 0:S], ev[:])
                if j == 5:
                    a.wait_ge(piece_src, l * 6 + 6)
                    piece(ckv_act[:, :, 0:S], th[:, 0:2])
            with a.Fori(0, 4) as i:
                c = a.snap(l * CHUNKS + C_C + i * 16)
                g = a.snap(l * GROUPS + G_C + 2 * i)
                n = a.snap(l * 4 + i)
                h = a.snap(l * 16 + 2 * i)
                for j in range(16):
                    split_ahead(c, j)
                    if j % 8 == 7:
                        empty(c, g, j, group=j // 8)
                    if j == 0:
                        a.wait_ge(acc_free, l * (2 * GROUPS) + (2 * G_C + 2))
                        a.wait_ge(h_out, h + FREE)
                        nc.scalar.copy(c_in[:, 3:7], lat[:, i, 3:7, :]).then_inc(c_kv_in, 1)
                    for u in range(2):
                        s = 4 + 6 * u
                        if j == s + 1:
                            head_vt(h + (u + 1))
                            head_exp(h + (u + 1))
                        if j == s + 4:
                            head_pt(h + (u + 1))
            with a.Fori(0, 2) as n:
                a.wait_ge(h_out, l * 16 + 8 + FREE)
                a.wait_ge(chunk_used, l * CHUNKS + C_G + n * 48 + FREE)
                for q in range(2):
                    piece(y_act[:, 4 * q:4 * q + 4, 0:S], y_bc[:, n, 4 * q:4 * q + 4, :])
                with a.Fori(0, 4) as i:
                    c = a.snap(l * CHUNKS + C_G + n * 48 + i * 12)
                    g = a.snap(l * GROUPS + G_G + n * 8 + i * 2)
                    h = a.snap(l * 16 + 8 + n * 4 + i)
                    for j in range(12):
                        split_ahead(c, j)
                        if j == 7:
                            empty(c, g, 7)
                            gate_tanh(a.snap(2 * g))
                        if j == 11:
                            empty(c, g, 11, group=1)
                        if j == 2:
                            head_vt(h + 1, a_in[:, 3])
                            head_exp(h + 1)
                        if j == 5:
                            head_pt(h + 1)
            a.wait_ge(h_out, l * 16 + 16 + FREE)
            a.wait_ge(chunk_used, l * CHUNKS + C_M + FREE)
            for q in range(2):
                piece(y_act[:, 4 * q:4 * q + 4, 0:S], moba[:, 4 * q:4 * q + 4, 3, :])
            with a.Fori(0, 4) as i:
                c = a.snap(l * CHUNKS + C_M + i * 12)
                g = a.snap(l * GROUPS + G_M + i * 2)
                for j in range(12):
                    split_ahead(c, j)
                    if j == 7:
                        empty(c, g, 7)
                        gate_tanh(a.snap(2 * g))
                    if j == 11:
                        empty(c, g, 11, group=1)
            a.wait_ge(merged_done, l * 12 + 12 + FREE)
            for q in range(4):
                piece(act[:, 4 * q:4 * q + 4, 0:S], merged[:, 4 * q:4 * q + 4], scale=0.5)
            a.wait_ge(chunk_used, l * CHUNKS + C_O + FREE)
            a.wait_ge(x_saved, 16 * l + 16)
            a.dma_start(x[:].rearrange("p t s -> p (t s)"), x_saved_dram).then_inc(x_back, 16)
            with a.Fori(0, 4) as i:
                c = a.snap(l * CHUNKS + C_O + i * 8)
                g = a.snap(l * GROUPS + G_O + i)
                for j in range(8):
                    split_ahead(c, j)
                empty(c, g, 7)
            a.wait_ge(x_added, l * 8 + 8 + FREE)
            a.dma_start(x_saved_dram, x[:].rearrange("p t s -> p (t s)")).then_inc(x_saved, 16)
            a.wait_ge(var_ready, l + 2)
            nc.scalar.activation(rstd[:], rstd[:], ACT.Sqrt).then_inc(std_ready, 1)

    @block.vector
    def _(v):
        V = nc.vector

        def split_ahead(c, j):
            m = (j + AHEAD) % RING
            v.wait_ge(hi_ready, c + (j + AHEAD + 1))
            V.tensor_tensor(w_lo[:, m], raw[:, m], w_hi[:, m].bitcast(F32), ALU.subtract).then_inc(split_ready, 1)

        def empty(g2, dst, strips=4, group=0, free=None):
            v.drain()
            if free is not None:
                v.wait_ge(*free)
            for q in range(2):
                n = min(strips, 2 * q + 2)
                v.wait_ge(carry_ready, g2 + (2 * group + q + 1))
                V.tensor_tensor(dst(2 * q, n), acc[:, 2 * q:n, 0:S], carry[:, 2 * q:n], ALU.add).then_inc(acc_free, 1)

        def piece(count, dst, src, hi, scale=None):
            v.wait_ge(piece_hi, count)
            if scale is None:
                V.tensor_tensor(dst, src, hi.bitcast(F32), ALU.subtract).then_inc(piece_lo, 1)
            else:
                V.scalar_tensor_tensor(dst, src, scale, hi.bitcast(F32), ALU.mult, ALU.subtract).then_inc(piece_lo, 1)

        def logits(scale, bias1, bias0, count):
            v.wait_ge(h_scores, count)
            V.scalar_tensor_tensor(t_log[:, 0:256], ps_s[:, 0:256], scale, bias1, ALU.mult, ALU.add)
            V.scalar_tensor_tensor(t_log[:, 256:384], ps_s[:, 256:384], scale, bias0, ALU.mult, ALU.add)
            v.drain()
            V.tensor_reduce(row_max[:, 1:2], t_log[:, 0:256], AX.X, ALU.max, negate=True)
            V.tensor_reduce(row_max[:, 0:1], t_log[:, 256:384], AX.X, ALU.max, negate=True).then_inc(h_max, 1)

        def norm_probs(count, z, tanh):
            v.wait_ge(h_exp, count)
            V.reciprocal(den_inv, den)
            if z is not None:
                V.scalar_tensor_tensor(z_gate[:], tanh, 1.0, z, ALU.add, ALU.mult)
            v.drain()
            V.tensor_scalar(probs[:, 0:256], probs[:, 0:256], den_inv[:, 1:2], 0.5, ALU.mult, ALU.mult)
            V.tensor_scalar(probs[:, 256:384], probs[:, 256:384], den_inv[:, 0:1], 0.5, ALU.mult,
                            ALU.mult).then_inc(h_probs, 1)

        def norm_stats(count):
            v.wait_ge(sums_ready, count)
            V.tensor_scalar(rstd[:], ps_g[:, 0:S], 1.0 / D, EPS, ALU.mult, ALU.add).then_inc(var_ready, 1)
            v.wait_ge(std_ready, count)
            V.reciprocal(rstd[:], rstd[:])
            v.drain()

        V.memset(ones[:], 1.0).then_inc(h_out, FREE)
        V.memset(table_bc[32:33], NEG).then_inc(piece_lo, FREE)
        v.wait_ge(table_in, 32)
        V.tensor_copy(table_bc[0:32], table_sb[0:32].rearrange("p (h o) -> p h o", o=1).to_broadcast([32, 8, P])
                      ).then_inc(table_ready, 1)
        v.wait_ge(bias_mm, 1)
        V.tensor_copy(bias_wide[:, 0:4], acc[:, :, 0:384])
        for n, bank in enumerate((ps_s, ps_t, ps_o, ps_g)):
            last = V.tensor_copy(bias_wide[:, 4 + n], bank[:, 0:384])
        last.then_inc(bias_sb, 1)
        v.wait_ge(sq_pair, 1)
        V.tensor_reduce(sq_sum[:, 0], x_sq[:].rearrange("p t s -> p s t"), AX.X, ALU.add)
        V.memset(sq_sum[:, 1], 0.0).then_inc(sq_ready, 1)
        V.memset(small[:], 0.0).then_inc(acc_free, 1)
        V.memset(stats[:], 0.0).then_inc(acc_free, 1)
        for n in range(AHEAD):
            v.wait_ge(hi_ready, n + 1)
            V.tensor_tensor(w_lo[:, n], raw[:, n], w_hi[:, n].bitcast(F32), ALU.subtract).then_inc(split_ready, 1)
        v.wait_ge(consts_in, 32)
        norm_stats(1)

        with v.Fori(0, L) as l:
            pieces = v.snap(l * PIECES)
            v.wait_ge(par_ready, l + 1)

            def normed(q):
                for s in range(4):
                    last = V.scalar_tensor_tensor((ev, th)[q % 2][:, s], x[:, 4 * q + s],
                                                  par[:, Q_NG + 4 * q + s:Q_NG + 4 * q + s + 1], rstd[:],
                                                  ALU.mult, ALU.mult)
                last.then_inc(piece_src, 1)

            def normed_low(q):
                strips = slice(4 * q, 4 * q + 4)
                piece(pieces + (q + 1), act[:, strips, S:2 * S], (ev, th)[q % 2][:], act[:, strips, 0:S])

            normed(0)
            normed(1)
            v.drain()
            normed_low(0)
            v.drain()
            normed(2)
            normed_low(1)
            v.drain()
            normed(3)
            v.drain()
            normed_low(2)
            normed_low(3)
            c = v.snap(l * CHUNKS + C_A)
            g2 = v.snap(2 * (l * GROUPS + G_A))
            f_in, i_in, e_f, u_f, r_f, z_f, z2, ser, neg_m, m_b, _, one4 = (t[0:4, :] for t in gi)
            for j in range(16):
                split_ahead(c, j)
                if j % 8 == 7:
                    empty(g2, lambda a, b: first[:, 4 * (j // 8) + a:4 * (j // 8) + b], group=j // 8)
                if j == 8:
                    v.drain()
                    V.tensor_scalar(f_in, first[32:36, 1], par[32:36, Q_FB:Q_FB + 1], None, ALU.add)
                    V.tensor_scalar(i_in, first[0:4, 1], par[0:4, Q_IB:Q_IB + 1], None, ALU.add)
                    V.memset(one4, 1.0)
                    v.drain()
                    V.scalar_tensor_tensor(e_f, f_in, -1.0, f_in, ALU.mult, ALU.max).then_inc(f_abs, 1)
                if j == 9:
                    v.wait_ge(f_exp, l + 1)
                    V.tensor_scalar(u_f, e_f, 2.0, None, ALU.add)
                    v.drain()
                    V.reciprocal(r_f, u_f)
                    v.drain()
                    V.tensor_tensor(z_f, e_f, r_f, ALU.mult)
                if j == 10:
                    v.drain()
                    V.tensor_tensor(z2, z_f, z_f, ALU.mult)
                    v.drain()
                    V.tensor_scalar(ser, z2, 1 / 17, None, ALU.mult)
                    for coef in LOG1P[:3]:
                        v.drain()
                        V.scalar_tensor_tensor(ser, ser, coef, z2, ALU.add, ALU.mult)
                if j == 11:
                    for coef in LOG1P[3:]:
                        v.drain()
                        V.scalar_tensor_tensor(ser, ser, coef, z2, ALU.add, ALU.mult)
                    v.drain()
                    V.scalar_tensor_tensor(ser, ser, 1.0, z_f, ALU.add, ALU.mult)
                    V.tensor_scalar(u_f, f_in, 0.0, None, ALU.min)
                if j == 12:
                    v.drain()
                    V.scalar_tensor_tensor(r_f, ser, -2.0, u_f, ALU.mult, ALU.add)
                    v.drain()
                    V.tensor_tensor_scan(z2, one4, r_f, 0.0, ALU.mult, ALU.add)
                    v.drain()
                    V.tensor_tensor(e_f, i_in, z2, ALU.subtract)
                    v.drain()
                    V.tensor_tensor_scan(z_f, e_f, e_f, 0.0, ALU.max, ALU.max)
                    v.drain()
                    V.tensor_tensor(m_b, z_f, z2, ALU.add).then_inc(m_sum, 1)
                if j == 13:
                    v.drain()
                    V.tensor_scalar(neg_m, z_f, -1.0, None, ALU.mult)
                    V.tensor_tensor(g_diag[0:4], e_f.rearrange("p (o s) -> p o s", o=1).to_broadcast([4, 4, S]),
                                    const[0:4, 0:4].rearrange("p (h o) -> p h o", o=1).to_broadcast([4, 4, S]), ALU.mult)
                    v.wait_ge(m_exp, l + 1)
                    V.memset(stats[:], 0.0).then_inc(g_ready, 1)
                if j == 15:
                    v.wait_ge(g_cols, l + 1)
                    V.tensor_copy(b_cols[:], ps_t[:, 0:16].rearrange("p (n h) -> p n h", n=4))
            with v.Fori(0, 4) as i:
                c = v.snap(l * CHUNKS + C_B + i * 8)
                g2 = v.snap(2 * (l * GROUPS + G_B + i))
                for j in range(8):
                    split_ahead(c, j)
                empty(g2, lambda a, b: first[:, bass.ds(8 + 4 * i + a, b - a), :])
            with v.Fori(0, 4) as i:
                c = v.snap(l * CHUNKS + C_H + i * 8)
                g2 = v.snap(2 * (l * GROUPS + G_H + i))
                n = v.snap(l * 4 + i)
                cp = v.snap(i * 10 + Q_CONV)
                for j in range(8):
                    split_ahead(c, j)
                    if j == 0:
                        v.drain()
                        for s in range(2):
                            src = first[:, bass.ds(8 + 4 * s + i, 1), :]
                            V.tensor_scalar(qk_conv[:, s], src, par[:, bass.ds(cp + (5 * s + 3), 1)],
                                            par[:, bass.ds(cp + (5 * s + 4), 1)], ALU.mult, ALU.add)
                        for back in range(1, 4):
                            v.drain()
                            for s in range(2):
                                src = first[:, bass.ds(8 + 4 * s + i, 1), 0:S - back]
                                last = V.scalar_tensor_tensor(
                                    qk_conv[:, s, back:S], src, par[:, bass.ds(cp + (5 * s + 3 - back), 1)],
                                    qk_conv[:, s, back:S], ALU.mult, ALU.add)
                        last.then_inc(b_conv, 1)
                    if j == 2:
                        v.wait_ge(b_tanh, n + 1)
                        V.scalar_tensor_tensor(qk[:], qk_tanh[:], 1.0, qk_conv[:], ALU.add, ALU.mult)
                        v.wait_ge(b_vg, n + 1)
                        V.tensor_tensor(t_log[:, 0:256], ps_g[:, 0:256], mask, ALU.add)
                        V.tensor_tensor(t_log[:, 256:384], ps_g[:, 0:128], mask[:, 128:256], ALU.add).then_inc(b_log, 1)
                    if j == 4:
                        v.wait_ge(b_exp, n + 1)
                        v.wait_ge(b_s, n + 1)
                        V.scalar_tensor_tensor(probs[:, 0:256], ps_s[:, 0:256], B_SCALE, probs[:, 0:256],
                                               ALU.mult, ALU.mult, accum_out=den[:, 1:2])
                        V.scalar_tensor_tensor(probs[:, 256:384], ps_s[:, 256:384], B_SCALE, probs[:, 256:384],
                                               ALU.mult, ALU.mult, accum_out=den[:, 0:1]).then_inc(b_sc, 1)
                        v.drain()
                        V.scalar_tensor_tensor(den_inv, den, -1.0, den, ALU.mult, ALU.max)
                        v.drain()
                        V.tensor_tensor(den_inv, den_inv, b_cols[:, 2:4, bass.ds(i, 1)].rearrange("p n o -> p (n o)"),
                                        ALU.max)
                        v.drain()
                        V.reciprocal(den_inv, den_inv)
                    if j == 7:
                        v.drain()
                        v.wait_ge(b_pv, n + 1 + FREE)
                        v.wait_ge(b_kept, n + FREE)
                        for t in range(2):
                            V.tensor_scalar(b_h[:, t], ps_o[:, t * S:(t + 1) * S], den_inv[:, t:t + 1], None, ALU.mult)
                        v.drain()
                        for t in range(2):
                            V.bn_stats(stats[:, t], b_h[:, t])
                        v.drain()
                        for t in range(2):
                            last = V.bn_aggr(mean_var[:, t], stats[:, t])
                        last.then_inc(b_out, 1)
                empty(g2, lambda a, b: ev[:, a:b])
                v.drain()
                v.wait_ge(th_ready, l * 18 + i + 1)
                V.scalar_tensor_tensor(ev[:, 2:4], th[:, 0:2], 1.0, ev[:, 2:4], ALU.add, ALU.mult)
                v.drain()
                V.scalar_tensor_tensor(y_bc[:, 0, bass.ds(2 * i, 2), :], th[:, 2:4], 1.0, ev[:, 2:4], ALU.add, ALU.mult)
            c = v.snap(l * CHUNKS + C_U)
            g2 = v.snap(2 * (l * GROUPS + G_U))

            def normed_head(b):
                for t in range(2):
                    last = V.tensor_scalar(b_norm[:, t], hb[:, b, t], b_mv[:, b, t, 0:1],
                                           b_var[:, 2 * b + t:2 * b + t + 1], ALU.subtract, ALU.mult)
                last.then_inc(n_in, 1)

            for j in range(28):
                split_ahead(c, j)
                if j < 16 and j % 8 == 7:
                    empty(g2, lambda a, b: ev[:, a:b], group=j // 8)
                    v.drain()
                    v.wait_ge(th_ready, l * 18 + (4 + j // 8 + 1))
                    V.scalar_tensor_tensor(y_bc[:, 1, 4 * (j // 8):4 * (j // 8) + 4], th[:], 1.0, ev[:], ALU.add, ALU.mult)
                if 16 <= j < 24 and j % 2 == 1:
                    empty(g2, lambda a, b: lat[:, (j - 16) // 2, a:b], strips=3, group=2 + (j - 16) // 2,
                          free=(x_saved, 16 * l + 16))
                if j >= 24:
                    empty(g2, lambda a, b: lat[:, j - 24, 3 + a:3 + b], group=6 + j - 24)
                if j == 1:
                    v.drain()
                    v.wait_ge(l_sums, l + 1)
                    V.tensor_scalar(th[:, 2], ps_g[:, 0:S], 1 / 512, EPS, ALU.mult, ALU.add)
                    V.tensor_scalar(th[:, 3], ps_g[:, S:2 * S], 1 / 256, EPS, ALU.mult, ALU.add)
                    v.wait_ge(b_kept, l * 4 + 4 + FREE)
                    V.tensor_scalar(b_var[:], b_mv[:, :, :, 1:2].rearrange("p b t o -> p (b t o)"), EPS, None,
                                    ALU.add).then_inc(l_var, 1)
                    V.tensor_tensor(z_tanh[:], ps_s[:, 0:S], sin, ALU.mult)
                    V.tensor_tensor(z_gate[:], first[:, 0], cos, ALU.mult)
                    v.drain()
                    V.tensor_tensor(kr[:], z_tanh[:], z_gate[:], ALU.add)
                if j == 2:
                    v.drain()
                    v.wait_ge(l_std, l + 1)
                    V.reciprocal(th[:, 2:4], th[:, 2:4])
                    V.reciprocal(b_var[:], b_var[:])
                    v.drain()
                    V.tensor_scalar(b_var[:], b_var[:], 0.25, None, ALU.mult)
                if j == 3:
                    v.drain()
                    for s in range(4):
                        last = V.scalar_tensor_tensor(ev[:, s], first[:, 4 + s], par[:, Q_QN + s:Q_QN + s + 1],
                                                      th[:, 2], ALU.mult, ALU.mult)
                    last.then_inc(piece_src, 1)
                if j == 4:
                    v.drain()
                    for s in range(2):
                        last = V.scalar_tensor_tensor(th[:, s], first[:, 2 + s], par[:, Q_KVN + s:Q_KVN + s + 1],
                                                      th[:, 3], ALU.mult, ALU.mult)
                    last.then_inc(piece_src, 1)
                    piece(pieces + 5, cq_act[:, :, S:2 * S], ev[:], cq_act[:, :, 0:S])
                if j == 5:
                    piece(pieces + 6, ckv_act[:, :, S:2 * S], th[:, 0:2], ckv_act[:, :, 0:S])
                if j == 6:
                    normed_head(0)
                if j in (8, 10, 12, 14):
                    b = (j - 8) // 2
                    v.wait_ge(n_t, l * 4 + (b + 1))
                    for s in range(2):
                        V.scalar_tensor_tensor(y_bc[:, 0, 2 * b + s], ps_t[:, s * S:(s + 1) * S],
                                               par[:, Q_ON + 2 * b + s:Q_ON + 2 * b + s + 1],
                                               y_bc[:, 0, 2 * b + s], ALU.mult, ALU.mult)
                    if b < 3:
                        normed_head(b + 1)
            with v.Fori(0, 4) as i:
                c = v.snap(l * CHUNKS + C_C + i * 16)
                g2 = v.snap(2 * (l * GROUPS + G_C + 2 * i))
                n = v.snap(l * 4 + i)
                h = v.snap(l * 16 + 2 * i)
                for j in range(16):
                    split_ahead(c, j)
                    if j % 8 == 7:
                        empty(g2, lambda a, b: moba[:, bass.ds(2 * i + j // 8, 1), a:b, :], group=j // 8)
                    if j == 3:
                        v.wait_ge(c_swap, n + 1)
                        V.tensor_tensor(c_rot[:, 0], ps_g[:, S:2 * S], sin, ALU.mult)
                        V.tensor_tensor(c_rot[:, 1], c_in[:, 2], cos, ALU.mult)
                        v.drain()
                        V.tensor_tensor(c_qr[:], c_rot[:, 0], c_rot[:, 1], ALU.add).then_inc(c_rope, 1)
                    for u in range(2):
                        s = 4 + 6 * u
                        if j == s + 1:
                            logits(C_SCALE, mask, mask[:, 128:256], h + (u + 1))
                        if j == s + 2:
                            norm_probs(h + (u + 1), None, None)
                        if j == s + 5:
                            v.wait_ge(h_pv, h + (u + 1))
                            y = y_bc[:, 1, bass.ds(2 * i + u, 1), :]
                            V.tensor_tensor(y, ps_o[:, 0:S].rearrange("p (o s) -> p o s", o=1), y, ALU.mult).then_inc(h_out, 1)
            V.memset(merged[:], 0.0)
            with v.Fori(0, 2) as n:
                for q in range(2):
                    strips = slice(4 * q, 4 * q + 4)
                    piece(pieces + n * 2 + (7 + q), y_act[:, strips, S:2 * S], y_bc[:, n, strips, :], y_act[:, strips, 0:S])
                with v.Fori(0, 4) as i:
                    c = v.snap(l * CHUNKS + C_G + n * 48 + i * 12)
                    g2 = v.snap(2 * (l * GROUPS + G_G + n * 8 + i * 2))
                    turn = v.snap(l * 12 + n * 4 + i)
                    head = v.snap(n * 4 + i)
                    h = v.snap(l * 16 + 8 + n * 4 + i)
                    for j in range(12):
                        split_ahead(c, j)
                        if j == 7:
                            empty(g2, lambda a, b: ev[:, a:b], free=(merged_done, turn + FREE))
                        if j == 11:
                            empty(g2, lambda a, b: ev[:, a:b], group=1, free=(th_ready, turn + l * 6 + 7))
                            v.drain()
                            V.scalar_tensor_tensor(ev[:], th[:], 1.0, ev[:], ALU.add, ALU.mult).then_inc(prod_ready, 1)
                        if j == 2:
                            if_first = bias[:, bass.ds(head, 1), :]
                            v.wait_ge(bias_ready, 16)
                            logits(A_SCALE, if_first.rearrange("p o s -> p (o s)"),
                                   bias[:, bass.ds(head, 1), 128:256].rearrange("p o s -> p (o s)"), h + 1)
                        if j == 3:
                            norm_probs(h + 1, a_in[:, 3], z_tanh[:])
                        if j == 6:
                            v.wait_ge(h_pv, h + 1)
                            V.tensor_tensor(moba[:, bass.ds(head, 1), 3, :], ps_o[:, 0:S].rearrange("p (o s) -> p o s", o=1),
                                            z_gate[:].rearrange("p (o s) -> p o s", o=1), ALU.mult).then_inc(h_out, 1)
            for q in range(2):
                strips = slice(4 * q, 4 * q + 4)
                piece(pieces + (11 + q), y_act[:, strips, S:2 * S], moba[:, strips, 3, :], y_act[:, strips, 0:S])
            with v.Fori(0, 4) as i:
                c = v.snap(l * CHUNKS + C_M + i * 12)
                g2 = v.snap(2 * (l * GROUPS + G_M + i * 2))
                turn = v.snap(l * 12 + 8 + i)
                for j in range(12):
                    split_ahead(c, j)
                    if j == 7:
                        empty(g2, lambda a, b: ev[:, a:b], free=(merged_done, turn + FREE))
                    if j == 11:
                        empty(g2, lambda a, b: ev[:, a:b], group=1, free=(th_ready, turn + l * 6 + 7))
                        v.drain()
                        V.scalar_tensor_tensor(ev[:], th[:], 1.0, ev[:], ALU.add, ALU.mult).then_inc(prod_ready, 1)
            v.wait_ge(merged_done, l * 12 + 12 + FREE)
            for q in range(4):
                strips = slice(4 * q, 4 * q + 4)
                piece(pieces + (13 + q), act[:, strips, S:2 * S], merged[:, strips], act[:, strips, 0:S], scale=0.5)
            with v.Fori(0, 4) as i:
                c = v.snap(l * CHUNKS + C_O + i * 8)
                g2 = v.snap(2 * (l * GROUPS + G_O + i))
                for j in range(8):
                    split_ahead(c, j)
                empty(g2, lambda a, b: ev[:, a:b], free=(x_added, 2 * (l * 4 + i) + FREE))
            norm_stats(l + 2)
        for q in range(4):
            for s in range(4 * q, 4 * q + 4):
                last = V.scalar_tensor_tensor(merged[:, s], x[:, s], par_all[:, L * NPAR + s:L * NPAR + s + 1], rstd[:],
                                              ALU.mult, ALU.mult)
            last.then_inc(final_ready, 1)

    @block.gpsimd
    def _(g):
        G = nc.gpsimd
        for n, free in enumerate((b_kept, merged_done, x_added)):
            G.memset(b_mv[:, n], 0.0).then_inc(free, FREE)
        g.wait_ge(bias_sb, 1)
        g.dma_start(bias_scratch.rearrange("h (p m) -> p h m", p=P), bias_wide[:]).then_inc(bias_out, 16)
        g.wait_ge(bias_out, 16)
        skewed = bias_scratch[:, 127:127 + P * 383].rearrange("h (p m) -> p h m", m=383)[:, :, 0:S]
        g.dma_start(bias[:], skewed).then_inc(bias_ready, 16)
        g.wait_ge(consts_in, 32)

        with g.Fori(0, L) as l:
            g.wait_ge(piece_lo, l * PIECES + FREE)
            G.tensor_copy(par[:], par_all[:, bass.ds(l * NPAR, NPAR)]).then_inc(par_ready, 1)
            g.wait_ge(acc_free, l * (2 * GROUPS) + (2 * G_B + 2))
            g.wait_ge(g_ready, l + 1)
            G.tensor_tensor(c_sq[:], first[:, 2:8], first[:, 2:8], ALU.mult)
            g.drain()
            G.tensor_tensor(c_sq[:, 0], c_sq[:, 0], c_sq[:, 1], ALU.add)
            G.tensor_tensor(c_sq[:, 2:4], c_sq[:, 2:4], c_sq[:, 4:6], ALU.add)
            g.drain()
            G.tensor_tensor(c_sq[:, 2], c_sq[:, 2], c_sq[:, 3], ALU.add).then_inc(c_squares, 1)
            with g.Fori(0, 4) as i:
                n = g.snap(l * 4 + i)
                g.wait_ge(acc_free, l * (2 * GROUPS) + (2 * G_H + 2))
                g.wait_ge(b_pv, n + FREE)
                g.wait_ge(g_cols, l + 1)
                G.tensor_copy(b_v[:], first[:, bass.ds(16 + 2 * i, 2), :]).then_inc(b_vs, 1)
                g.wait_ge(b_out, n + 1)
                G.tensor_copy(hb[:, bass.ds(i, 1)], b_h[:].rearrange("p (o t) s -> p o t s", o=1))
                G.tensor_copy(b_mv[:, bass.ds(i, 1)], mean_var[:].rearrange("p (o t) s -> p o t s", o=1)).then_inc(b_kept, 1)
            with g.Fori(0, 4) as i:
                g.wait_ge(acc_free, l * (2 * GROUPS) + (2 * G_C + 2))
                g.wait_ge(h_out, l * 16 + 2 * i + FREE)
                G.tensor_copy(c_in[:, 2], lat[:, bass.ds(i, 1), 2, :])
                G.tensor_copy(c_in[:, 0:2], lat[:, bass.ds(i, 1), 0:2, :]).then_inc(c_q_in, 1)
            def merge(turn, i):
                g.wait_ge(prod_ready, turn + 1)
                G.tensor_tensor(merged[:, bass.ds(4 * i, 4), :], merged[:, bass.ds(4 * i, 4), :], ev[:],
                                ALU.add).then_inc(merged_done, 1)

            with g.Fori(0, 2) as n:
                with g.Fori(0, 4) as i:
                    head = g.snap(n * 4 + i)
                    g.wait_ge(acc_free, l * (2 * GROUPS) + (2 * G_G + 2))
                    g.wait_ge(h_out, l * 16 + 8 + head + FREE)
                    G.tensor_copy(a_in[:], moba[:, bass.ds(head, 1)].rearrange("p o n s -> p (o n) s")).then_inc(a_staged, 1)
                    merge(l * 12 + head, i)
            with g.Fori(0, 4) as i:
                g.drain()
                merge(l * 12 + 8 + i, i)
            G.memset(sq_sum[:], 0.0)
            with g.Fori(0, 4) as i:
                a2 = g.snap(l * (2 * GROUPS) + 2 * G_O + 2 * i + 3)
                for q in range(2):
                    g.wait_ge(x_back, 16 * l + 16)
                    g.wait_ge(acc_free, a2 + q)
                    strips = x[:, bass.ds(4 * i + 2 * q, 2), :]
                    G.tensor_tensor(strips, strips, ev[:, 2 * q:2 * q + 2], ALU.add).then_inc(x_added, 1)
                    g.drain()
                    G.tensor_tensor(sq_new[:], strips, strips, ALU.mult)
                    g.drain()
                    last = G.tensor_tensor(sq_sum[:], sq_sum[:], sq_new[:], ALU.add)
                    g.drain()
                last.then_inc(sq_pair, 1)

    block_cm.__exit__(None, None, None)


def _stream(w_in, w_uq, w_ukv, w_branch, w_out):
    out = np.zeros((TOTAL, P, 2, 512), np.float32)
    n = 0

    def put(m):
        nonlocal n
        k = m.shape[0] // 256
        out[n:n + k, :, :, :m.shape[1]] = m.reshape(k, 2, P, m.shape[1]).transpose(0, 2, 1, 3)
        n += k

    for l in range(L):
        w, uq, ukv = w_in[l], w_uq[l], w_ukv[l]
        qa, ka, va, za, qb, kb, vb, ib, fb, ob, zb, cq, ckv, kr, zc, gt = np.cumsum(
            [0, 1024, 1024, 1024, 1024, 512, 512, 1024, 4, 4, 1024, 1024, 512, 256, 64, 1024])

        def cols(at, k=1):
            return w[:, at:at + 128 * k]

        gates = np.zeros((D, P), np.float32)
        gates[:, 0:4] = w[:, ib:ib + 4]
        gates[:, 32:36] = w[:, fb:fb + 4]
        put(np.concatenate([w[:, kr:kr + 64], w[:, kr:kr + 64], gates, cols(ckv, 2)], 1))
        for at in (cq, qb, kb, vb, vb + 512):
            put(cols(at, 4))
        for b in range(4):
            put(np.concatenate([cols(ob + 256 * b, 2), cols(zb + 256 * b, 2)], 1))
        put(cols(zc, 4))
        put(cols(zc + 512, 4))
        for p in range(4):
            a, b = 384 * p, 384 * p + 192
            put(np.concatenate([uq[:, a:a + 128], uq[:, b:b + 128], uq[:, a + 128:a + 192], uq[:, b + 128:b + 192]], 1))
        for p in range(4):
            a, b = 512 * p, 512 * p + 256
            put(np.concatenate([ukv[:, a:a + 128], ukv[:, b:b + 128], ukv[:, a + 128:a + 256], ukv[:, b + 128:b + 256]], 1))
        for h in range(8):
            put(np.concatenate([cols(at + 128 * h) for at in (qa, ka, va, za)], 1))
        for branch in (1, 2, 0):
            for g in range(4):
                put(cols(gt + branch * D + 512 * g, 4))
                put(w_branch[l, branch][:, 512 * g:512 * g + 512])
        for g in range(4):
            put(w_out[l][:, 512 * g:512 * g + 512])
    return out.reshape(TOTAL, P, 1024)


def _constants():
    c = np.zeros((P, 1024), np.float32)
    i = np.arange(P)
    c[:, 0:128] = np.eye(P)
    swap = i ^ 32
    c[swap, 128 + i] = 1.0
    c[:, 384:512] = np.where(i[None, :] > i[:, None], np.float32(NEG), np.float32(0))
    half = 32
    inv = np.float32(10000.0) ** (-np.arange(half, dtype=np.float32) / half)
    ang = np.arange(S, dtype=np.float32)[None, :] * inv.astype(np.float32)[i % half][:, None]
    c[:, 512:768] = np.cos(ang)
    c[:, 768:1024] = np.sin(ang) * np.where(i % 64 < 32, -1, 1)[:, None]
    d = 255 - np.arange(384)
    big = 16 + (np.log(np.maximum(d, 1).astype(np.float32) / 16) / np.log(128 / 16) * 16).astype(np.int32)
    bucket = np.where(d < 0, 32, np.where(d < 16, d, np.minimum(big, 31)))
    onehot = (np.arange(33)[:, None] == bucket[None, :]).astype(np.float32)
    return c, onehot


def kernel(**inputs):
    import concourse.bacc as _bacc
    from concourse.bass_utils import run_bass_kernel_spmd as _run

    f = {k: np.ascontiguousarray(v) for k, v in inputs.items()}
    consts, onehot = _constants()

    def strips(vec):
        return vec.reshape(-1, P).T

    par = np.zeros((P, L * NPAR + DT), np.float32)
    for l in range(L):
        q = par[:, l * NPAR:(l + 1) * NPAR]
        q[:, Q_NG:Q_NG + 16] = strips(f["norm_gain"][l])
        for b in range(4):
            for s in range(2):
                at = Q_CONV + 10 * b + 5 * s
                ch = slice(512 * s + 128 * b, 512 * s + 128 * b + 128)
                q[:, at:at + 4] = f["mlstm_conv_w"][l][:, ch].T
                q[:, at + 4] = f["mlstm_conv_b"][l][ch]
        q[:, Q_ON:Q_ON + 8] = strips(f["mlstm_out_norm"][l])
        q[:, Q_QN:Q_QN + 4] = strips(f["mla_q_norm"][l])
        q[:, Q_KVN:Q_KVN + 2] = strips(f["mla_kv_norm"][l])
        q[0:4, Q_IB] = f["mlstm_i_bias"][l]
        q[32:36, Q_FB] = f["mlstm_f_bias"][l]
    par[:, L * NPAR:] = strips(f["final_norm"])

    arrays = {
        "w": _stream(f["w_in"], f["mla_w_uq"], f["mla_w_ukv"], f["w_branch"], f["w_out"]),
        "xin": np.ascontiguousarray(f["x"][0].T.reshape(DT, P, S).transpose(1, 0, 2)),
        "consts": consts,
        "params": par,
        "table": f["t5_table"],
        "onehot": onehot,
    }
    nc = _bacc.Bacc("TRN2", target_bir_lowering=False, num_devices=1)
    args = [nc.dram_tensor(k, a.shape, F32, kind="ExternalInput").ap() for k, a in arrays.items()]
    args.append(nc.dram_tensor("out_t", (P, DT, S), F32, kind="ExternalOutput").ap())
    build(nc, *args)
    got = _run(nc, [arrays], core_ids=[0]).results[0]["out_t"]
    return np.ascontiguousarray(got.transpose(2, 1, 0).reshape(1, S, D))
```

```python
import numpy as np
import concourse.bass as bass
from concourse import mybir

F32, F32R = mybir.dt.float32, mybir.dt.float32r
ALU, ACT, AX = mybir.AluOpType, mybir.ActivationFunctionType, mybir.AxisListType

P = 128
L = 2
S = 256
D = 2048
DT = D // P
EPS = 1e-6
NEG = -1e30
RING = 4
AHEAD = 3
C_A, C_B, C_H, C_U, C_C, C_G, C_M, C_O = 0, 24, 48, 80, 108, 172, 268, 316
CHUNKS = 348
G_A, G_B, G_H, G_U, G_C, G_G, G_M, G_O = 0, 3, 6, 10, 20, 28, 44, 52
WIDTHS = [3] + [4] * 11 + [3] * 4 + [4] * 40
BEFORE = [sum(WIDTHS[:g]) for g in range(len(WIDTHS) + 1)]
EARLY = [BEFORE[g] - g for g in range(len(WIDTHS) + 1)]
STRIPS, EARLIES = BEFORE[-1], EARLY[-1]
TOTAL = L * CHUNKS + RING
FREE = 1
PC_G, PC_N, PC_Q, PC_KV, PC_Y, PC_M = 0, 8, 16, 17, 18, 24
PIECES = 28
EARLY_PIECES = 4
Q_NG, Q_CONV, Q_ON, Q_QN, Q_KVN, Q_IB, Q_FB, NPAR = 0, 16, 56, 64, 68, 70, 71, 72
A_SCALE = 128 ** -0.5
C_SCALE = 192 ** -0.5
B_SCALE = 128 ** -0.5 / 4
LOG1P = [1 / 15, 1 / 13, 1 / 11, 1 / 9, 1 / 7, 1 / 5, 1 / 3]


def build(nc, w, xin, consts, params, table, onehot, out):
    bias_scratch = nc.dram_tensor("bias_scratch", (8, P * 384), F32).ap()
    x_saved_dram = nc.dram_tensor("x_saved_dram", (P, DT * S), F32).ap()

    base = 16512
    offset = [base]

    def at(name, shape, dtype, where):
        return nc.alloc_sbuf_tensor_at(name, [P, *shape] if isinstance(shape, tuple) else shape, dtype, offset=where)

    def new(name, shape, dtype=F32):
        size = 4 * int(np.prod(shape))
        t = at(name, shape, dtype, offset[0])
        offset[0] += (size + 31) // 32 * 32
        return t

    def region(size):
        where = offset[0]
        offset[0] += size
        return where

    act = new("act", (DT, 512), F32R)
    raw = new("raw", (RING, 2, 512))
    w_hi = new("w_hi", (RING, 2, 512), F32R)
    w_lo = new("w_lo", (RING, 2, 512), F32R)
    r1 = region(32768)
    first = at("first", (23, S), F32, r1)
    hb = at("hb", (4, 2, S), F32, r1 + 24576)
    moba = at("moba", (8, 4, S), F32, r1)
    table_bc = at("table_bc", (8, P), F32, r1)
    bias_wide = at("bias_wide", (8, 384), F32, r1 + 4096)
    r2 = region(32768)
    lat = at("lat", (4, 7, S), F32, r2)
    y_act = at("y_act", (8, 512), F32R, r2)
    x = at("x", (DT, S), F32, r2)
    merged = at("merged", (DT, S), F32, r2 + 16384)
    x_sq = at("x_sq", (DT, S), F32, r2 + 16384)
    c_sq = at("c_sq", (6, S), F32, r2 + 16384)
    g_diag = at("g_diag", (4, S), F32, r2 + 16384 + 8192)
    y_bc = new("y_bc", (2, 8, S))
    bias = new("bias", (8, S))
    r3 = region(12288)
    gi = [at(f"gi{n}", (S,), F32, r3 + 1024 * n) for n in range(12)]
    qk_conv = at("qk_conv", (2, S), F32, r3)
    qk_tanh = at("qk_tanh", (2, S), F32, r3 + 2048)
    qk = at("qk", (2, S), F32, r3 + 4096)
    b_v = at("b_v", (2, S), F32, r3 + 6144)
    b_h = at("b_h", (2, S), F32, r3 + 8192)
    b_vt = at("b_vt", (2, S), F32, r3 + 10240)
    cq_act = at("cq_act", (4, 512), F32R, r3)
    ckv_act = at("ckv_act", (2, 512), F32R, r3 + 8192)
    c_in = at("c_in", (7, S), F32, r3)
    c_rot = at("c_rot", (2, S), F32, r3 + 7168)
    c_qr = at("c_qr", (S,), F32, r3 + 9216)
    a_in = at("a_in", (4, S), F32, r3)
    sq_sum = at("sq_sum", (2, S), F32, r3)
    sq_new = at("sq_new", (4, S), F32, r3 + 2048)
    onehot_sb = at("onehot_sb", (384,), F32, r3 + 6144)
    table_sb = at("table_sb", (8,), F32, r3 + 8192)
    carry = new("carry", (4, S))
    ev = new("ev", (4, S))
    th = new("th", (4, S))
    tp = region(3072)
    t_log = at("t_log", (384,), F32, tp)
    probs = at("probs", (384,), F32, tp + 1536)
    b_norm = at("b_norm", (2, S), F32, tp)
    c_rstd = at("c_rstd", (2, S), F32, tp)
    probs_t = new("probs_t", (384,))
    v_t = new("v_t", (S,))
    z_tanh = new("z_tanh", (S,))
    z_gate = new("z_gate", (S,))
    kr = new("kr", (S,))
    rstd = new("rstd", (S,))
    const = new("const", (1024,))
    ones = new("ones", (P,))
    par_all = new("par_all", (L * NPAR + DT,))
    par = new("par", (NPAR,))
    b_cols = new("b_cols", (4, 4))
    b_mv = new("b_mv", (4, 2, 2))
    b_var = new("b_var", (8,))
    small = new("small", (32,))
    stats = new("stats", (2, 6))
    mean_var = new("mean_var", (2, 2))
    assert offset[0] <= nc.sbuf_usable_end, offset[0]
    ones4 = ones[:, 0:1].rearrange("p (t s) -> p t s", t=1).to_broadcast([P, 4, S])
    ident, perm = const[:, 0:128], const[:, 128:256]
    mask, cos, sin = const[:, 256:512], const[:, 512:768], const[:, 768:1024]
    row_max, den, den_inv = small[:, 0:2], small[:, 8:10], small[:, 16:18]

    acc = nc.alloc_psum_tensor("acc", [P, 4, 512], F32)
    ps_s = nc.alloc_psum_tensor("ps_s", [P, 512], F32)
    ps_t = nc.alloc_psum_tensor("ps_t", [P, 512], F32)
    ps_o = nc.alloc_psum_tensor("ps_o", [P, 512], F32)
    ps_g = nc.alloc_psum_tensor("ps_g", [P, 512], F32)

    sem = nc.alloc_semaphore
    consts_in, params_in, table_in, x_in = sem("consts_in"), sem("params_in"), sem("table_in"), sem("x_in")
    raw_in = [sem(f"raw_in{r}") for r in range(RING)]
    hi_ready, split_ready, chunk_used = sem("hi_ready"), sem("split_ready"), sem("chunk_used")
    strip_done, carry_ready, acc_free = sem("strip_done"), sem("carry_ready"), sem("acc_free")
    piece_src, piece_hi, piece_lo = sem("piece_src"), sem("piece_hi"), sem("piece_lo")
    ones_ready, table_ready, bias_mm, bias_sb = sem("ones_ready"), sem("table_ready"), sem("bias_mm"), sem("bias_sb")
    bias_out, bias_ready = sem("bias_out"), sem("bias_ready")
    x_squared, sq_ready, sums_ready, var_ready, std_ready = (
        sem("x_squared"), sem("sq_ready"), sem("sums_ready"), sem("var_ready"), sem("std_ready"))
    par_ready, x_saved, x_back, x_added, gated = (
        sem("par_ready"), sem("x_saved"), sem("x_back"), sem("x_added"), sem("gated"))
    th_ready, prod_ready, merged_done = sem("th_ready"), sem("prod_ready"), sem("merged_done")
    f_abs, f_exp, m_sum, m_exp, g_ready, g_cols = (
        sem("f_abs"), sem("f_exp"), sem("m_sum"), sem("m_exp"), sem("g_ready"), sem("g_cols"))
    b_tap, b_conv, b_tanh, b_vs, b_g, b_log, b_exp, b_s, b_vt_mm, b_sc, b_den, b_pt, b_ptc, b_pv, b_hn, b_out, b_kept = (
        sem(f"b_{n}") for n in ("tap", "conv", "tanh", "vs", "g", "log", "exp", "s", "vt_mm", "sc", "den", "pt", "ptc",
                                "pv", "hn", "out", "kept"))
    c_squares, l_sums, l_var, l_std, n_in, n_t, n_out = (
        sem(n) for n in ("c_squares", "l_sums", "l_var", "l_std", "n_in", "n_t", "n_out"))
    c_r_in, c_q_in, c_kv_in, c_swap, c_rope = sem("c_r_in"), sem("c_q_in"), sem("c_kv_in"), sem("c_swap"), sem("c_rope")
    a_staged = sem("a_staged")
    h_scores, h_vt, h_max, h_exp, h_probs, h_pt, h_ptc, h_pv, h_out = (
        sem(f"h_{n}") for n in ("scores", "vt", "max", "exp", "probs", "pt", "ptc", "pv", "out"))
    stored, final_ready = sem("stored"), sem("final_ready")

    block_cm = nc.Block()
    block = block_cm.__enter__()

    @block.sync
    def _(sp):
        sp.dma_start(onehot_sb[0:33, :], onehot).then_inc(table_in, 16)
        sp.dma_start(table_sb[0:32, :], table).then_inc(table_in, 16)
        sp.dma_start(par_all[:], params).then_inc(params_in, 16)
        sp.dma_start(raw[:, 0], w[0]).then_inc(raw_in[0], 16)
        sp.dma_start(x[:], xin).then_inc(x_in, 16)
        for r in range(1, RING):
            sp.dma_start(raw[:, r], w[r]).then_inc(raw_in[r], 16)
        sp.dma_start(const[:], consts).then_inc(consts_in, 16)
        sp.wait_ge(x_in, 16)
        sp.dma_start(x_saved_dram, x[:].rearrange("p t s -> p (t s)")).then_inc(x_saved, 16)
        with sp.Fori(1, TOTAL // RING) as turn:
            for r in range(RING):
                sp.wait_ge(split_ready, RING * turn + (r - RING + 1))
                sp.dma_start(raw[:, r], w[RING * turn + r]).then_inc(raw_in[r], 16)
        for r in range(RING):
            sp.wait_ge(raw_in[r], 16 * (TOTAL // RING))
        sp.wait_ge(final_ready, 4)
        sp.dma_start(out, merged[:]).then_inc(stored, 16)
        sp.wait_ge(x_saved, 16 * (L + 1))
        sp.wait_ge(stored, 16)

    @block.tensor
    def _(pe):
        mm = nc.tensor.matmul

        def chunk(c, free, j, operand, k0, begin, end, strips=4):
            slot = j % RING
            pe.wait_ge(split_ready, c + (j + 1))
            for s in range(strips):
                if begin:
                    pe.wait_ge(acc_free, free(s))
                for kk in range(2):
                    mm(acc[:, s, :], w_hi[:, slot, kk, s * P:(s + 1) * P], operand[:, k0 + kk, :],
                       start=begin and kk == 0, stop=False)
                    last = mm(acc[:, s, 0:S], w_lo[:, slot, kk, s * P:(s + 1) * P], operand[:, k0 + kk, 0:S],
                              start=False, stop=end and kk == 1)
                if end and s < strips - 1:
                    last.then_inc(strip_done, 1)
            last.then_inc(chunk_used, 1)

        def after_four(e, group=0):
            return lambda s: e + (4 * group + s + 1)

        def after_layer_group(e0, group):
            def free(s):
                g = max((g for g in range(group) if WIDTHS[g] > s), default=None)
                return e0 + ((s - 4 if g is None else BEFORE[g] + s) + 5)
            return free

        def causal_scores(q, k):
            n = len(q)
            for cols, qs, ks in ((slice(0, 256), slice(128, 256), slice(0, 256)),
                                 (slice(256, 384), slice(0, 128), slice(0, 128))):
                for t in range(n):
                    last = mm(ps_s[:, cols], q[t][:, qs], k[t][:, ks], start=t == 0, stop=t == n - 1)
            return last

        def transpose_probs():
            nc.tensor.transpose(ps_t[:, 0:128], probs[:, 256:384], ident)
            nc.tensor.transpose(ps_t[:, 128:256], probs[:, 0:128], ident)
            return nc.tensor.transpose(ps_t[:, 256:384], probs[:, 128:256], ident)

        def head_scores(q, k, v):
            causal_scores(q, k)
            nc.tensor.transpose(ps_g[:, 0:128], v[:, 0:128], ident)
            nc.tensor.transpose(ps_g[:, 128:256], v[:, 128:256], ident).then_inc(h_scores, 1)

        def head_transposes(count):
            pe.wait_ge(h_probs, count)
            transpose_probs().then_inc(h_pt, 1)

        def head_values(count):
            pe.wait_ge(h_ptc, count)
            mm(ps_o[:, 0:256], v_t[:, 0:128], probs_t[:, 0:256], start=True, stop=False)
            mm(ps_o[:, 128:256], v_t[:, 128:256], probs_t[:, 256:384], start=False, stop=True).then_inc(h_pv, 1)

        def sum_squares(count):
            pe.wait_ge(sq_ready, count)
            mm(ps_g[:, 0:S], ones[:], sq_sum[:, 0], start=True, stop=False)
            mm(ps_g[:, 0:S], ones[:], sq_sum[:, 1], start=False, stop=True).then_inc(sums_ready, 1)

        pe.wait_ge(table_ready, 1)
        for h in range(8):
            bank = acc[:, h, 0:384] if h < 4 else (ps_s, ps_t, ps_o, ps_g)[h - 4][:, 0:384]
            last = mm(bank, table_bc[0:33, h, :], onehot_sb[0:33, :], start=True, stop=True)
            if h < 2:
                last.then_inc((chunk_used, b_pv)[h], FREE)
        last.then_inc(bias_mm, 1)
        pe.wait_ge(bias_sb, 1)
        pe.wait_ge(consts_in, 16)

        with pe.Fori(0, L) as l:
            pieces = pe.snap(l * PIECES + FREE)
            c = pe.snap(l * CHUNKS + C_A)
            e0 = pe.snap(l * STRIPS)
            for j in range(24):
                pe.wait_ge(piece_lo, pieces + ((PC_G if j < 8 else PC_N) + j % 8 + 1) if j < 16 else pieces + PC_Q)
                if j == 22:
                    pe.wait_ge(g_ready, l + 1)
                chunk(c, after_layer_group(e0, j // 8), j, act, 2 * (j % 8), j % 8 == 0, j % 8 == 7,
                      strips=WIDTHS[j // 8])
                if j == 3:
                    sum_squares(l + 1)
                if j == 22:
                    for n, rows in enumerate((gi[8], gi[10])):
                        for t in range(2):
                            last = nc.tensor.transpose(ps_t[:, 8 * n + 4 * t:8 * n + 4 * t + 4],
                                                       rows[0:4, t * P:(t + 1) * P], ident[0:4, 0:4])
                    last.then_inc(g_cols, 1)
            with pe.Fori(0, 3) as i:
                c = pe.snap(l * CHUNKS + C_B + i * 8)
                e = pe.snap(l * STRIPS + BEFORE[G_B] + 4 * i)
                for j in range(8):
                    chunk(c, after_four(e), j, act, 2 * j, j == 0, j == 7)
            with pe.Fori(0, 4) as i:
                c = pe.snap(l * CHUNKS + C_H + i * 8)
                e = pe.snap(l * STRIPS + BEFORE[G_H] + 4 * i)
                n = pe.snap(l * 4 + i)
                for j in range(8):
                    chunk(c, after_four(e), j, act, 2 * j, j == 0, j == 7)
                    if j == 0:
                        mm(ps_g[:, 0:S], ones[0:4, :], g_diag[0:4, i, :], start=True, stop=True).then_inc(b_g, 1)
                    if j == 4:
                        pe.wait_ge(b_vs, n + 1)
                        for t in range(2):
                            for s in range(2):
                                last = nc.tensor.transpose(ps_g[:, t * S + s * P:t * S + (s + 1) * P],
                                                           b_v[:, s, t * P:(t + 1) * P], ident)
                        last.then_inc(b_vt_mm, 1)
                    if j == 3:
                        pe.wait_ge(b_log, n + 1)
                        causal_scores([qk[:, 0]], [qk[:, 1]]).then_inc(b_s, 1)
                    if j == 5:
                        pe.wait_ge(b_sc, n + 1)
                        transpose_probs().then_inc(b_pt, 1)
                    if j == 6:
                        pe.wait_ge(b_ptc, n + 1)
                        mm(ps_o[:, 0:256], probs_t[:, 0:128], b_vt[:, 0], start=True, stop=True)
                        mm(ps_o[:, 256:512], probs_t[:, 128:256], b_vt[:, 0], start=True, stop=False)
                        mm(ps_o[:, 256:512], probs_t[:, 256:384], b_vt[:, 1], start=False, stop=True).then_inc(b_pv, 1)
            c = pe.snap(l * CHUNKS + C_U)
            for j in range(28):
                if j < 16:
                    chunk(c, after_layer_group(e0, G_U + j // 8), j, act, 2 * (j % 8), j % 8 == 0, j % 8 == 7)
                elif j < 24:
                    if j == 16:
                        pe.wait_ge(piece_lo, pieces + PC_Y)
                    chunk(c, after_layer_group(e0, G_U + 2 + (j - 16) // 2), j, cq_act, 2 * (j % 2), j % 2 == 0,
                          j % 2 == 1, strips=3)
                else:
                    chunk(c, after_layer_group(e0, G_U + 6 + j - 24), j, ckv_act, 0, True, True)
                if j == 0:
                    pe.wait_ge(c_squares, l + 1)
                    pe.wait_ge(b_out, l * 4 + 4)
                    mm(ps_g[:, 0:S], ones[:], c_sq[:, 2], start=True, stop=True)
                    mm(ps_g[:, S:2 * S], ones[:], c_sq[:, 0], start=True, stop=True)
                    for half in range(2):
                        rows = slice(64 * half, 64 * half + 64)
                        mm(ps_s[rows, 0:S], perm[0:64, 0:64], first[0:64, 0], start=True, stop=True)
                        last = mm(ps_o[rows, 0:S], ident[0:64, 0:64], first[0:64, 0], start=True, stop=True)
                    last.then_inc(l_sums, 1)
                if j in (7, 9, 11, 13):
                    b = (j - 7) // 2
                    pe.wait_ge(n_in, l * 4 + (b + 1))
                    for s in range(2):
                        for t in range(2):
                            last = nc.tensor.transpose(ps_t[:, s * S + t * P:s * S + (t + 1) * P],
                                                       b_norm[:, t, s * P:(s + 1) * P], ident)
                    last.then_inc(n_t, 1)
            with pe.Fori(0, 4) as i:
                c = pe.snap(l * CHUNKS + C_C + i * 16)
                e = pe.snap(l * STRIPS + BEFORE[G_C] + 8 * i)
                n = pe.snap(l * 4 + i)
                h = pe.snap(l * 16 + 2 * i)
                for j in range(16):
                    chunk(c, after_four(e, j // 8), j, act, 2 * (j % 8), j % 8 == 0, j % 8 == 7)
                    if j == 2:
                        pe.wait_ge(c_r_in, n + 1)
                        mm(ps_g[:, S:2 * S], perm, c_in[:, 2], start=True, stop=True).then_inc(c_swap, 1)
                    if j in (4, 10):
                        u = j // 10
                        if u == 0:
                            pe.wait_ge(c_rope, n + 1)
                            pe.wait_ge(c_q_in, n + 1)
                            pe.wait_ge(c_kv_in, n + 1)
                        rot = slice(64 * u, 64 * u + 64)
                        head_scores([c_in[:, u], c_qr[rot]], [c_in[:, 3 + u], kr[rot]], c_in[:, 5 + u])
                    if j in (7, 13):
                        head_transposes(h + ((j - 7) // 6 + 1))
                    if j in (8, 14):
                        head_values(h + ((j - 8) // 6 + 1))
            def gate_and_branch(c, e, j):
                if j < 8:
                    chunk(c, after_four(e), j, act, 2 * j, j == 0, j == 7)
                else:
                    chunk(c, after_four(e, 1), j, y_act, 2 * (j - 8), j == 8, j == 11)

            with pe.Fori(0, 2) as n:
                with pe.Fori(0, 4) as i:
                    c = pe.snap(l * CHUNKS + C_G + n * 48 + i * 12)
                    e = pe.snap(l * STRIPS + BEFORE[G_G] + n * 32 + i * 8)
                    h = pe.snap(l * 16 + 8 + n * 4 + i)
                    for j in range(12):
                        if j == 8:
                            pe.wait_ge(piece_lo, pieces + n * 2 + (PC_Y + 2))
                        gate_and_branch(c, e, j)
                        if j == 1:
                            pe.wait_ge(a_staged, l * 8 + n * 4 + i + 1)
                            head_scores([a_in[:, 0]], [a_in[:, 1]], a_in[:, 2])
                        if j == 4:
                            head_transposes(h + 1)
                        if j == 5:
                            head_values(h + 1)
            with pe.Fori(0, 4) as i:
                c = pe.snap(l * CHUNKS + C_M + i * 12)
                e = pe.snap(l * STRIPS + BEFORE[G_M] + i * 8)
                for j in range(12):
                    if j == 8:
                        pe.wait_ge(piece_lo, pieces + (PC_Y + 6))
                    gate_and_branch(c, e, j)
            with pe.Fori(0, 4) as i:
                c = pe.snap(l * CHUNKS + C_O + i * 8)
                e = pe.snap(l * STRIPS + BEFORE[G_O] + 4 * i)
                for j in range(8):
                    if j % 2 == 0:
                        pe.wait_ge(piece_lo, pieces + (PC_M + j // 2 + 1))
                    chunk(c, after_four(e), j, act, 2 * j, j == 0, j == 7)
        sum_squares(L + 1)

    @block.scalar
    def _(a):
        def split_ahead(c, j):
            m = j + AHEAD
            a.wait_ge(raw_in[m % RING], 4 * c + (16 * (m // RING) + 16))
            a.wait_ge(chunk_used, c + j + FREE)
            nc.scalar.activation(w_hi[:, m % RING], raw[:, m % RING], ACT.Copy).then_inc(hi_ready, 1)

        def empty(c, early, j, strips=4):
            for s in range(strips):
                if s < strips - 1:
                    a.wait_ge(strip_done, early + (s + 1))
                else:
                    a.wait_ge(chunk_used, c + (j + 1) + FREE)
                nc.scalar.copy(carry[:, s], acc[:, s, S:2 * S]).then_inc(carry_ready, 1)

        def gate_tanh(e):
            a.wait_ge(acc_free, e + 8)
            nc.scalar.activation(th[:], ev[:], ACT.Tanh, scale=0.5).then_inc(th_ready, 1)

        def piece(dst, src, scale=1.0):
            nc.scalar.activation(dst, src, ACT.Copy, scale=scale).then_inc(piece_hi, 1)

        def head_vt(count, z=None):
            a.wait_ge(h_scores, count)
            if z is not None:
                nc.scalar.activation(z_tanh[:], z, ACT.Tanh, scale=0.5)
            nc.scalar.copy(v_t[:], ps_g[:, 0:S])

        def exps(bias0, bias1, scale, done, sums):
            kw = ({}, {}) if not sums else (dict(accum_out=den[:, 1:2]), dict(accum_out=den[:, 0:1]))
            nc.scalar.activation(probs[:, 0:256], t_log[:, 0:256], ACT.Exp, bias=bias1, scale=scale, **kw[0])
            nc.scalar.activation(probs[:, 256:384], t_log[:, 256:384], ACT.Exp, bias=bias0, scale=scale,
                                 **kw[1]).then_inc(done, 1)

        def head_exp(count):
            a.wait_ge(h_max, count)
            exps(row_max[:, 0:1], row_max[:, 1:2], 1.0, h_exp, True)

        def head_pt(count):
            a.wait_ge(h_pt, count)
            nc.scalar.copy(probs_t[:], ps_t[:, 0:384]).then_inc(h_ptc, 1)

        def two_strips(k):
            return act[:, 2 * k:2 * k + 2, 0:S], (ev, th)[k // 2 % 2][:, 2 * (k % 2):2 * (k % 2) + 2]

        for n in range(AHEAD):
            a.wait_ge(raw_in[n], 16)
            nc.scalar.activation(w_hi[:, n], raw[:, n], ACT.Copy).then_inc(hi_ready, 1)
        for k in range(EARLY_PIECES):
            a.wait_ge(piece_src, k + 1)
            piece(*two_strips(k))
        nc.scalar.activation(x_sq[:], x[:], ACT.Square).then_inc(x_squared, 1)

        with a.Fori(0, L) as l:
            sources = a.snap(l * 18)
            c = a.snap(l * CHUNKS + C_A)
            early = a.snap(l * EARLIES)
            for j in range(24):
                split_ahead(c, j)
                if j < 8 - EARLY_PIECES:
                    k = j + EARLY_PIECES
                    a.wait_ge(piece_src, sources + (k + 1))
                    piece(*two_strips(k))
                if j == 4:
                    a.wait_ge(var_ready, l + 1)
                    nc.scalar.activation(rstd[:], rstd[:], ACT.Sqrt).then_inc(std_ready, 1)
                if j % 8 == 7:
                    empty(c, early + EARLY[j // 8], j, strips=WIDTHS[j // 8])
                if 6 <= j < 14:
                    k = j - 6
                    a.wait_ge(piece_src, sources + (8 + k + 1))
                    a.wait_ge(chunk_used, c + (k + 1) + FREE)
                    piece(*two_strips(k))
                if j == 15:
                    a.wait_ge(f_abs, l + 1)
                    nc.scalar.activation(gi[2][0:4], gi[2][0:4], ACT.Exp, scale=-1.0).then_inc(f_exp, 1)
                if j == 21:
                    a.wait_ge(m_sum, l + 1)
                    nc.scalar.activation(gi[10][0:4], gi[9][0:4], ACT.Exp, scale=-1.0).then_inc(m_exp, 1)
            with a.Fori(0, 3) as i:
                c = a.snap(l * CHUNKS + C_B + i * 8)
                for j in range(8):
                    split_ahead(c, j)
                empty(c, l * EARLIES + EARLY[G_B] + 3 * i, 7)
            with a.Fori(0, 4) as i:
                c = a.snap(l * CHUNKS + C_H + i * 8)
                n = a.snap(l * 4 + i)
                cp = a.snap(i * 10 + Q_CONV)
                for j in range(8):
                    split_ahead(c, j)
                    if j == 0:
                        a.wait_ge(acc_free, l * STRIPS + (BEFORE[G_H] + 4))
                        for s in range(2):
                            last = nc.scalar.activation(
                                qk_conv[:, s], first[:, bass.ds(7 + 4 * s + i, 1), :], ACT.Identity,
                                scale=par[:, bass.ds(cp + (5 * s + 3), 1)], bias=par[:, bass.ds(cp + (5 * s + 4), 1)])
                        last.then_inc(b_tap, 1)
                    if j == 1:
                        a.wait_ge(b_conv, n + 1)
                        nc.scalar.activation(qk_tanh[:], qk_conv[:], ACT.Tanh, scale=0.5).then_inc(b_tanh, 1)
                    if j == 2:
                        a.wait_ge(b_log, n + 1)
                        exps(b_cols[:, 0, bass.ds(i, 1)], b_cols[:, 1, bass.ds(i, 1)], 1.0, b_exp, False)
                    if j == 5:
                        a.wait_ge(b_vt_mm, n + 1)
                        nc.scalar.copy(b_vt[:], ps_g[:].rearrange("p (t s) -> p t s", t=2))
                    if j == 6:
                        a.wait_ge(b_pt, n + 1)
                        nc.scalar.copy(probs_t[:], ps_t[:, 0:384]).then_inc(b_ptc, 1)
                    if j == 7:
                        a.wait_ge(b_den, n + 1)
                        a.wait_ge(b_kept, n + FREE)
                        a.wait_ge(b_pv, n + 1 + FREE)
                        for t in range(2):
                            last = nc.scalar.activation(b_h[:, t], ps_o[:, t * S:(t + 1) * S], ACT.Copy,
                                                        scale=den_inv[:, t:t + 1])
                        last.then_inc(b_hn, 1)
                empty(c, l * EARLIES + EARLY[G_H] + 3 * i, 7)
                gate_tanh(l * STRIPS + BEFORE[G_H] + 4 * i)
            c = a.snap(l * CHUNKS + C_U)
            early = a.snap(l * EARLIES)
            for j in range(28):
                split_ahead(c, j)
                if j < 16 and j % 8 == 7:
                    empty(c, early + EARLY[G_U + j // 8], j)
                    gate_tanh(l * STRIPS + BEFORE[G_U + j // 8])
                if 16 <= j < 24 and j % 2 == 1:
                    empty(c, early + EARLY[G_U + 2 + (j - 16) // 2], j, strips=3)
                if j >= 24:
                    empty(c, early + EARLY[G_U + 6 + j - 24], j)
                if j == 1:
                    a.wait_ge(l_var, l + 1)
                    nc.scalar.activation(c_rstd[:], c_rstd[:], ACT.Sqrt)
                    nc.scalar.activation(b_var[:], b_var[:], ACT.Sqrt).then_inc(l_std, 1)
                if j == 4:
                    a.wait_ge(piece_src, l * 18 + 17)
                    piece(cq_act[:, :, 0:S], ev[:])
                if j == 5:
                    a.wait_ge(piece_src, l * 18 + 18)
                    piece(ckv_act[:, :, 0:S], th[:, 0:2])
            with a.Fori(0, 4) as i:
                c = a.snap(l * CHUNKS + C_C + i * 16)
                early = a.snap(l * EARLIES + EARLY[G_C] + 6 * i)
                n = a.snap(l * 4 + i)
                h = a.snap(l * 16 + 2 * i)
                for j in range(16):
                    split_ahead(c, j)
                    if j % 8 == 7:
                        empty(c, early + 3 * (j // 8), j)
                    if j == 0:
                        a.wait_ge(acc_free, l * STRIPS + (BEFORE[G_C] + 4))
                        a.wait_ge(h_out, h + FREE)
                        nc.scalar.copy(c_in[:, 3:7], lat[:, bass.ds(i, 1), 3:7, :].rearrange("p o n s -> p (o n) s")).then_inc(c_kv_in, 1)
                    for u in range(2):
                        s = 4 + 6 * u
                        if j == s + 1:
                            head_vt(h + (u + 1))
                            head_exp(h + (u + 1))
                        if j == s + 4:
                            head_pt(h + (u + 1))
            with a.Fori(0, 2) as n:
                a.wait_ge(h_out, l * 16 + 8 + FREE)
                a.wait_ge(chunk_used, l * CHUNKS + C_G + n * 48 + FREE)
                for q in range(2):
                    piece(y_act[:, 4 * q:4 * q + 4, 0:S], y_bc[:, n, 4 * q:4 * q + 4, :])
                with a.Fori(0, 4) as i:
                    c = a.snap(l * CHUNKS + C_G + n * 48 + i * 12)
                    early = a.snap(l * EARLIES + EARLY[G_G] + n * 24 + i * 6)
                    h = a.snap(l * 16 + 8 + n * 4 + i)
                    for j in range(12):
                        split_ahead(c, j)
                        if j == 7:
                            empty(c, early, 7)
                            gate_tanh(l * STRIPS + BEFORE[G_G] + n * 32 + i * 8)
                        if j == 11:
                            empty(c, early + 3, 11)
                        if j == 2:
                            head_vt(h + 1, a_in[:, 3])
                            head_exp(h + 1)
                        if j == 5:
                            head_pt(h + 1)
            a.wait_ge(h_out, l * 16 + 16 + FREE)
            a.wait_ge(chunk_used, l * CHUNKS + C_M + FREE)
            for q in range(2):
                piece(y_act[:, 4 * q:4 * q + 4, 0:S], moba[:, 4 * q:4 * q + 4, 3, :])

            def moba_gate_and_branch(i, merging):
                c = a.snap(l * CHUNKS + C_M + i * 12)
                early = a.snap(l * EARLIES + EARLY[G_M] + i * 6)
                for j in range(12):
                    split_ahead(c, j)
                    if j == 7:
                        empty(c, early, 7)
                        gate_tanh(l * STRIPS + BEFORE[G_M] + i * 8)
                    if j == 11:
                        empty(c, early + 3, 11)
                    if merging and 8 <= j < 11:
                        if j == 8:
                            a.wait_ge(merged_done, l * 12 + 11 + FREE)
                            a.wait_ge(chunk_used, c + 8 + FREE)
                        q = j - 8
                        piece(act[:, 4 * q:4 * q + 4, 0:S], merged[:, 4 * q:4 * q + 4], scale=0.5)

            with a.Fori(0, 3) as i:
                moba_gate_and_branch(i, False)
            moba_gate_and_branch(3, True)
            a.wait_ge(merged_done, l * 12 + 12 + FREE)
            piece(act[:, 12:16, 0:S], merged[:, 12:16], scale=0.5)
            a.wait_ge(chunk_used, l * CHUNKS + C_O + FREE)
            a.wait_ge(x_saved, 16 * l + 16)
            a.dma_start(x[:].rearrange("p t s -> p (t s)"), x_saved_dram).then_inc(x_back, 16)

            def output(i, preparing):
                c = a.snap(l * CHUNKS + C_O + i * 8)
                for j in range(8):
                    split_ahead(c, j)
                    if preparing and 4 <= j < 4 + EARLY_PIECES:
                        k = j - 4
                        a.wait_ge(piece_src, l * 18 + (18 + k + 1))
                        a.wait_ge(chunk_used, c + (k + 1) + FREE)
                        piece(*two_strips(k))
                empty(c, l * EARLIES + EARLY[G_O] + 3 * i, 7)
                a.wait_ge(x_added, l * 4 + i + 1)
                nc.scalar.activation(sq_new[:], x[:, bass.ds(4 * i, 4), :], ACT.Square).then_inc(x_squared, 1)

            with a.Fori(0, 3) as i:
                output(i, False)
            output(3, True)
            a.dma_start(x_saved_dram, x[:].rearrange("p t s -> p (t s)")).then_inc(x_saved, 16)
        a.wait_ge(var_ready, L + 1)
        nc.scalar.activation(rstd[:], rstd[:], ACT.Sqrt).then_inc(std_ready, 1)

    @block.vector
    def _(v):
        V = nc.vector

        def split_ahead(c, j):
            m = (j + AHEAD) % RING
            v.wait_ge(hi_ready, c + (j + AHEAD + 1))
            V.tensor_tensor(w_lo[:, m], raw[:, m], w_hi[:, m].bitcast(F32), ALU.subtract).then_inc(split_ready, 1)

        def empty(e, dst, strips=4, free=None):
            v.drain()
            if free is not None:
                v.wait_ge(*free)
            for s in range(strips):
                v.wait_ge(carry_ready, e + (s + 1))
                V.tensor_tensor(dst(s), acc[:, s:s + 1, 0:S], carry[:, s:s + 1], ALU.add).then_inc(acc_free, 1)

        def piece(count, dst, src, hi, scale=None):
            v.wait_ge(piece_hi, count)
            if scale is None:
                V.tensor_tensor(dst, src, hi.bitcast(F32), ALU.subtract).then_inc(piece_lo, 1)
            else:
                V.scalar_tensor_tensor(dst, src, scale, hi.bitcast(F32), ALU.mult, ALU.subtract).then_inc(piece_lo, 1)

        def logits(scale, bias1, bias0, count):
            v.wait_ge(h_scores, count)
            V.scalar_tensor_tensor(t_log[:, 0:256], ps_s[:, 0:256], scale, bias1, ALU.mult, ALU.add)
            V.scalar_tensor_tensor(t_log[:, 256:384], ps_s[:, 256:384], scale, bias0, ALU.mult, ALU.add)
            v.drain()
            V.tensor_reduce(row_max[:, 1:2], t_log[:, 0:256], AX.X, ALU.max, negate=True)
            V.tensor_reduce(row_max[:, 0:1], t_log[:, 256:384], AX.X, ALU.max, negate=True).then_inc(h_max, 1)

        def norm_probs(count, z, tanh):
            v.wait_ge(h_exp, count)
            V.reciprocal(den_inv, den)
            if z is not None:
                V.scalar_tensor_tensor(z_gate[:], tanh, 1.0, z, ALU.add, ALU.mult)
            v.drain()
            V.tensor_scalar(probs[:, 0:256], probs[:, 0:256], den_inv[:, 1:2], 0.5, ALU.mult, ALU.mult)
            V.tensor_scalar(probs[:, 256:384], probs[:, 256:384], den_inv[:, 0:1], 0.5, ALU.mult,
                            ALU.mult).then_inc(h_probs, 1)

        def norm_stats(count):
            v.wait_ge(sums_ready, count)
            V.tensor_scalar(rstd[:], ps_g[:, 0:S], 1.0 / D, EPS, ALU.mult, ALU.add).then_inc(var_ready, 1)
            v.wait_ge(std_ready, count)
            V.reciprocal(rstd[:], rstd[:])
            v.drain()

        V.memset(ones[:], 1.0).then_inc(h_out, FREE)
        V.memset(table_bc[32:33], NEG).then_inc(piece_lo, FREE)
        v.wait_ge(table_in, 32)
        V.tensor_copy(table_bc[0:32], table_sb[0:32].rearrange("p (h o) -> p h o", o=1).to_broadcast([32, 8, P])
                      ).then_inc(table_ready, 1)
        v.wait_ge(bias_mm, 1)
        V.tensor_copy(bias_wide[:, 0:4], acc[:, :, 0:384])
        for n, bank in enumerate((ps_s, ps_t, ps_o, ps_g)):
            last = V.tensor_copy(bias_wide[:, 4 + n], bank[:, 0:384])
        last.then_inc(bias_sb, 1)
        for _ in range(4):
            v.drain()
            V.memset(stats[:], 0.0).then_inc(acc_free, 1)

        def two_strips(k):
            return (ev, th)[k // 2 % 2][:, 2 * (k % 2):2 * (k % 2) + 2], act[:, 2 * k:2 * k + 2]

        def gained(k, l):
            for s in range(2):
                last = V.tensor_scalar(two_strips(k)[0][:, s], x[:, 2 * k + s],
                                       par_all[:, bass.ds(l * NPAR + (2 * k + s), 1)], None, ALU.mult)
            last.then_inc(piece_src, 1)

        def normed(k):
            for s in range(2):
                last = V.scalar_tensor_tensor(two_strips(k)[0][:, s], x[:, 2 * k + s],
                                              par[:, Q_NG + 2 * k + s:Q_NG + 2 * k + s + 1], rstd[:], ALU.mult, ALU.mult)
            last.then_inc(piece_src, 1)

        def low(k, count):
            src, dst = two_strips(k)
            piece(count, dst[:, :, S:2 * S], src, dst[:, :, 0:S])

        v.wait_ge(x_in, 16)
        v.wait_ge(params_in, 16)
        for k in range(EARLY_PIECES):
            gained(k, 0)
        v.wait_ge(hi_ready, 1)
        V.tensor_tensor(w_lo[:, 0], raw[:, 0], w_hi[:, 0].bitcast(F32), ALU.subtract).then_inc(split_ready, 1)
        v.drain()
        for k in range(EARLY_PIECES):
            low(k, k + 1)
        for n in range(1, AHEAD):
            v.wait_ge(hi_ready, n + 1)
            V.tensor_tensor(w_lo[:, n], raw[:, n], w_hi[:, n].bitcast(F32), ALU.subtract).then_inc(split_ready, 1)
        v.wait_ge(x_squared, 1)
        V.tensor_reduce(sq_sum[:, 0], x_sq[:].rearrange("p t s -> p s t"), AX.X, ALU.add)
        V.memset(sq_sum[:, 1], 0.0).then_inc(sq_ready, 1)

        with v.Fori(0, L) as l:
            pieces = v.snap(l * PIECES)
            e0 = v.snap(l * STRIPS)
            c = v.snap(l * CHUNKS + C_A)
            f_in, i_in, e_f, u_f, r_f, z_f, z2, ser, neg_m, m_b, _, one4 = (t[0:4, :] for t in gi)
            for j in range(24):
                if j % 8 == 7:
                    empty(e0 + BEFORE[j // 8], lambda s: first[:, BEFORE[j // 8] + s:BEFORE[j // 8] + s + 1],
                          strips=WIDTHS[j // 8])
                    if j == 7:
                        v.drain()
                        for s in range(3):
                            V.tensor_tensor(first[:, s], first[:, s], rstd[:], ALU.mult)
                split_ahead(c, j)
                if j < 8 - EARLY_PIECES:
                    k = j + EARLY_PIECES
                    v.drain()
                    gained(k, l)
                    v.drain()
                    low(k, pieces + (k + 1))
                if j == 4:
                    v.drain()
                    v.wait_ge(sums_ready, l + 1)
                    V.tensor_scalar(rstd[:], ps_g[:, 0:S], 1.0 / D, EPS, ALU.mult, ALU.add).then_inc(var_ready, 1)
                if j == 5:
                    v.drain()
                    v.wait_ge(std_ready, l + 1)
                    V.reciprocal(rstd[:], rstd[:])
                    v.wait_ge(par_ready, l + 1)
                if 6 <= j < 14:
                    v.drain()
                    normed(j - 6)
                    v.drain()
                    low(j - 6, pieces + (8 + j - 6 + 1))
                if j == 14:
                    v.drain()
                    V.tensor_scalar(f_in, first[96:100, 0], par[96:100, Q_FB:Q_FB + 1], None, ALU.add)
                    V.tensor_scalar(i_in, first[64:68, 0], par[64:68, Q_IB:Q_IB + 1], None, ALU.add)
                    V.memset(one4, 1.0)
                    v.drain()
                    V.scalar_tensor_tensor(e_f, f_in, -1.0, f_in, ALU.mult, ALU.max).then_inc(f_abs, 1)
                if j == 16:
                    v.wait_ge(f_exp, l + 1)
                    V.tensor_scalar(u_f, e_f, 2.0, None, ALU.add)
                    v.drain()
                    V.reciprocal(r_f, u_f)
                    v.drain()
                    V.tensor_tensor(z_f, e_f, r_f, ALU.mult)
                if j == 17:
                    v.drain()
                    V.tensor_tensor(z2, z_f, z_f, ALU.mult)
                    v.drain()
                    V.tensor_scalar(ser, z2, 1 / 17, None, ALU.mult)
                    for coef in LOG1P[:3]:
                        v.drain()
                        V.scalar_tensor_tensor(ser, ser, coef, z2, ALU.add, ALU.mult)
                if j == 18:
                    for coef in LOG1P[3:]:
                        v.drain()
                        V.scalar_tensor_tensor(ser, ser, coef, z2, ALU.add, ALU.mult)
                    v.drain()
                    V.scalar_tensor_tensor(ser, ser, 1.0, z_f, ALU.add, ALU.mult)
                    V.tensor_scalar(u_f, f_in, 0.0, None, ALU.min)
                if j == 19:
                    v.drain()
                    V.scalar_tensor_tensor(r_f, ser, -2.0, u_f, ALU.mult, ALU.add)
                    v.drain()
                    V.tensor_tensor_scan(z2, one4, r_f, 0.0, ALU.mult, ALU.add)
                if j == 20:
                    v.drain()
                    V.tensor_tensor(e_f, i_in, z2, ALU.subtract)
                    v.drain()
                    V.tensor_tensor_scan(z_f, e_f, e_f, 0.0, ALU.max, ALU.max)
                    v.drain()
                    V.tensor_tensor(m_b, z_f, z2, ALU.add).then_inc(m_sum, 1)
                if j == 21:
                    v.drain()
                    V.tensor_scalar(neg_m, z_f, -1.0, None, ALU.mult)
                    V.tensor_tensor(g_diag[0:4], e_f.rearrange("p (o s) -> p o s", o=1).to_broadcast([4, 4, S]),
                                    const[0:4, 0:4].rearrange("p (h o) -> p h o", o=1).to_broadcast([4, 4, S]), ALU.mult)
                    v.wait_ge(m_exp, l + 1)
                    V.memset(stats[:], 0.0).then_inc(g_ready, 1)
                if j == 23:
                    v.wait_ge(g_cols, l + 1)
                    V.tensor_copy(b_cols[:], ps_t[:, 0:16].rearrange("p (n h) -> p n h", n=4))
            with v.Fori(0, 3) as i:
                c = v.snap(l * CHUNKS + C_B + i * 8)
                for j in range(8):
                    if j == 7:
                        empty(l * STRIPS + BEFORE[G_B] + 4 * i, lambda s: first[:, bass.ds(11 + 4 * i + s, 1), :])
                    split_ahead(c, j)
            with v.Fori(0, 4) as i:
                c = v.snap(l * CHUNKS + C_H + i * 8)
                n = v.snap(l * 4 + i)
                cp = v.snap(i * 10 + Q_CONV)
                for j in range(8):
                    if j == 7:
                        empty(l * STRIPS + BEFORE[G_H] + 4 * i, lambda s: ev[:, s:s + 1], free=(gated, l * 6 + i + FREE))
                    split_ahead(c, j)
                    if j == 0:
                        v.wait_ge(b_tap, n + 1)
                        for back in range(1, 4):
                            if back > 1:
                                v.drain()
                            for s in range(2):
                                src = first[:, bass.ds(7 + 4 * s + i, 1), 0:S - back]
                                last = V.scalar_tensor_tensor(
                                    qk_conv[:, s, back:S], src, par[:, bass.ds(cp + (5 * s + 3 - back), 1)],
                                    qk_conv[:, s, back:S], ALU.mult, ALU.add)
                        last.then_inc(b_conv, 1)
                    if j == 2:
                        v.wait_ge(b_tanh, n + 1)
                        V.scalar_tensor_tensor(qk[:], qk_tanh[:], 1.0, qk_conv[:], ALU.add, ALU.mult)
                        v.wait_ge(b_g, n + 1)
                        V.tensor_tensor(t_log[:, 0:256], ps_g[:, 0:256], mask, ALU.add)
                        V.tensor_tensor(t_log[:, 256:384], ps_g[:, 0:128], mask[:, 128:256], ALU.add).then_inc(b_log, 1)
                    if j == 4:
                        v.wait_ge(b_exp, n + 1)
                        v.wait_ge(b_s, n + 1)
                        V.scalar_tensor_tensor(probs[:, 0:256], ps_s[:, 0:256], B_SCALE, probs[:, 0:256],
                                               ALU.mult, ALU.mult, accum_out=den[:, 1:2])
                        V.scalar_tensor_tensor(probs[:, 256:384], ps_s[:, 256:384], B_SCALE, probs[:, 256:384],
                                               ALU.mult, ALU.mult, accum_out=den[:, 0:1]).then_inc(b_sc, 1)
                        v.drain()
                        V.scalar_tensor_tensor(den_inv, den, -1.0, den, ALU.mult, ALU.max)
                        v.drain()
                        V.tensor_tensor(den_inv, den_inv, b_cols[:, 2:4, bass.ds(i, 1)].rearrange("p n o -> p (n o)"),
                                        ALU.max)
                        v.drain()
                        V.reciprocal(den_inv, den_inv).then_inc(b_den, 1)
                    if j == 7:
                        v.wait_ge(b_hn, n + 1)
                        for t in range(2):
                            V.bn_stats(stats[:, t], b_h[:, t])
                        v.drain()
                        for t in range(2):
                            last = V.bn_aggr(mean_var[:, t], stats[:, t])
                        last.then_inc(b_out, 1)
            c = v.snap(l * CHUNKS + C_U)

            def normed_head(b):
                for t in range(2):
                    last = V.tensor_scalar(b_norm[:, t], hb[:, b, t], b_mv[:, b, t, 0:1],
                                           b_var[:, 2 * b + t:2 * b + t + 1], ALU.subtract, ALU.mult)
                last.then_inc(n_in, 1)

            for j in range(28):
                if j < 16 and j % 8 == 7:
                    empty(e0 + BEFORE[G_U + j // 8], lambda s: ev[:, s:s + 1], free=(gated, l * 6 + 4 + j // 8 + FREE))
                if 16 <= j < 24 and j % 2 == 1:
                    p = (j - 16) // 2
                    empty(e0 + BEFORE[G_U + 2 + p], lambda s: lat[:, p, s:s + 1], strips=3, free=(x_saved, 16 * l + 16))
                if j >= 24:
                    empty(e0 + BEFORE[G_U + 6 + j - 24], lambda s: lat[:, j - 24, 3 + s:4 + s])
                split_ahead(c, j)
                if j == 1:
                    v.drain()
                    v.wait_ge(l_sums, l + 1)
                    V.tensor_scalar(c_rstd[:, 0], ps_g[:, 0:S], 1 / 512, EPS, ALU.mult, ALU.add)
                    V.tensor_scalar(c_rstd[:, 1], ps_g[:, S:2 * S], 1 / 256, EPS, ALU.mult, ALU.add)
                    v.wait_ge(b_kept, l * 4 + 4 + FREE)
                    V.tensor_scalar(b_var[:], b_mv[:, :, :, 1:2].rearrange("p b t o -> p (b t o)"), EPS, None,
                                    ALU.add).then_inc(l_var, 1)
                    V.tensor_tensor(z_tanh[:], ps_s[:, 0:S], sin, ALU.mult)
                    V.tensor_tensor(z_gate[:], ps_o[:, 0:S], cos, ALU.mult)
                    v.drain()
                    V.tensor_tensor(kr[:], z_tanh[:], z_gate[:], ALU.add)
                if j == 2:
                    v.drain()
                    v.wait_ge(l_std, l + 1)
                    V.reciprocal(c_rstd[:], c_rstd[:])
                    V.reciprocal(b_var[:], b_var[:])
                    v.drain()
                    V.tensor_scalar(b_var[:], b_var[:], 0.25, None, ALU.mult)
                if j == 3:
                    v.drain()
                    v.wait_ge(gated, l * 6 + 4 + FREE)
                    for s in range(4):
                        last = V.scalar_tensor_tensor(ev[:, s], first[:, 3 + s], par[:, Q_QN + s:Q_QN + s + 1],
                                                      c_rstd[:, 0], ALU.mult, ALU.mult)
                    last.then_inc(piece_src, 1)
                if j == 4:
                    v.drain()
                    for s in range(2):
                        last = V.scalar_tensor_tensor(th[:, s], first[:, 1 + s], par[:, Q_KVN + s:Q_KVN + s + 1],
                                                      c_rstd[:, 1], ALU.mult, ALU.mult)
                    last.then_inc(piece_src, 1)
                    piece(pieces + (PC_Q + 1), cq_act[:, :, S:2 * S], ev[:], cq_act[:, :, 0:S])
                if j == 5:
                    piece(pieces + (PC_KV + 1), ckv_act[:, :, S:2 * S], th[:, 0:2], ckv_act[:, :, 0:S])
                if j == 6:
                    normed_head(0)
                if j in (8, 10, 12, 14):
                    b = (j - 8) // 2
                    v.wait_ge(n_t, l * 4 + (b + 1))
                    for s in range(2):
                        V.scalar_tensor_tensor(y_bc[:, 0, 2 * b + s], ps_t[:, s * S:(s + 1) * S],
                                               par[:, Q_ON + 2 * b + s:Q_ON + 2 * b + s + 1],
                                               y_bc[:, 0, 2 * b + s], ALU.mult, ALU.mult)
                    if b < 3:
                        normed_head(b + 1)
            with v.Fori(0, 4) as i:
                v.wait_ge(gated, l * 6 + 6 + FREE)
                c = v.snap(l * CHUNKS + C_C + i * 16)
                n = v.snap(l * 4 + i)
                h = v.snap(l * 16 + 2 * i)
                for j in range(16):
                    if j % 8 == 7:
                        empty(l * STRIPS + BEFORE[G_C] + 8 * i + 4 * (j // 8),
                              lambda s: moba[:, bass.ds(2 * i + j // 8, 1), s, :])
                    split_ahead(c, j)
                    if j == 3:
                        v.wait_ge(c_swap, n + 1)
                        V.tensor_tensor(c_rot[:, 0], ps_g[:, S:2 * S], sin, ALU.mult)
                        V.tensor_tensor(c_rot[:, 1], c_in[:, 2], cos, ALU.mult)
                        v.drain()
                        V.tensor_tensor(c_qr[:], c_rot[:, 0], c_rot[:, 1], ALU.add).then_inc(c_rope, 1)
                    for u in range(2):
                        s = 4 + 6 * u
                        if j == s + 1:
                            logits(C_SCALE, mask, mask[:, 128:256], h + (u + 1))
                        if j == s + 2:
                            norm_probs(h + (u + 1), None, None)
                        if j == s + 5:
                            v.wait_ge(h_pv, h + (u + 1))
                            y = y_bc[:, 1, bass.ds(2 * i + u, 1), :]
                            V.tensor_tensor(y, ps_o[:, 0:S].rearrange("p (o s) -> p o s", o=1), y, ALU.mult).then_inc(h_out, 1)
            V.memset(merged[:], 0.0)
            def gate_and_branch(e, turn, j):
                if j == 7:
                    empty(e, lambda s: ev[:, s:s + 1], free=(merged_done, turn + FREE))
                if j == 11:
                    empty(e + 4, lambda s: ev[:, s:s + 1], free=(th_ready, turn + l * 6 + 7))

            def weight():
                v.drain()
                V.scalar_tensor_tensor(ev[:], th[:], 1.0, ev[:], ALU.add, ALU.mult).then_inc(prod_ready, 1)

            with v.Fori(0, 2) as n:
                for q in range(2):
                    strips = slice(4 * q, 4 * q + 4)
                    piece(pieces + n * 2 + (PC_Y + q + 1), y_act[:, strips, S:2 * S], y_bc[:, n, strips, :],
                          y_act[:, strips, 0:S])
                with v.Fori(0, 4) as i:
                    c = v.snap(l * CHUNKS + C_G + n * 48 + i * 12)
                    e = v.snap(l * STRIPS + BEFORE[G_G] + n * 32 + i * 8)
                    turn = v.snap(l * 12 + n * 4 + i)
                    head = v.snap(n * 4 + i)
                    h = v.snap(l * 16 + 8 + n * 4 + i)
                    for j in range(12):
                        gate_and_branch(e, turn, j)
                        split_ahead(c, j)
                        if j == 11:
                            weight()
                        if j == 2:
                            v.wait_ge(bias_ready, 16)
                            logits(A_SCALE, bias[:, bass.ds(head, 1), :].rearrange("p o s -> p (o s)"),
                                   bias[:, bass.ds(head, 1), 128:256].rearrange("p o s -> p (o s)"), h + 1)
                        if j == 3:
                            norm_probs(h + 1, a_in[:, 3], z_tanh[:])
                        if j == 6:
                            v.wait_ge(h_pv, h + 1)
                            V.tensor_tensor(moba[:, bass.ds(head, 1), 3, :], ps_o[:, 0:S].rearrange("p (o s) -> p o s", o=1),
                                            z_gate[:].rearrange("p (o s) -> p o s", o=1), ALU.mult).then_inc(h_out, 1)
            for q in range(2):
                strips = slice(4 * q, 4 * q + 4)
                piece(pieces + (PC_Y + 4 + q + 1), y_act[:, strips, S:2 * S], moba[:, strips, 3, :], y_act[:, strips, 0:S])

            def merged_low(q):
                strips = slice(4 * q, 4 * q + 4)
                piece(pieces + (PC_M + q + 1), act[:, strips, S:2 * S], merged[:, strips], act[:, strips, 0:S], scale=0.5)

            def moba_gate_and_branch(i, merging):
                c = v.snap(l * CHUNKS + C_M + i * 12)
                e = v.snap(l * STRIPS + BEFORE[G_M] + i * 8)
                turn = v.snap(l * 12 + 8 + i)
                for j in range(12):
                    gate_and_branch(e, turn, j)
                    if j == 11:
                        weight()
                    split_ahead(c, j)
                    if merging and 8 <= j < 11:
                        merged_low(j - 8)

            with v.Fori(0, 3) as i:
                moba_gate_and_branch(i, False)
            moba_gate_and_branch(3, True)
            merged_low(3)
            V.memset(sq_sum[:], 0.0)

            def output(i, preparing):
                c = v.snap(l * CHUNKS + C_O + i * 8)
                for j in range(8):
                    if j == 7:
                        empty(l * STRIPS + BEFORE[G_O] + 4 * i, lambda s: ev[:, s:s + 1])
                        v.drain()
                        v.wait_ge(x_back, 16 * l + 16)
                        strips = x[:, bass.ds(4 * i, 4), :]
                        V.tensor_tensor(strips, strips, ev[:], ALU.add).then_inc(x_added, 1)
                    split_ahead(c, j)
                    if preparing and 4 <= j < 4 + EARLY_PIECES:
                        k = j - 4
                        if k == 0:
                            v.drain()
                            for early in range(EARLY_PIECES):
                                gained(early, l + 1)
                            v.drain()
                        low(k, pieces + (PIECES + k + 1))
                for q in range(2):
                    v.wait_ge(x_squared, l * 4 + i + 2)
                    last = V.tensor_tensor(sq_sum[:], sq_sum[:], sq_new[:, 2 * q:2 * q + 2], ALU.add)
                    v.drain()

            with v.Fori(0, 3) as i:
                output(i, False)
            output(3, True)
            V.memset(stats[:], 0.0).then_inc(sq_ready, 1)
        norm_stats(L + 1)
        for q in range(4):
            for s in range(4 * q, 4 * q + 4):
                last = V.scalar_tensor_tensor(merged[:, s], x[:, s], par_all[:, L * NPAR + s:L * NPAR + s + 1], rstd[:],
                                              ALU.mult, ALU.mult)
            last.then_inc(final_ready, 1)

    @block.gpsimd
    def _(g):
        G = nc.gpsimd
        for n, free in enumerate((b_kept, merged_done, gated)):
            G.memset(b_mv[:, n], 0.0).then_inc(free, FREE)
        g.wait_ge(bias_sb, 1)
        g.dma_start(bias_scratch.rearrange("h (p m) -> p h m", p=P), bias_wide[:]).then_inc(bias_out, 16)
        g.wait_ge(bias_out, 16)
        skewed = bias_scratch[:, 127:127 + P * 383].rearrange("h (p m) -> p h m", m=383)[:, :, 0:S]
        g.dma_start(bias[:], skewed).then_inc(bias_ready, 16)
        g.wait_ge(params_in, 16)

        def merge(turn, i):
            g.wait_ge(prod_ready, turn + 1)
            G.tensor_tensor(merged[:, bass.ds(4 * i, 4), :], merged[:, bass.ds(4 * i, 4), :], ev[:],
                            ALU.add).then_inc(merged_done, 1)

        with g.Fori(0, L) as l:
            g.wait_ge(piece_lo, l * PIECES + FREE)
            G.tensor_copy(par[:], par_all[:, bass.ds(l * NPAR, NPAR)]).then_inc(par_ready, 1)
            g.wait_ge(g_ready, l + 1)
            G.tensor_tensor(c_sq[:], first[:, 1:7], first[:, 1:7], ALU.mult)
            g.drain()
            G.tensor_tensor(c_sq[:, 0], c_sq[:, 0], c_sq[:, 1], ALU.add)
            G.tensor_tensor(c_sq[:, 2:4], c_sq[:, 2:4], c_sq[:, 4:6], ALU.add)
            g.drain()
            G.tensor_tensor(c_sq[:, 2], c_sq[:, 2], c_sq[:, 3], ALU.add).then_inc(c_squares, 1)
            with g.Fori(0, 4) as i:
                n = g.snap(l * 4 + i)
                g.wait_ge(acc_free, l * STRIPS + (BEFORE[G_H] + 4))
                g.wait_ge(b_pv, n + FREE)
                g.wait_ge(g_cols, l + 1)
                G.tensor_copy(b_v[:], first[:, bass.ds(15 + 2 * i, 2), :]).then_inc(b_vs, 1)
                g.wait_ge(b_out, n + 1)
                G.tensor_copy(hb[:, bass.ds(i, 1)], b_h[:].rearrange("p (o t) s -> p o t s", o=1))
                G.tensor_copy(b_mv[:, bass.ds(i, 1)], mean_var[:].rearrange("p (o t) s -> p o t s", o=1)).then_inc(b_kept, 1)
                g.wait_ge(th_ready, l * 18 + i + 1)
                G.tensor_tensor(th[:], th[:], ones4, ALU.add)
                g.drain()
                G.tensor_tensor(ev[:, 2:4], ev[:, 2:4], th[:, 0:2], ALU.mult)
                g.drain()
                G.tensor_tensor(y_bc[:, 0, bass.ds(2 * i, 2), :], ev[:, 2:4], th[:, 2:4], ALU.mult).then_inc(gated, 1)
            for k in range(2):
                g.wait_ge(th_ready, l * 18 + (4 + k + 1))
                G.tensor_tensor(th[:], th[:], ones4, ALU.add)
                g.drain()
                G.tensor_tensor(y_bc[:, 1, 4 * k:4 * k + 4], ev[:], th[:], ALU.mult).then_inc(gated, 1)
            with g.Fori(0, 4) as i:
                g.wait_ge(acc_free, l * STRIPS + (BEFORE[G_C] + 4))
                g.wait_ge(h_out, l * 16 + 2 * i + FREE)
                G.tensor_copy(c_in[:, 2], lat[:, bass.ds(i, 1), 2, :]).then_inc(c_r_in, 1)
                G.tensor_copy(c_in[:, 0:2], lat[:, bass.ds(i, 1), 0:2, :]).then_inc(c_q_in, 1)
            with g.Fori(0, 2) as n:
                with g.Fori(0, 4) as i:
                    head = g.snap(n * 4 + i)
                    g.wait_ge(acc_free, l * STRIPS + (BEFORE[G_G] + 4))
                    g.wait_ge(h_out, l * 16 + 8 + head + FREE)
                    G.tensor_copy(a_in[:], moba[:, bass.ds(head, 1)].rearrange("p o n s -> p (o n) s")).then_inc(a_staged, 1)
                    merge(l * 12 + head, i)
            with g.Fori(0, 4) as i:
                g.drain()
                merge(l * 12 + 8 + i, i)

    block_cm.__exit__(None, None, None)


def _stream(w_in, w_uq, w_ukv, w_branch, w_out):
    out = np.zeros((TOTAL, P, 2, 512), np.float32)
    n = 0

    def put(m):
        nonlocal n
        k = m.shape[0] // 256
        out[n:n + k, :, :, 0:m.shape[1]] = m.reshape(k, 2, P, m.shape[1]).transpose(0, 2, 1, 3)
        n += k

    for l in range(L):
        w, uq, ukv = w_in[l], w_uq[l], w_ukv[l]
        qa, ka, va, za, qb, kb, vb, ib, fb, ob, zb, cq, ckv, kr, zc, gt = np.cumsum(
            [0, 1024, 1024, 1024, 1024, 512, 512, 1024, 4, 4, 1024, 1024, 512, 256, 64, 1024])

        def cols(at, k=1):
            return w[:, at:at + 128 * k]

        gates = np.zeros((D, P), np.float32)
        gates[:, 0:64] = w[:, kr:kr + 64]
        gates[:, 64:68] = w[:, ib:ib + 4]
        gates[:, 96:100] = w[:, fb:fb + 4]
        put(np.concatenate([gates, cols(ckv, 2)], 1))
        for at in (cq, qb, kb, vb, vb + 512):
            put(cols(at, 4))
        for b in range(4):
            put(np.concatenate([cols(ob + 256 * b, 2), cols(zb + 256 * b, 2)], 1))
        put(cols(zc, 4))
        put(cols(zc + 512, 4))
        for p in range(4):
            a, b = 384 * p, 384 * p + 192
            put(np.concatenate([uq[:, a:a + 128], uq[:, b:b + 128], uq[:, a + 128:a + 192], uq[:, b + 128:b + 192]], 1))
        for p in range(4):
            a, b = 512 * p, 512 * p + 256
            put(np.concatenate([ukv[:, a:a + 128], ukv[:, b:b + 128], ukv[:, a + 128:a + 256], ukv[:, b + 128:b + 256]], 1))
        for h in range(8):
            put(np.concatenate([cols(at + 128 * h) for at in (qa, ka, va, za)], 1))
        for branch in (1, 2, 0):
            for g in range(4):
                put(cols(gt + branch * D + 512 * g, 4))
                put(w_branch[l, branch][:, 512 * g:512 * g + 512])
        for g in range(4):
            put(w_out[l][:, 512 * g:512 * g + 512])
    return out.reshape(TOTAL, P, 1024)


def _constants():
    c = np.zeros((P, 1024), np.float32)
    i = np.arange(P)
    c[:, 0:128] = np.eye(P)
    swap = i ^ 32
    c[swap, 128 + i] = 1.0
    c[:, 384:512] = np.where(i[None, :] > i[:, None], np.float32(NEG), np.float32(0))
    half = 32
    inv = np.float32(10000.0) ** (-np.arange(half, dtype=np.float32) / half)
    ang = np.arange(S, dtype=np.float32)[None, :] * inv.astype(np.float32)[i % half][:, None]
    c[:, 512:768] = np.cos(ang)
    c[:, 768:1024] = np.sin(ang) * np.where(i % 64 < 32, -1, 1)[:, None]
    d = 255 - np.arange(384)
    big = 16 + (np.log(np.maximum(d, 1).astype(np.float32) / 16) / np.log(128 / 16) * 16).astype(np.int32)
    bucket = np.where(d < 0, 32, np.where(d < 16, d, np.minimum(big, 31)))
    onehot = (np.arange(33)[:, None] == bucket[None, :]).astype(np.float32)
    return c, onehot


def kernel(**inputs):
    import concourse.bacc as _bacc
    from concourse.bass_utils import run_bass_kernel_spmd as _run

    f = {k: np.ascontiguousarray(v) for k, v in inputs.items()}
    consts, onehot = _constants()

    def strips(vec):
        return vec.reshape(-1, P).T

    par = np.zeros((P, L * NPAR + DT), np.float32)
    for l in range(L):
        q = par[:, l * NPAR:(l + 1) * NPAR]
        q[:, Q_NG:Q_NG + 16] = strips(f["norm_gain"][l])
        for b in range(4):
            for s in range(2):
                at = Q_CONV + 10 * b + 5 * s
                ch = slice(512 * s + 128 * b, 512 * s + 128 * b + 128)
                q[:, at:at + 4] = f["mlstm_conv_w"][l][:, ch].T
                q[:, at + 4] = f["mlstm_conv_b"][l][ch]
        q[:, Q_ON:Q_ON + 8] = strips(f["mlstm_out_norm"][l])
        q[:, Q_QN:Q_QN + 4] = strips(f["mla_q_norm"][l])
        q[:, Q_KVN:Q_KVN + 2] = strips(f["mla_kv_norm"][l])
        q[64:68, Q_IB] = f["mlstm_i_bias"][l]
        q[96:100, Q_FB] = f["mlstm_f_bias"][l]
    par[:, L * NPAR:] = strips(f["final_norm"])

    arrays = {
        "w": _stream(f["w_in"], f["mla_w_uq"], f["mla_w_ukv"], f["w_branch"], f["w_out"]),
        "xin": np.ascontiguousarray(f["x"][0].T.reshape(DT, P, S).transpose(1, 0, 2)),
        "consts": consts,
        "params": par,
        "table": f["t5_table"],
        "onehot": onehot,
    }
    nc = _bacc.Bacc("TRN2", target_bir_lowering=False, num_devices=1)
    args = [nc.dram_tensor(k, a.shape, F32, kind="ExternalInput").ap() for k, a in arrays.items()]
    args.append(nc.dram_tensor("out_t", (P, DT, S), F32, kind="ExternalOutput").ap())
    build(nc, *args)
    got = _run(nc, [arrays], core_ids=[0]).results[0]["out_t"]
    return np.ascontiguousarray(got.transpose(2, 1, 0).reshape(1, S, D))
```

```python
import numpy as np
import concourse.bass as bass
from concourse import mybir

F32, F32R = mybir.dt.float32, mybir.dt.float32r
ALU, ACT, AX = mybir.AluOpType, mybir.ActivationFunctionType, mybir.AxisListType

P = 128
L = 2
S = 256
D = 2048
DT = D // P
EPS = 1e-6
NEG = -1e30
RING = 4
AHEAD = 3
C_A, C_B, C_H, C_U, C_C, C_G, C_M, C_O = 0, 32, 48, 80, 108, 172, 268, 316
CHUNKS = 348
G_A, G_B, G_H, G_U, G_C, G_G, G_M, G_O = 0, 4, 6, 10, 20, 28, 44, 52
WIDTHS = [4, 3] + [4] * 10 + [3] * 4 + [4] * 40
BEFORE = [sum(WIDTHS[:g]) for g in range(len(WIDTHS) + 1)]
EARLY = [BEFORE[g] - g for g in range(len(WIDTHS) + 1)]
STRIPS, EARLIES = BEFORE[-1], EARLY[-1]
TOTAL = L * CHUNKS + RING
FREE = 1
PC_G, PC_N, PC_Q, PC_KV, PC_Y, PC_M = 0, 8, 16, 17, 18, 24
PIECES = 28
EARLY_PIECES = 6
Q_NG, Q_CONV, Q_ON, Q_QN, Q_KVN, Q_IB, Q_FB, NPAR = 0, 16, 56, 64, 68, 70, 71, 72
A_SCALE = 128 ** -0.5
C_SCALE = 192 ** -0.5
B_SCALE = 128 ** -0.5 / 4
LOG1P = [1 / 15, 1 / 13, 1 / 11, 1 / 9, 1 / 7, 1 / 5, 1 / 3]


def build(nc, w, xin, consts, params, table, onehot, out):
    bias_scratch = nc.dram_tensor("bias_scratch", (8, P * 384), F32).ap()
    x_saved_dram = nc.dram_tensor("x_saved_dram", (P, DT * S), F32).ap()

    base = 16512
    offset = [base]

    def at(name, shape, dtype, where):
        return nc.alloc_sbuf_tensor_at(name, [P, *shape] if isinstance(shape, tuple) else shape, dtype, offset=where)

    def new(name, shape, dtype=F32):
        size = 4 * int(np.prod(shape))
        t = at(name, shape, dtype, offset[0])
        offset[0] += (size + 31) // 32 * 32
        return t

    def region(size):
        where = offset[0]
        offset[0] += size
        return where

    act = new("act", (DT, 512), F32R)
    raw = new("raw", (RING, 2, 512))
    w_hi = new("w_hi", (RING, 2, 512), F32R)
    w_lo = new("w_lo", (RING, 2, 512), F32R)
    r1 = region(32768)
    first = at("first", (23, S), F32, r1)
    hb = at("hb", (4, 2, S), F32, r1 + 24576)
    moba = at("moba", (8, 4, S), F32, r1)
    table_hi = at("table_hi", (8, P), F32R, r1)
    table_lo = at("table_lo", (8, P), F32R, r1 + 16384)
    onehot_r = at("onehot_r", (384,), F32R, r1 + 20480)
    bias_wide = at("bias_wide", (8, 384), F32, r1 + 4096)
    r2 = region(32768)
    lat = at("lat", (4, 7, S), F32, r2)
    y_act = at("y_act", (8, 512), F32R, r2)
    x = at("x", (DT, S), F32, r2)
    merged = at("merged", (DT, S), F32, r2 + 16384)
    x_sq = at("x_sq", (DT, S), F32, r2 + 16384)
    c_sq = at("c_sq", (6, S), F32, r2 + 16384)
    g_diag = at("g_diag", (4, S), F32, r2 + 16384 + 8192)
    y_bc = new("y_bc", (2, 8, S))
    bias = new("bias", (8, S))
    r3 = region(12288)
    gi = [at(f"gi{n}", (S,), F32, r3 + 1024 * n) for n in range(12)]
    qk_conv = at("qk_conv", (2, S), F32, r3)
    qk_tanh = at("qk_tanh", (2, S), F32, r3 + 2048)
    qk = at("qk", (2, S), F32, r3 + 4096)
    b_v = at("b_v", (2, S), F32, r3 + 6144)
    b_h = at("b_h", (2, S), F32, r3 + 8192)
    b_vt = at("b_vt", (2, S), F32, r3 + 10240)
    cq_act = at("cq_act", (4, 512), F32R, r3)
    ckv_act = at("ckv_act", (2, 512), F32R, r3 + 8192)
    c_in = at("c_in", (7, S), F32, r3)
    c_rot = at("c_rot", (2, S), F32, r3 + 7168)
    c_qr = at("c_qr", (S,), F32, r3 + 9216)
    a_in = at("a_in", (4, S), F32, r3)
    sq_sum = at("sq_sum", (2, S), F32, r3)
    sq_new = at("sq_new", (4, S), F32, r3 + 2048)
    onehot_sb = at("onehot_sb", (384,), F32, r3 + 6144)
    table_sb = at("table_sb", (8,), F32, r3 + 8192)
    carry = new("carry", (4, S))
    ev = new("ev", (4, S))
    th = new("th", (4, S))
    tp = region(3072)
    t_log = at("t_log", (384,), F32, tp)
    probs = at("probs", (384,), F32, tp + 1536)
    b_norm = at("b_norm", (2, S), F32, tp)
    c_rstd = at("c_rstd", (2, S), F32, tp)
    probs_t = new("probs_t", (384,))
    v_t = new("v_t", (S,))
    z_tanh = new("z_tanh", (S,))
    z_gate = new("z_gate", (S,))
    kr = new("kr", (S,))
    rstd = new("rstd", (S,))
    const = new("const", (1024,))
    ones = new("ones", (P,))
    par_all = new("par_all", (L * NPAR + DT,))
    par = new("par", (NPAR,))
    b_cols = new("b_cols", (4, 4))
    b_mv = new("b_mv", (4, 2, 2))
    b_var = new("b_var", (8,))
    small = new("small", (32,))
    stats = new("stats", (2, 6))
    mean_var = new("mean_var", (2, 2))
    assert offset[0] <= nc.sbuf_usable_end, offset[0]
    ones4 = ones[:, 0:1].rearrange("p (t s) -> p t s", t=1).to_broadcast([P, 4, S])
    ident, perm = const[:, 0:128], const[:, 128:256]
    mask, cos, sin = const[:, 256:512], const[:, 512:768], const[:, 768:1024]
    row_max, den, den_inv = small[:, 0:2], small[:, 8:10], small[:, 16:18]

    acc = nc.alloc_psum_tensor("acc", [P, 4, 512], F32)
    ps_s = nc.alloc_psum_tensor("ps_s", [P, 512], F32)
    ps_t = nc.alloc_psum_tensor("ps_t", [P, 512], F32)
    ps_o = nc.alloc_psum_tensor("ps_o", [P, 512], F32)
    ps_g = nc.alloc_psum_tensor("ps_g", [P, 512], F32)

    sem = nc.alloc_semaphore
    consts_in, params_in, table_in = sem("consts_in"), sem("params_in"), sem("table_in")
    x_in = [sem(f"x_in{q}") for q in range(4)]
    raw_in = [sem(f"raw_in{r}") for r in range(RING)]
    hi_ready, split_ready, chunk_used = sem("hi_ready"), sem("split_ready"), sem("chunk_used")
    strip_done, carry_ready, acc_free = sem("strip_done"), sem("carry_ready"), sem("acc_free")
    piece_src, piece_hi, piece_lo = sem("piece_src"), sem("piece_hi"), sem("piece_lo")
    table_split, table_ready, bias_mm, bias_sb, bias_ps = (
        sem("table_split"), sem("table_ready"), sem("bias_mm"), sem("bias_sb"), sem("bias_ps"))
    bias_out, bias_ready = sem("bias_out"), sem("bias_ready")
    x_squared, sq_ready, x_normed, first_normed, sums_ready, var_ready, std_ready, rstd_ready = (
        sem("x_squared"), sem("sq_ready"), sem("x_normed"), sem("first_normed"), sem("sums_ready"), sem("var_ready"),
        sem("std_ready"), sem("rstd_ready"))
    par_ready, x_saved, x_back, x_added, gated = (
        sem("par_ready"), sem("x_saved"), sem("x_back"), sem("x_added"), sem("gated"))
    th_ready, prod_ready, merged_done = sem("th_ready"), sem("prod_ready"), sem("merged_done")
    f_abs, f_exp, m_sum, m_exp, g_ready, g_cols = (
        sem("f_abs"), sem("f_exp"), sem("m_sum"), sem("m_exp"), sem("g_ready"), sem("g_cols"))
    b_tap, b_conv, b_tanh, b_vs, b_g, b_log, b_exp, b_s, b_vt_mm, b_sc, b_den, b_pt, b_ptc, b_pv, b_hn, b_out, b_kept = (
        sem(f"b_{n}") for n in ("tap", "conv", "tanh", "vs", "g", "log", "exp", "s", "vt_mm", "sc", "den", "pt", "ptc",
                                "pv", "hn", "out", "kept"))
    c_squares, l_sums, l_var, l_std, n_in, n_t = (
        sem(n) for n in ("c_squares", "l_sums", "l_var", "l_std", "n_in", "n_t"))
    c_r_in, c_q_in, c_kv_in, c_swap, c_rope = sem("c_r_in"), sem("c_q_in"), sem("c_kv_in"), sem("c_swap"), sem("c_rope")
    a_staged = sem("a_staged")
    h_scores, h_max, h_exp, h_probs, h_pt, h_ptc, h_pv, h_out = (
        sem(f"h_{n}") for n in ("scores", "max", "exp", "probs", "pt", "ptc", "pv", "out"))
    stored, final_ready = sem("stored"), sem("final_ready")

    table_wide = table_sb[0:33].rearrange("p (h o) -> p h o", o=1).to_broadcast([33, 8, P])

    def normed(s):
        return (ev, th)[s // 4 % 2][:, s % 4]

    def gain_of(l):
        return lambda s: par_all[:, bass.ds(l * NPAR + s, 1)]

    def own_gain(s):
        return par[:, Q_NG + s:Q_NG + s + 1]

    block_cm = nc.Block()
    block = block_cm.__enter__()

    @block.sync
    def _(sp):
        sp.dma_start(onehot_sb[0:33, :], onehot).then_inc(table_in, 16)
        sp.dma_start(table_sb[0:32, :], table).then_inc(table_in, 16)
        sp.dma_start(par_all[:], params).then_inc(params_in, 16)
        for r in range(RING):
            sp.dma_start(raw[:, r], w[r]).then_inc(raw_in[r], 16)
            for q in ((0, 1), (2, 3), (), ())[r]:
                sp.dma_start(x[:, 4 * q:4 * q + 4], xin[:, 4 * q:4 * q + 4]).then_inc(x_in[q], 16)

        def refill(begin, end):
            with sp.Fori(begin, end) as turn:
                for r in range(RING):
                    sp.wait_ge(split_ready, RING * turn + (r - RING + 1))
                    sp.dma_start(raw[:, r], w[RING * turn + r]).then_inc(raw_in[r], 16)

        refill(1, 3)
        sp.dma_start(const[:], consts).then_inc(consts_in, 16)
        refill(3, 8)
        for q in range(4):
            sp.wait_ge(x_in[q], 16)
        sp.dma_start(x_saved_dram, x[:].rearrange("p t s -> p (t s)")).then_inc(x_saved, 16)
        refill(8, TOTAL // RING)
        for r in range(RING):
            sp.wait_ge(raw_in[r], 16 * (TOTAL // RING))
        for q in range(4):
            sp.wait_ge(final_ready, q + 1)
            sp.dma_start(out[:, 4 * q:4 * q + 4], merged[:, 4 * q:4 * q + 4]).then_inc(stored, 16)
        sp.wait_ge(x_saved, 16 * (L + 1))
        sp.wait_ge(stored, 64)

    @block.tensor
    def _(pe):
        mm = nc.tensor.matmul

        def chunk(c, free, j, operand, k0, begin, end, strips=4):
            slot = j % RING
            pe.wait_ge(split_ready, c + (j + 1))
            for s in range(strips):
                if begin:
                    pe.wait_ge(acc_free, free(s))
                for kk in range(2):
                    mm(acc[:, s, :], w_hi[:, slot, kk, s * P:(s + 1) * P], operand[:, k0 + kk, :],
                       start=begin and kk == 0, stop=False)
                    last = mm(acc[:, s, 0:S], w_lo[:, slot, kk, s * P:(s + 1) * P], operand[:, k0 + kk, 0:S],
                              start=False, stop=end and kk == 1)
                if end and s < strips - 1:
                    last.then_inc(strip_done, 1)
            last.then_inc(chunk_used, 1)

        def after_four(e, group=0):
            return lambda s: e + (4 * group + s + 1)

        def after_layer_group(e0, group):
            def free(s):
                g = max((g for g in range(group) if WIDTHS[g] > s), default=None)
                return e0 + ((s - 4 if g is None else BEFORE[g] + s) + 5)
            return free

        def causal_scores(q, k):
            n = len(q)
            for cols, qs, ks in ((slice(0, 256), slice(128, 256), slice(0, 256)),
                                 (slice(256, 384), slice(0, 128), slice(0, 128))):
                for t in range(n):
                    last = mm(ps_s[:, cols], q[t][:, qs], k[t][:, ks], start=t == 0, stop=t == n - 1)
            return last

        def transpose_probs():
            nc.tensor.transpose(ps_t[:, 0:128], probs[:, 256:384], ident)
            nc.tensor.transpose(ps_t[:, 128:256], probs[:, 0:128], ident)
            return nc.tensor.transpose(ps_t[:, 256:384], probs[:, 128:256], ident)

        def head_scores(q, k, v):
            causal_scores(q, k)
            nc.tensor.transpose(ps_g[:, 0:128], v[:, 0:128], ident)
            nc.tensor.transpose(ps_g[:, 128:256], v[:, 128:256], ident).then_inc(h_scores, 1)

        def head_transposes(count):
            pe.wait_ge(h_probs, count)
            transpose_probs().then_inc(h_pt, 1)

        def head_values(count):
            pe.wait_ge(h_ptc, count)
            mm(ps_o[:, 0:256], v_t[:, 0:128], probs_t[:, 0:256], start=True, stop=False)
            mm(ps_o[:, 128:256], v_t[:, 128:256], probs_t[:, 256:384], start=False, stop=True).then_inc(h_pv, 1)

        def sum_squares(count):
            pe.wait_ge(sq_ready, count)
            mm(ps_g[:, 0:S], ones[:], sq_sum[:, 0], start=True, stop=False)
            mm(ps_g[:, 0:S], ones[:], sq_sum[:, 1], start=False, stop=True).then_inc(sums_ready, 1)

        pe.wait_ge(table_ready, 1)
        for h in range(8):
            bank = acc[:, h, 0:384] if h < 4 else (ps_s, ps_t, ps_o, ps_g)[h - 4][:, 0:384]
            mm(bank, table_hi[0:33, h, :], onehot_r[0:33, :], start=True, stop=False)
            last = mm(bank, table_lo[0:33, h, :], onehot_r[0:33, :], start=False, stop=True)
            if h < 2:
                last.then_inc((chunk_used, b_pv)[h], FREE)
        last.then_inc(bias_mm, 1)
        pe.wait_ge(bias_sb, 1)
        pe.wait_ge(bias_ps, 1)

        with pe.Fori(0, L) as l:
            pieces = pe.snap(l * PIECES + FREE)
            c = pe.snap(l * CHUNKS + C_A)
            e0 = pe.snap(l * STRIPS)
            for j in range(32):
                pe.wait_ge(piece_lo, pieces + (min(j, 7) + 1 if j < 16 else PC_N + min(j - 16, 7) + 1))
                chunk(c, after_layer_group(e0, j // 8), j, act, 2 * (j % 8), j % 8 == 0, j % 8 == 7,
                      strips=WIDTHS[j // 8])
                if j == 6:
                    sum_squares(l + 1)
            with pe.Fori(0, 2) as i:
                c = pe.snap(l * CHUNKS + C_B + i * 8)
                e = pe.snap(l * STRIPS + BEFORE[G_B] + 4 * i)
                for j in range(8):
                    chunk(c, after_four(e), j, act, 2 * j, j == 0, j == 7)
            pe.wait_ge(g_ready, l + 1)
            for n, rows in enumerate((gi[8], gi[10])):
                for t in range(2):
                    last = mm(ps_t[:, 8 * n + 4 * t:8 * n + 4 * t + 4], rows[0:4, t * P:(t + 1) * P], ident[0:4, 0:4],
                              start=True, stop=True)
            last.then_inc(g_cols, 1)
            with pe.Fori(0, 4) as i:
                c = pe.snap(l * CHUNKS + C_H + i * 8)
                e = pe.snap(l * STRIPS + BEFORE[G_H] + 4 * i)
                n = pe.snap(l * 4 + i)
                for j in range(8):
                    chunk(c, after_four(e), j, act, 2 * j, j == 0, j == 7)
                    if j == 0:
                        mm(ps_g[:, 0:S], ones[0:4, :], g_diag[0:4, i, :], start=True, stop=True).then_inc(b_g, 1)
                    if j == 4:
                        pe.wait_ge(b_vs, n + 1)
                        for t in range(2):
                            for s in range(2):
                                last = nc.tensor.transpose(ps_g[:, t * S + s * P:t * S + (s + 1) * P],
                                                           b_v[:, s, t * P:(t + 1) * P], ident)
                        last.then_inc(b_vt_mm, 1)
                    if j == 3:
                        pe.wait_ge(b_log, n + 1)
                        causal_scores([qk[:, 0]], [qk[:, 1]]).then_inc(b_s, 1)
                    if j == 5:
                        pe.wait_ge(b_sc, n + 1)
                        transpose_probs().then_inc(b_pt, 1)
                    if j == 6:
                        pe.wait_ge(b_ptc, n + 1)
                        mm(ps_o[:, 0:256], probs_t[:, 0:128], b_vt[:, 0], start=True, stop=True)
                        mm(ps_o[:, 256:512], probs_t[:, 128:256], b_vt[:, 0], start=True, stop=False)
                        mm(ps_o[:, 256:512], probs_t[:, 256:384], b_vt[:, 1], start=False, stop=True).then_inc(b_pv, 1)
            c = pe.snap(l * CHUNKS + C_U)
            for j in range(28):
                if j < 16:
                    chunk(c, after_layer_group(e0, G_U + j // 8), j, act, 2 * (j % 8), j % 8 == 0, j % 8 == 7)
                elif j < 24:
                    if j == 16:
                        pe.wait_ge(piece_lo, pieces + PC_Y)
                    chunk(c, after_layer_group(e0, G_U + 2 + (j - 16) // 2), j, cq_act, 2 * (j % 2), j % 2 == 0,
                          j % 2 == 1, strips=3)
                else:
                    chunk(c, after_layer_group(e0, G_U + 6 + j - 24), j, ckv_act, 0, True, True)
                if j == 0:
                    pe.wait_ge(c_squares, l + 1)
                    pe.wait_ge(b_out, l * 4 + 4)
                    mm(ps_g[:, 0:S], ones[:], c_sq[:, 2], start=True, stop=True)
                    mm(ps_g[:, S:2 * S], ones[:], c_sq[:, 0], start=True, stop=True)
                    for half in range(2):
                        rows = slice(64 * half, 64 * half + 64)
                        mm(ps_s[rows, 0:S], perm[0:64, 0:64], first[0:64, 0], start=True, stop=True)
                        last = mm(ps_o[rows, 0:S], ident[0:64, 0:64], first[0:64, 0], start=True, stop=True)
                    last.then_inc(l_sums, 1)
                if j in (8, 10, 12, 14):
                    b = (j - 8) // 2
                    pe.wait_ge(n_in, l * 4 + (b + 1))
                    for s in range(2):
                        for t in range(2):
                            last = nc.tensor.transpose(ps_t[:, s * S + t * P:s * S + (t + 1) * P],
                                                       b_norm[:, t, s * P:(s + 1) * P], ident)
                    last.then_inc(n_t, 1)
            with pe.Fori(0, 4) as i:
                c = pe.snap(l * CHUNKS + C_C + i * 16)
                e = pe.snap(l * STRIPS + BEFORE[G_C] + 8 * i)
                n = pe.snap(l * 4 + i)
                h = pe.snap(l * 16 + 2 * i)
                for j in range(16):
                    chunk(c, after_four(e, j // 8), j, act, 2 * (j % 8), j % 8 == 0, j % 8 == 7)
                    if j == 2:
                        pe.wait_ge(c_r_in, n + 1)
                        mm(ps_g[:, S:2 * S], perm, c_in[:, 2], start=True, stop=True).then_inc(c_swap, 1)
                    if j in (4, 10):
                        u = j // 10
                        if u == 0:
                            pe.wait_ge(c_rope, n + 1)
                            pe.wait_ge(c_q_in, n + 1)
                            pe.wait_ge(c_kv_in, n + 1)
                        rot = slice(64 * u, 64 * u + 64)
                        head_scores([c_in[:, u], c_qr[rot]], [c_in[:, 3 + u], kr[rot]], c_in[:, 5 + u])
                    if j in (7, 13):
                        head_transposes(h + ((j - 7) // 6 + 1))
                    if j in (8, 14):
                        head_values(h + ((j - 8) // 6 + 1))
            def gate_and_branch(c, e, j):
                if j < 8:
                    chunk(c, after_four(e), j, act, 2 * j, j == 0, j == 7)
                else:
                    chunk(c, after_four(e, 1), j, y_act, 2 * (j - 8), j == 8, j == 11)

            with pe.Fori(0, 2) as n:
                with pe.Fori(0, 4) as i:
                    c = pe.snap(l * CHUNKS + C_G + n * 48 + i * 12)
                    e = pe.snap(l * STRIPS + BEFORE[G_G] + n * 32 + i * 8)
                    h = pe.snap(l * 16 + 8 + n * 4 + i)
                    for j in range(12):
                        if j == 8:
                            pe.wait_ge(piece_lo, pieces + n * 2 + (PC_Y + 2))
                        gate_and_branch(c, e, j)
                        if j == 1:
                            pe.wait_ge(a_staged, l * 8 + n * 4 + i + 1)
                            head_scores([a_in[:, 0]], [a_in[:, 1]], a_in[:, 2])
                        if j == 5:
                            head_transposes(h + 1)
                        if j == 7:
                            head_values(h + 1)
            with pe.Fori(0, 4) as i:
                c = pe.snap(l * CHUNKS + C_M + i * 12)
                e = pe.snap(l * STRIPS + BEFORE[G_M] + i * 8)
                for j in range(12):
                    if j == 8:
                        pe.wait_ge(piece_lo, pieces + (PC_Y + 6))
                    gate_and_branch(c, e, j)
            with pe.Fori(0, 4) as i:
                c = pe.snap(l * CHUNKS + C_O + i * 8)
                e = pe.snap(l * STRIPS + BEFORE[G_O] + 4 * i)
                for j in range(8):
                    if j % 2 == 0:
                        pe.wait_ge(piece_lo, pieces + (PC_M + j // 2 + 1))
                    chunk(c, after_four(e), j, act, 2 * j, j == 0, j == 7)
        sum_squares(L + 1)

    @block.scalar
    def _(a):
        def split_ahead(c, j):
            m = j + AHEAD
            a.wait_ge(raw_in[m % RING], 4 * c + (16 * (m // RING) + 16))
            a.wait_ge(chunk_used, c + j + FREE)
            nc.scalar.activation(w_hi[:, m % RING], raw[:, m % RING], ACT.Copy).then_inc(hi_ready, 1)

        def empty(c, early, j, strips=4):
            for s in range(strips):
                if s < strips - 1:
                    a.wait_ge(strip_done, early + (s + 1))
                else:
                    a.wait_ge(chunk_used, c + (j + 1) + FREE)
                nc.scalar.copy(carry[:, s], acc[:, s, S:2 * S]).then_inc(carry_ready, 1)

        def gate_tanh(e):
            a.wait_ge(acc_free, e + 8)
            nc.scalar.activation(th[:], ev[:], ACT.Tanh, scale=0.5).then_inc(th_ready, 1)

        def piece(dst, src, scale=1.0):
            nc.scalar.activation(dst, src, ACT.Copy, scale=scale).then_inc(piece_hi, 1)

        def head_vt(count, z=None):
            a.wait_ge(h_scores, count)
            if z is not None:
                nc.scalar.activation(z_tanh[:], z, ACT.Tanh, scale=0.5)
            nc.scalar.copy(v_t[:], ps_g[:, 0:S])

        def exps(bias0, bias1, scale, done, sums):
            kw = ({}, {}) if not sums else (dict(accum_out=den[:, 1:2]), dict(accum_out=den[:, 0:1]))
            nc.scalar.activation(probs[:, 0:256], t_log[:, 0:256], ACT.Exp, bias=bias1, scale=scale, **kw[0])
            nc.scalar.activation(probs[:, 256:384], t_log[:, 256:384], ACT.Exp, bias=bias0, scale=scale,
                                 **kw[1]).then_inc(done, 1)

        def head_exp(count):
            a.wait_ge(h_max, count)
            exps(row_max[:, 0:1], row_max[:, 1:2], 1.0, h_exp, True)

        def head_pt(count):
            a.wait_ge(h_pt, count)
            nc.scalar.copy(probs_t[:], ps_t[:, 0:384]).then_inc(h_ptc, 1)

        def gained(k, gain, source):
            for s in range(2 * k, 2 * k + 2):
                last = nc.scalar.activation(act[:, s, 0:S], source(s), ACT.Copy, scale=gain(s))
            last.then_inc(piece_hi, 1)

        a.wait_ge(table_in, 32)
        a.wait_ge(piece_lo, FREE)
        nc.scalar.activation(onehot_r[0:33], onehot_sb[0:33], ACT.Copy)
        nc.scalar.activation(table_hi[0:33], table_wide, ACT.Copy).then_inc(table_split, 1)
        for n in range(AHEAD):
            a.wait_ge(raw_in[n], 16)
            nc.scalar.activation(w_hi[:, n], raw[:, n], ACT.Copy).then_inc(hi_ready, 1)
            if n == 0:
                a.wait_ge(params_in, 16)
            for k in ((0, 1, 2, 3), (4, 5), ())[n]:
                a.wait_ge(x_in[k // 2], 16)
                gained(k, gain_of(0), lambda s: x[:, s])
            if n == 0:
                a.wait_ge(bias_mm, 1)
                for b, bank in enumerate((ps_s, ps_t, ps_o, ps_g)):
                    last = nc.scalar.copy(bias_wide[:, 4 + b], bank[:, 0:384])
                last.then_inc(bias_ps, 1)
        a.wait_ge(x_in[3], 16)
        nc.scalar.activation(x_sq[:], x[:], ACT.Square).then_inc(x_squared, 1)

        with a.Fori(0, L) as l:
            c = a.snap(l * CHUNKS + C_A)
            early = a.snap(l * EARLIES)
            for j in range(32):
                split_ahead(c, j)
                if j < 8 - EARLY_PIECES:
                    gained(j + EARLY_PIECES, gain_of(l), lambda s: x[:, s])
                if j == 8:
                    a.wait_ge(var_ready, l + 1)
                    nc.scalar.activation(rstd[:], rstd[:], ACT.Sqrt).then_inc(std_ready, 1)
                if j % 8 == 7:
                    empty(c, early + EARLY[j // 8], j, strips=WIDTHS[j // 8])
                if j == 12:
                    a.wait_ge(par_ready, l + 1)
                if 12 <= j < 20:
                    k = j - 12
                    a.wait_ge(x_normed, l * 8 + (k + 1))
                    a.wait_ge(chunk_used, c + (8 + k + 1) + FREE)
                    gained(k, own_gain, normed)
                if j == 21:
                    a.wait_ge(f_abs, l + 1)
                    nc.scalar.activation(gi[2][0:4], gi[2][0:4], ACT.Exp, scale=-1.0).then_inc(f_exp, 1)
                if j == 28:
                    a.wait_ge(m_sum, l + 1)
                    nc.scalar.activation(gi[8][0:4], gi[5][0:4], ACT.Copy, scale=-1.0)
                    nc.scalar.activation(gi[10][0:4], gi[9][0:4], ACT.Exp, scale=-1.0).then_inc(m_exp, 1)
            with a.Fori(0, 2) as i:
                c = a.snap(l * CHUNKS + C_B + i * 8)
                for j in range(8):
                    split_ahead(c, j)
                empty(c, l * EARLIES + EARLY[G_B] + 3 * i, 7)
            with a.Fori(0, 4) as i:
                c = a.snap(l * CHUNKS + C_H + i * 8)
                n = a.snap(l * 4 + i)
                cp = a.snap(i * 10 + Q_CONV)
                for j in range(8):
                    if j > 0:
                        split_ahead(c, j)
                    if j == 0:
                        a.wait_ge(acc_free, l * STRIPS + (BEFORE[G_H] + 4))
                        for s in range(2):
                            last = nc.scalar.activation(
                                qk_conv[:, s], first[:, bass.ds(7 + 4 * s + i, 1), :], ACT.Identity,
                                scale=par[:, bass.ds(cp + (5 * s + 3), 1)], bias=par[:, bass.ds(cp + (5 * s + 4), 1)])
                        last.then_inc(b_tap, 1)
                        split_ahead(c, j)
                    if j == 1:
                        a.wait_ge(b_conv, n + 1)
                        nc.scalar.activation(qk_tanh[:], qk_conv[:], ACT.Tanh, scale=0.5).then_inc(b_tanh, 1)
                    if j == 2:
                        a.wait_ge(b_log, n + 1)
                        exps(b_cols[:, 0, bass.ds(i, 1)], b_cols[:, 1, bass.ds(i, 1)], 1.0, b_exp, False)
                    if j == 5:
                        a.wait_ge(b_vt_mm, n + 1)
                        nc.scalar.copy(b_vt[:], ps_g[:].rearrange("p (t s) -> p t s", t=2))
                    if j == 6:
                        a.wait_ge(b_pt, n + 1)
                        nc.scalar.copy(probs_t[:], ps_t[:, 0:384]).then_inc(b_ptc, 1)
                    if j == 7:
                        a.wait_ge(b_den, n + 1)
                        a.wait_ge(b_kept, n + FREE)
                        a.wait_ge(b_pv, n + 1 + FREE)
                        for t in range(2):
                            last = nc.scalar.activation(b_h[:, t], ps_o[:, t * S:(t + 1) * S], ACT.Copy,
                                                        scale=den_inv[:, t:t + 1])
                        last.then_inc(b_hn, 1)
                empty(c, l * EARLIES + EARLY[G_H] + 3 * i, 7)
                gate_tanh(l * STRIPS + BEFORE[G_H] + 4 * i)
            c = a.snap(l * CHUNKS + C_U)
            early = a.snap(l * EARLIES)
            for j in range(28):
                split_ahead(c, j)
                if j < 16 and j % 8 == 7:
                    empty(c, early + EARLY[G_U + j // 8], j)
                    gate_tanh(l * STRIPS + BEFORE[G_U + j // 8])
                if 16 <= j < 24 and j % 2 == 1:
                    empty(c, early + EARLY[G_U + 2 + (j - 16) // 2], j, strips=3)
                if j >= 24:
                    empty(c, early + EARLY[G_U + 6 + j - 24], j)
                if j == 1:
                    a.wait_ge(l_var, l + 1)
                    nc.scalar.activation(c_rstd[:], c_rstd[:], ACT.Sqrt)
                    nc.scalar.activation(b_var[:], b_var[:], ACT.Sqrt).then_inc(l_std, 1)
                if j == 4:
                    a.wait_ge(piece_src, l * 2 + 1)
                    piece(cq_act[:, :, 0:S], ev[:])
                if j == 5:
                    a.wait_ge(piece_src, l * 2 + 2)
                    piece(ckv_act[:, :, 0:S], th[:, 0:2])
            with a.Fori(0, 4) as i:
                c = a.snap(l * CHUNKS + C_C + i * 16)
                early = a.snap(l * EARLIES + EARLY[G_C] + 6 * i)
                n = a.snap(l * 4 + i)
                h = a.snap(l * 16 + 2 * i)
                for j in range(16):
                    split_ahead(c, j)
                    if j % 8 == 7:
                        empty(c, early + 3 * (j // 8), j)
                    if j == 0:
                        a.wait_ge(acc_free, l * STRIPS + (BEFORE[G_C] + 4))
                        a.wait_ge(h_out, h + FREE)
                        nc.scalar.copy(c_in[:, 3:7], lat[:, bass.ds(i, 1), 3:7, :].rearrange("p o n s -> p (o n) s")).then_inc(c_kv_in, 1)
                    for u in range(2):
                        s = 4 + 6 * u
                        if j == s + 1:
                            head_vt(h + (u + 1))
                            head_exp(h + (u + 1))
                        if j == s + 4:
                            head_pt(h + (u + 1))
            with a.Fori(0, 2) as n:
                a.wait_ge(h_out, l * 16 + 8 + FREE)
                a.wait_ge(chunk_used, l * CHUNKS + C_G + n * 48 + FREE)
                for q in range(2):
                    piece(y_act[:, 4 * q:4 * q + 4, 0:S], y_bc[:, n, 4 * q:4 * q + 4, :])
                with a.Fori(0, 4) as i:
                    c = a.snap(l * CHUNKS + C_G + n * 48 + i * 12)
                    early = a.snap(l * EARLIES + EARLY[G_G] + n * 24 + i * 6)
                    h = a.snap(l * 16 + 8 + n * 4 + i)
                    for j in range(12):
                        split_ahead(c, j)
                        if j == 7:
                            empty(c, early, 7)
                            gate_tanh(l * STRIPS + BEFORE[G_G] + n * 32 + i * 8)
                        if j == 11:
                            empty(c, early + 3, 11)
                        if j == 2:
                            head_vt(h + 1, a_in[:, 3])
                            head_exp(h + 1)
                        if j == 6:
                            head_pt(h + 1)
            a.wait_ge(h_out, l * 16 + 16 + FREE)
            a.wait_ge(chunk_used, l * CHUNKS + C_M + FREE)
            for q in range(2):
                piece(y_act[:, 4 * q:4 * q + 4, 0:S], moba[:, 4 * q:4 * q + 4, 3, :])

            def moba_gate_and_branch(i, merging):
                c = a.snap(l * CHUNKS + C_M + i * 12)
                early = a.snap(l * EARLIES + EARLY[G_M] + i * 6)
                for j in range(12):
                    split_ahead(c, j)
                    if j == 7:
                        empty(c, early, 7)
                        gate_tanh(l * STRIPS + BEFORE[G_M] + i * 8)
                    if j == 11:
                        empty(c, early + 3, 11)
                    if merging and 8 <= j < 11:
                        if j == 8:
                            a.wait_ge(merged_done, l * 12 + 11 + FREE)
                            a.wait_ge(chunk_used, c + 8 + FREE)
                        q = j - 8
                        piece(act[:, 4 * q:4 * q + 4, 0:S], merged[:, 4 * q:4 * q + 4], scale=0.5)

            with a.Fori(0, 3) as i:
                moba_gate_and_branch(i, False)
            moba_gate_and_branch(3, True)
            a.wait_ge(merged_done, l * 12 + 12 + FREE)
            piece(act[:, 12:16, 0:S], merged[:, 12:16], scale=0.5)
            a.wait_ge(chunk_used, l * CHUNKS + C_O + FREE)
            a.wait_ge(x_saved, 16 * l + 16)
            a.dma_start(x[:].rearrange("p t s -> p (t s)"), x_saved_dram).then_inc(x_back, 16)

            def output(i, preparing):
                c = a.snap(l * CHUNKS + C_O + i * 8)
                for j in range(8):
                    split_ahead(c, j)
                    if preparing and 2 <= j < 2 + EARLY_PIECES:
                        gained(j - 2, gain_of(l + 1), lambda s: x[:, s])
                empty(c, l * EARLIES + EARLY[G_O] + 3 * i, 7)
                a.wait_ge(x_added, l * 4 + i + 1)
                nc.scalar.activation(sq_new[:], x[:, bass.ds(4 * i, 4), :], ACT.Square).then_inc(x_squared, 1)

            with a.Fori(0, 3) as i:
                output(i, False)
            output(3, True)
            a.dma_start(x_saved_dram, x[:].rearrange("p t s -> p (t s)")).then_inc(x_saved, 16)
        a.wait_ge(var_ready, L + 1)
        nc.scalar.activation(rstd[:], rstd[:], ACT.Sqrt).then_inc(std_ready, 1)

    @block.vector
    def _(v):
        V = nc.vector

        def split_ahead(c, j):
            m = (j + AHEAD) % RING
            v.wait_ge(hi_ready, c + (j + AHEAD + 1))
            V.tensor_tensor(w_lo[:, m], raw[:, m], w_hi[:, m].bitcast(F32), ALU.subtract).then_inc(split_ready, 1)

        def empty(e, dst, strips=4, free=None):
            v.drain()
            if free is not None:
                v.wait_ge(*free)
            for s in range(strips):
                v.wait_ge(carry_ready, e + (s + 1))
                V.tensor_tensor(dst(s), acc[:, s:s + 1, 0:S], carry[:, s:s + 1], ALU.add).then_inc(acc_free, 1)

        def piece(count, dst, src, hi, scale=None):
            v.wait_ge(piece_hi, count)
            if scale is None:
                V.tensor_tensor(dst, src, hi.bitcast(F32), ALU.subtract).then_inc(piece_lo, 1)
            else:
                V.scalar_tensor_tensor(dst, src, scale, hi.bitcast(F32), ALU.mult, ALU.subtract).then_inc(piece_lo, 1)

        def logits(scale, bias1, bias0, count):
            v.wait_ge(h_scores, count)
            V.scalar_tensor_tensor(t_log[:, 0:256], ps_s[:, 0:256], scale, bias1, ALU.mult, ALU.add)
            V.scalar_tensor_tensor(t_log[:, 256:384], ps_s[:, 256:384], scale, bias0, ALU.mult, ALU.add)
            v.drain()
            V.tensor_reduce(row_max[:, 1:2], t_log[:, 0:256], AX.X, ALU.max, negate=True)
            V.tensor_reduce(row_max[:, 0:1], t_log[:, 256:384], AX.X, ALU.max, negate=True).then_inc(h_max, 1)

        def norm_probs(count, z, tanh):
            v.wait_ge(h_exp, count)
            V.reciprocal(den_inv, den)
            if z is not None:
                V.scalar_tensor_tensor(z_gate[:], tanh, 1.0, z, ALU.add, ALU.mult)
            v.drain()
            V.tensor_scalar(probs[:, 0:256], probs[:, 0:256], den_inv[:, 1:2], 0.5, ALU.mult, ALU.mult)
            V.tensor_scalar(probs[:, 256:384], probs[:, 256:384], den_inv[:, 0:1], 0.5, ALU.mult,
                            ALU.mult).then_inc(h_probs, 1)

        def norm_stats(count):
            v.wait_ge(sums_ready, count)
            V.tensor_scalar(rstd[:], ps_g[:, 0:S], 1.0 / D, EPS, ALU.mult, ALU.add).then_inc(var_ready, 1)
            v.wait_ge(std_ready, count)
            V.reciprocal(rstd[:], rstd[:])
            v.drain()

        V.memset(ones[:], 1.0).then_inc(h_out, FREE)
        V.memset(table_sb[32:33], NEG).then_inc(piece_lo, FREE)
        v.wait_ge(table_split, 1)
        V.tensor_tensor(table_lo[0:33], table_wide, table_hi[0:33].bitcast(F32), ALU.subtract).then_inc(table_ready, 1)

        def gained_low(k, gain, source, count):
            v.wait_ge(piece_hi, count)
            for s in range(2 * k, 2 * k + 2):
                last = V.scalar_tensor_tensor(act[:, s, S:2 * S], source(s), gain(s),
                                              act[:, s, 0:S].bitcast(F32), ALU.mult, ALU.subtract)
            last.then_inc(piece_lo, 1)

        for n in range(AHEAD):
            v.wait_ge(hi_ready, n + 1)
            V.tensor_tensor(w_lo[:, n], raw[:, n], w_hi[:, n].bitcast(F32), ALU.subtract).then_inc(split_ready, 1)
            for k in ((0, 1, 2, 3), (4, 5), ())[n]:
                gained_low(k, gain_of(0), lambda s: x[:, s], k + 1)
            if n == 0:
                v.wait_ge(bias_mm, 1)
                V.tensor_copy(bias_wide[:, 0:4], acc[:, :, 0:384]).then_inc(bias_sb, 1)
                for _ in range(4):
                    v.drain()
                    V.memset(stats[:], 0.0).then_inc(acc_free, 1)

        with v.Fori(0, L) as l:
            pieces = v.snap(l * PIECES)
            e0 = v.snap(l * STRIPS)
            c = v.snap(l * CHUNKS + C_A)
            f_in, i_in, e_f, u_f, r_f, z_f, z2, ser, _, m_b, _, one4 = (t[0:4, :] for t in gi)
            for j in range(32):
                if j % 8 == 7:
                    place = (3, 0, 7, 11)[j // 8]
                    empty(e0 + BEFORE[j // 8], lambda s: first[:, place + s:place + s + 1],
                          strips=WIDTHS[j // 8])
                split_ahead(c, j)
                if j < 8 - EARLY_PIECES:
                    k = j + EARLY_PIECES
                    gained_low(k, gain_of(l), lambda s: x[:, s], pieces + (k + 1))
                if j == 8:
                    v.wait_ge(sums_ready, l + 1)
                    V.tensor_scalar(rstd[:], ps_g[:, 0:S], 1.0 / D, EPS, ALU.mult, ALU.add).then_inc(var_ready, 1)
                if j == 9:
                    v.wait_ge(std_ready, l + 1)
                    V.reciprocal(rstd[:], rstd[:]).then_inc(rstd_ready, 1)
                    v.wait_ge(par_ready, l + 1)
                if 12 <= j < 20:
                    gained_low(j - 12, own_gain, normed, pieces + (8 + j - 12 + 1))
                if j == 20:
                    v.drain()
                    v.wait_ge(first_normed, l + 1)
                    V.tensor_scalar(f_in, first[96:100, 0], par[96:100, Q_FB:Q_FB + 1], None, ALU.add)
                    V.tensor_scalar(i_in, first[64:68, 0], par[64:68, Q_IB:Q_IB + 1], None, ALU.add)
                    V.memset(one4, 1.0)
                    v.drain()
                    V.scalar_tensor_tensor(e_f, f_in, -1.0, f_in, ALU.mult, ALU.max).then_inc(f_abs, 1)
                if j == 22:
                    v.wait_ge(f_exp, l + 1)
                    V.tensor_scalar(u_f, e_f, 2.0, None, ALU.add)
                    v.drain()
                    V.reciprocal(r_f, u_f)
                    v.drain()
                    V.tensor_tensor(z_f, e_f, r_f, ALU.mult)
                if j == 24:
                    v.drain()
                    V.tensor_tensor(z2, z_f, z_f, ALU.mult)
                    v.drain()
                    V.tensor_scalar(ser, z2, 1 / 17, None, ALU.mult)
                    for coef in LOG1P[:3]:
                        v.drain()
                        V.scalar_tensor_tensor(ser, ser, coef, z2, ALU.add, ALU.mult)
                if j == 25:
                    for coef in LOG1P[3:]:
                        v.drain()
                        V.scalar_tensor_tensor(ser, ser, coef, z2, ALU.add, ALU.mult)
                    v.drain()
                    V.scalar_tensor_tensor(ser, ser, 1.0, z_f, ALU.add, ALU.mult)
                    V.tensor_scalar(u_f, f_in, 0.0, None, ALU.min)
                if j == 26:
                    v.drain()
                    V.scalar_tensor_tensor(r_f, ser, -2.0, u_f, ALU.mult, ALU.add)
                    v.drain()
                    V.tensor_tensor_scan(z2, one4, r_f, 0.0, ALU.mult, ALU.add)
                if j == 27:
                    v.drain()
                    V.tensor_tensor(e_f, i_in, z2, ALU.subtract)
                    v.drain()
                    V.tensor_tensor_scan(z_f, e_f, e_f, 0.0, ALU.max, ALU.max)
                    v.drain()
                    V.tensor_tensor(m_b, z_f, z2, ALU.add).then_inc(m_sum, 1)
            with v.Fori(0, 2) as i:
                c = v.snap(l * CHUNKS + C_B + i * 8)
                for j in range(8):
                    if j == 7:
                        empty(l * STRIPS + BEFORE[G_B] + 4 * i, lambda s: first[:, bass.ds(15 + 4 * i + s, 1), :])
                    split_ahead(c, j)
            v.wait_ge(g_cols, l + 1)
            V.tensor_copy(b_cols[:], ps_t[:, 0:16].rearrange("p (n h) -> p n h", n=4))
            with v.Fori(0, 4) as i:
                c = v.snap(l * CHUNKS + C_H + i * 8)
                n = v.snap(l * 4 + i)
                cp = v.snap(i * 10 + Q_CONV)
                for j in range(8):
                    if j == 7:
                        empty(l * STRIPS + BEFORE[G_H] + 4 * i, lambda s: ev[:, s:s + 1], free=(gated, l * 6 + i + FREE))
                    if j == 0:
                        v.wait_ge(b_tap, n + 1)
                        for back in range(1, 4):
                            if back > 1:
                                v.drain()
                            for s in range(2):
                                src = first[:, bass.ds(7 + 4 * s + i, 1), 0:S - back]
                                last = V.scalar_tensor_tensor(
                                    qk_conv[:, s, back:S], src, par[:, bass.ds(cp + (5 * s + 3 - back), 1)],
                                    qk_conv[:, s, back:S], ALU.mult, ALU.add)
                        last.then_inc(b_conv, 1)
                    if j == 2:
                        v.wait_ge(b_tanh, n + 1)
                        V.scalar_tensor_tensor(qk[:], qk_tanh[:], 1.0, qk_conv[:], ALU.add, ALU.mult).then_inc(b_log, 1)
                    split_ahead(c, j)
                    if j == 1:
                        v.wait_ge(b_g, n + 1)
                        V.tensor_tensor(t_log[:, 0:256], ps_g[:, 0:256], mask, ALU.add)
                        V.tensor_tensor(t_log[:, 256:384], ps_g[:, 0:128], mask[:, 128:256], ALU.add)
                    if j == 4:
                        v.wait_ge(b_exp, n + 1)
                        v.wait_ge(b_s, n + 1)
                        V.scalar_tensor_tensor(probs[:, 0:256], ps_s[:, 0:256], B_SCALE, probs[:, 0:256],
                                               ALU.mult, ALU.mult, accum_out=den[:, 1:2])
                        V.scalar_tensor_tensor(probs[:, 256:384], ps_s[:, 256:384], B_SCALE, probs[:, 256:384],
                                               ALU.mult, ALU.mult, accum_out=den[:, 0:1]).then_inc(b_sc, 1)
                        v.drain()
                        V.scalar_tensor_tensor(den_inv, den, -1.0, den, ALU.mult, ALU.max)
                        v.drain()
                        V.tensor_tensor(den_inv, den_inv, b_cols[:, 2:4, bass.ds(i, 1)].rearrange("p n o -> p (n o)"),
                                        ALU.max)
                        v.drain()
                        V.reciprocal(den_inv, den_inv).then_inc(b_den, 1)
                    if j == 7:
                        v.wait_ge(b_hn, n + 1)
                        for t in range(2):
                            V.bn_stats(stats[:, t], b_h[:, t])
                        v.drain()
                        for t in range(2):
                            last = V.bn_aggr(mean_var[:, t], stats[:, t])
                        last.then_inc(b_out, 1)
            c = v.snap(l * CHUNKS + C_U)

            def normed_head(b):
                for t in range(2):
                    last = V.tensor_scalar(b_norm[:, t], hb[:, b, t], b_mv[:, b, t, 0:1],
                                           b_var[:, 2 * b + t:2 * b + t + 1], ALU.subtract, ALU.mult)
                last.then_inc(n_in, 1)

            for j in range(28):
                if j < 16 and j % 8 == 7:
                    empty(e0 + BEFORE[G_U + j // 8], lambda s: ev[:, s:s + 1], free=(gated, l * 6 + 4 + j // 8 + FREE))
                if 16 <= j < 24 and j % 2 == 1:
                    p = (j - 16) // 2
                    empty(e0 + BEFORE[G_U + 2 + p], lambda s: lat[:, p, s:s + 1], strips=3, free=(x_saved, 16 * l + 16))
                if j >= 24:
                    empty(e0 + BEFORE[G_U + 6 + j - 24], lambda s: lat[:, j - 24, 3 + s:4 + s])
                split_ahead(c, j)
                if j == 1:
                    v.drain()
                    v.wait_ge(l_sums, l + 1)
                    V.tensor_scalar(c_rstd[:, 0], ps_g[:, 0:S], 1 / 512, EPS, ALU.mult, ALU.add)
                    V.tensor_scalar(c_rstd[:, 1], ps_g[:, S:2 * S], 1 / 256, EPS, ALU.mult, ALU.add)
                    v.wait_ge(b_kept, l * 4 + 4 + FREE)
                    V.tensor_scalar(b_var[:], b_mv[:, :, :, 1:2].rearrange("p b t o -> p (b t o)"), EPS, None,
                                    ALU.add).then_inc(l_var, 1)
                    V.tensor_tensor(z_tanh[:], ps_s[:, 0:S], sin, ALU.mult)
                    V.tensor_tensor(z_gate[:], ps_o[:, 0:S], cos, ALU.mult)
                    v.drain()
                    V.tensor_tensor(kr[:], z_tanh[:], z_gate[:], ALU.add)
                if j == 2:
                    v.drain()
                    v.wait_ge(l_std, l + 1)
                    V.reciprocal(c_rstd[:], c_rstd[:])
                    V.reciprocal(b_var[:], b_var[:])
                    v.drain()
                    V.tensor_scalar(b_var[:], b_var[:], 0.25, None, ALU.mult)
                if j == 3:
                    v.drain()
                    v.wait_ge(gated, l * 6 + 4 + FREE)
                    for s in range(4):
                        last = V.scalar_tensor_tensor(ev[:, s], first[:, 3 + s], par[:, Q_QN + s:Q_QN + s + 1],
                                                      c_rstd[:, 0], ALU.mult, ALU.mult)
                    last.then_inc(piece_src, 1)
                if j == 4:
                    v.drain()
                    for s in range(2):
                        last = V.scalar_tensor_tensor(th[:, s], first[:, 1 + s], par[:, Q_KVN + s:Q_KVN + s + 1],
                                                      c_rstd[:, 1], ALU.mult, ALU.mult)
                    last.then_inc(piece_src, 1)
                    piece(pieces + (PC_Q + 1), cq_act[:, :, S:2 * S], ev[:], cq_act[:, :, 0:S])
                if j == 5:
                    piece(pieces + (PC_KV + 1), ckv_act[:, :, S:2 * S], th[:, 0:2], ckv_act[:, :, 0:S])
                if j == 6:
                    normed_head(0)
                if j in (9, 11, 13, 15):
                    b = (j - 9) // 2
                    v.wait_ge(n_t, l * 4 + (b + 1))
                    for s in range(2):
                        V.scalar_tensor_tensor(y_bc[:, 0, 2 * b + s], ps_t[:, s * S:(s + 1) * S],
                                               par[:, Q_ON + 2 * b + s:Q_ON + 2 * b + s + 1],
                                               y_bc[:, 0, 2 * b + s], ALU.mult, ALU.mult)
                    if b < 3:
                        normed_head(b + 1)
            with v.Fori(0, 4) as i:
                v.wait_ge(gated, l * 6 + 6 + FREE)
                c = v.snap(l * CHUNKS + C_C + i * 16)
                n = v.snap(l * 4 + i)
                h = v.snap(l * 16 + 2 * i)
                for j in range(16):
                    if j % 8 == 7:
                        empty(l * STRIPS + BEFORE[G_C] + 8 * i + 4 * (j // 8),
                              lambda s: moba[:, bass.ds(2 * i + j // 8, 1), s, :])
                    split_ahead(c, j)
                    if j == 3:
                        v.wait_ge(c_swap, n + 1)
                        V.tensor_tensor(c_rot[:, 0], ps_g[:, S:2 * S], sin, ALU.mult)
                        V.tensor_tensor(c_rot[:, 1], c_in[:, 2], cos, ALU.mult)
                        v.drain()
                        V.tensor_tensor(c_qr[:], c_rot[:, 0], c_rot[:, 1], ALU.add).then_inc(c_rope, 1)
                    for u in range(2):
                        s = 4 + 6 * u
                        if j == s + 1:
                            logits(C_SCALE, mask, mask[:, 128:256], h + (u + 1))
                        if j == s + 2:
                            norm_probs(h + (u + 1), None, None)
                        if j == s + 5:
                            v.wait_ge(h_pv, h + (u + 1))
                            y = y_bc[:, 1, bass.ds(2 * i + u, 1), :]
                            V.tensor_tensor(y, ps_o[:, 0:S].rearrange("p (o s) -> p o s", o=1), y, ALU.mult).then_inc(h_out, 1)

            def gate_and_branch(e, turn, j):
                if j == 7:
                    empty(e, lambda s: ev[:, s:s + 1], free=(merged_done, turn + FREE))
                if j == 11:
                    empty(e + 4, lambda s: ev[:, s:s + 1], free=(th_ready, turn + l * 6 + 7))

            def weight():
                v.drain()
                V.scalar_tensor_tensor(ev[:], th[:], 1.0, ev[:], ALU.add, ALU.mult).then_inc(prod_ready, 1)

            with v.Fori(0, 2) as n:
                for q in range(2):
                    strips = slice(4 * q, 4 * q + 4)
                    piece(pieces + n * 2 + (PC_Y + q + 1), y_act[:, strips, S:2 * S], y_bc[:, n, strips, :],
                          y_act[:, strips, 0:S])
                with v.Fori(0, 4) as i:
                    c = v.snap(l * CHUNKS + C_G + n * 48 + i * 12)
                    e = v.snap(l * STRIPS + BEFORE[G_G] + n * 32 + i * 8)
                    turn = v.snap(l * 12 + n * 4 + i)
                    head = v.snap(n * 4 + i)
                    h = v.snap(l * 16 + 8 + n * 4 + i)
                    for j in range(12):
                        gate_and_branch(e, turn, j)
                        split_ahead(c, j)
                        if j == 11:
                            weight()
                        if j == 2:
                            v.wait_ge(bias_ready, 16)
                            logits(A_SCALE, bias[:, bass.ds(head, 1), :].rearrange("p o s -> p (o s)"),
                                   bias[:, bass.ds(head, 1), 128:256].rearrange("p o s -> p (o s)"), h + 1)
                        if j == 3:
                            norm_probs(h + 1, a_in[:, 3], z_tanh[:])
                        if j == 8:
                            v.wait_ge(h_pv, h + 1)
                            V.tensor_tensor(moba[:, bass.ds(head, 1), 3, :], ps_o[:, 0:S].rearrange("p (o s) -> p o s", o=1),
                                            z_gate[:].rearrange("p (o s) -> p o s", o=1), ALU.mult).then_inc(h_out, 1)
            for q in range(2):
                strips = slice(4 * q, 4 * q + 4)
                piece(pieces + (PC_Y + 4 + q + 1), y_act[:, strips, S:2 * S], moba[:, strips, 3, :], y_act[:, strips, 0:S])

            def merged_low(q):
                strips = slice(4 * q, 4 * q + 4)
                piece(pieces + (PC_M + q + 1), act[:, strips, S:2 * S], merged[:, strips], act[:, strips, 0:S], scale=0.5)

            def moba_gate_and_branch(i, merging):
                c = v.snap(l * CHUNKS + C_M + i * 12)
                e = v.snap(l * STRIPS + BEFORE[G_M] + i * 8)
                turn = v.snap(l * 12 + 8 + i)
                for j in range(12):
                    gate_and_branch(e, turn, j)
                    if j == 11:
                        weight()
                    split_ahead(c, j)
                    if merging and 8 <= j < 11:
                        merged_low(j - 8)

            with v.Fori(0, 3) as i:
                moba_gate_and_branch(i, False)
            moba_gate_and_branch(3, True)
            merged_low(3)
            V.memset(sq_sum[:], 0.0)

            def output(i, preparing):
                c = v.snap(l * CHUNKS + C_O + i * 8)
                for j in range(8):
                    if preparing and 2 <= j < 2 + EARLY_PIECES:
                        gained_low(j - 2, gain_of(l + 1), lambda s: x[:, s], pieces + (PIECES + j - 2 + 1))
                    if j == 7:
                        empty(l * STRIPS + BEFORE[G_O] + 4 * i, lambda s: ev[:, s:s + 1])
                        v.drain()
                        v.wait_ge(x_back, 16 * l + 16)
                        strips = x[:, bass.ds(4 * i, 4), :]
                        V.tensor_tensor(strips, strips, ev[:], ALU.add).then_inc(x_added, 1)
                    split_ahead(c, j)
                for q in range(2):
                    v.wait_ge(x_squared, l * 4 + i + 2)
                    last = V.tensor_tensor(sq_sum[:], sq_sum[:], sq_new[:, 2 * q:2 * q + 2], ALU.add)
                    v.drain()

            with v.Fori(0, 3) as i:
                output(i, False)
            output(3, True)
            V.memset(stats[:], 0.0).then_inc(sq_ready, 1)
        norm_stats(L + 1)
        for q in range(4):
            for s in range(4 * q, 4 * q + 4):
                last = V.scalar_tensor_tensor(merged[:, s], x[:, s], par_all[:, L * NPAR + s:L * NPAR + s + 1], rstd[:],
                                              ALU.mult, ALU.mult)
            last.then_inc(final_ready, 1)

    @block.gpsimd
    def _(g):
        G = nc.gpsimd
        for n, free in enumerate((b_kept, merged_done, gated)):
            G.memset(b_mv[:, n], 0.0).then_inc(free, FREE)
        g.wait_ge(bias_sb, 1)
        g.wait_ge(bias_ps, 1)
        g.dma_start(bias_scratch.rearrange("h (p m) -> p h m", p=P), bias_wide[:]).then_inc(bias_out, 16)
        g.wait_ge(x_squared, 1)
        for n in (8, 4):
            G.tensor_tensor(x_sq[:, 0:n], x_sq[:, 0:n], x_sq[:, n:2 * n], ALU.add)
            g.drain()
        G.tensor_tensor(sq_sum[:], x_sq[:, 0:2], x_sq[:, 2:4], ALU.add).then_inc(sq_ready, 1)
        g.wait_ge(bias_out, 16)
        skewed = bias_scratch[:, 127:127 + P * 383].rearrange("h (p m) -> p h m", m=383)[:, :, 0:S]
        g.dma_start(bias[:], skewed).then_inc(bias_ready, 16)
        g.wait_ge(params_in, 16)

        def merge(turn, i):
            g.wait_ge(prod_ready, turn + 1)
            G.tensor_tensor(merged[:, bass.ds(4 * i, 4), :], merged[:, bass.ds(4 * i, 4), :], ev[:],
                            ALU.add).then_inc(merged_done, 1)

        with g.Fori(0, L) as l:
            g.wait_ge(piece_lo, l * PIECES + FREE)
            G.tensor_copy(par[:], par_all[:, bass.ds(l * NPAR, NPAR)]).then_inc(par_ready, 1)
            for k in range(8):
                if k == 0:
                    g.wait_ge(rstd_ready, l + 1)
                if k >= 4:
                    g.wait_ge(piece_lo, l * PIECES + (8 + k - 4 + 1) + FREE)
                for s in range(2 * k, 2 * k + 2):
                    last = G.tensor_tensor(normed(s), x[:, s], rstd[:], ALU.mult)
                last.then_inc(x_normed, 1)
            g.wait_ge(acc_free, l * STRIPS + (BEFORE[2] + 4))
            for s in range(BEFORE[2]):
                last = G.tensor_tensor(first[:, s], first[:, s], rstd[:], ALU.mult)
            last.then_inc(first_normed, 1)
            g.wait_ge(consts_in, 16)
            g.wait_ge(m_exp, l + 1)
            G.tensor_tensor(g_diag[0:4], gi[2][0:4].rearrange("p (o s) -> p o s", o=1).to_broadcast([4, 4, S]),
                            const[0:4, 0:4].rearrange("p (h o) -> p h o", o=1).to_broadcast([4, 4, S]),
                            ALU.mult).then_inc(g_ready, 1)
            G.tensor_tensor(c_sq[:], first[:, 1:7], first[:, 1:7], ALU.mult)
            g.drain()
            G.tensor_tensor(c_sq[:, 0], c_sq[:, 0], c_sq[:, 1], ALU.add)
            G.tensor_tensor(c_sq[:, 2:4], c_sq[:, 2:4], c_sq[:, 4:6], ALU.add)
            g.drain()
            G.tensor_tensor(c_sq[:, 2], c_sq[:, 2], c_sq[:, 3], ALU.add).then_inc(c_squares, 1)
            with g.Fori(0, 4) as i:
                n = g.snap(l * 4 + i)
                g.wait_ge(acc_free, l * STRIPS + (BEFORE[G_H] + 4))
                g.wait_ge(b_pv, n + FREE)
                g.wait_ge(g_cols, l + 1)
                G.tensor_copy(b_v[:], first[:, bass.ds(15 + 2 * i, 2), :]).then_inc(b_vs, 1)
                g.wait_ge(b_out, n + 1)
                G.tensor_copy(hb[:, bass.ds(i, 1)], b_h[:].rearrange("p (o t) s -> p o t s", o=1))
                G.tensor_copy(b_mv[:, bass.ds(i, 1)], mean_var[:].rearrange("p (o t) s -> p o t s", o=1)).then_inc(b_kept, 1)
                g.wait_ge(th_ready, l * 18 + i + 1)
                G.tensor_tensor(th[:], th[:], ones4, ALU.add)
                g.drain()
                G.tensor_tensor(ev[:, 2:4], ev[:, 2:4], th[:, 0:2], ALU.mult)
                g.drain()
                G.tensor_tensor(y_bc[:, 0, bass.ds(2 * i, 2), :], ev[:, 2:4], th[:, 2:4], ALU.mult).then_inc(gated, 1)
            for k in range(2):
                g.wait_ge(th_ready, l * 18 + (4 + k + 1))
                G.tensor_tensor(th[:], th[:], ones4, ALU.add)
                g.drain()
                G.tensor_tensor(y_bc[:, 1, 4 * k:4 * k + 4], ev[:], th[:], ALU.mult).then_inc(gated, 1)
            with g.Fori(0, 4) as i:
                g.wait_ge(acc_free, l * STRIPS + (BEFORE[G_C] + 4))
                g.wait_ge(h_out, l * 16 + 2 * i + FREE)
                G.tensor_copy(c_in[:, 2], lat[:, bass.ds(i, 1), 2, :]).then_inc(c_r_in, 1)
                G.tensor_copy(c_in[:, 0:2], lat[:, bass.ds(i, 1), 0:2, :]).then_inc(c_q_in, 1)

            def stage(head):
                g.wait_ge(acc_free, l * STRIPS + (BEFORE[G_G] + 4))
                g.wait_ge(h_out, l * 16 + 8 + head + FREE)
                G.tensor_tensor(a_in[:], moba[:, bass.ds(head, 1)].rearrange("p o n s -> p (o n) s"), ones4,
                                ALU.mult).then_inc(a_staged, 1)

            stage(0)
            G.memset(merged[:], 0.0)
            g.drain()
            with g.Fori(0, 4) as i:
                stage(i + 1)
                merge(l * 12 + i, i)
            with g.Fori(0, 3) as i:
                stage(i + 5)
                merge(l * 12 + 4 + i, i)
            g.drain()
            merge(l * 12 + 7, 3)
            with g.Fori(0, 4) as i:
                g.drain()
                merge(l * 12 + 8 + i, i)

    block_cm.__exit__(None, None, None)


def _stream(w_in, w_uq, w_ukv, w_branch, w_out):
    out = np.zeros((TOTAL, P, 2, 512), np.float32)
    n = 0

    def put(m):
        nonlocal n
        k = m.shape[0] // 256
        out[n:n + k, :, :, 0:m.shape[1]] = m.reshape(k, 2, P, m.shape[1]).transpose(0, 2, 1, 3)
        n += k

    for l in range(L):
        w, uq, ukv = w_in[l], w_uq[l], w_ukv[l]
        qa, ka, va, za, qb, kb, vb, ib, fb, ob, zb, cq, ckv, kr, zc, gt = np.cumsum(
            [0, 1024, 1024, 1024, 1024, 512, 512, 1024, 4, 4, 1024, 1024, 512, 256, 64, 1024])

        def cols(at, k=1):
            return w[:, at:at + 128 * k]

        gates = np.zeros((D, P), np.float32)
        gates[:, 0:64] = w[:, kr:kr + 64]
        gates[:, 64:68] = w[:, ib:ib + 4]
        gates[:, 96:100] = w[:, fb:fb + 4]
        put(cols(cq, 4))
        put(np.concatenate([gates, cols(ckv, 2)], 1))
        for at in (qb, kb, vb, vb + 512):
            put(cols(at, 4))
        for b in range(4):
            put(np.concatenate([cols(ob + 256 * b, 2), cols(zb + 256 * b, 2)], 1))
        put(cols(zc, 4))
        put(cols(zc + 512, 4))
        for p in range(4):
            a, b = 384 * p, 384 * p + 192
            put(np.concatenate([uq[:, a:a + 128], uq[:, b:b + 128], uq[:, a + 128:a + 192], uq[:, b + 128:b + 192]], 1))
        for p in range(4):
            a, b = 512 * p, 512 * p + 256
            put(np.concatenate([ukv[:, a:a + 128], ukv[:, b:b + 128], ukv[:, a + 128:a + 256], ukv[:, b + 128:b + 256]], 1))
        for h in range(8):
            put(np.concatenate([cols(at + 128 * h) for at in (qa, ka, va, za)], 1))
        for branch in (1, 2, 0):
            for g in range(4):
                put(cols(gt + branch * D + 512 * g, 4))
                put(w_branch[l, branch][:, 512 * g:512 * g + 512])
        for g in range(4):
            put(w_out[l][:, 512 * g:512 * g + 512])
    return out.reshape(TOTAL, P, 1024)


def _constants():
    c = np.zeros((P, 1024), np.float32)
    i = np.arange(P)
    c[:, 0:128] = np.eye(P)
    swap = i ^ 32
    c[swap, 128 + i] = 1.0
    c[:, 384:512] = np.where(i[None, :] > i[:, None], np.float32(NEG), np.float32(0))
    half = 32
    inv = np.float32(10000.0) ** (-np.arange(half, dtype=np.float32) / half)
    ang = np.arange(S, dtype=np.float32)[None, :] * inv.astype(np.float32)[i % half][:, None]
    c[:, 512:768] = np.cos(ang)
    c[:, 768:1024] = np.sin(ang) * np.where(i % 64 < 32, -1, 1)[:, None]
    d = 255 - np.arange(384)
    big = 16 + (np.log(np.maximum(d, 1).astype(np.float32) / 16) / np.log(128 / 16) * 16).astype(np.int32)
    bucket = np.where(d < 0, 32, np.where(d < 16, d, np.minimum(big, 31)))
    onehot = (np.arange(33)[:, None] == bucket[None, :]).astype(np.float32)
    return c, onehot


def kernel(**inputs):
    import concourse.bacc as _bacc
    from concourse.bass_utils import run_bass_kernel_spmd as _run

    f = {k: np.ascontiguousarray(v) for k, v in inputs.items()}
    consts, onehot = _constants()

    def strips(vec):
        return vec.reshape(-1, P).T

    par = np.zeros((P, L * NPAR + DT), np.float32)
    for l in range(L):
        q = par[:, l * NPAR:(l + 1) * NPAR]
        q[:, Q_NG:Q_NG + 16] = strips(f["norm_gain"][l])
        for b in range(4):
            for s in range(2):
                at = Q_CONV + 10 * b + 5 * s
                ch = slice(512 * s + 128 * b, 512 * s + 128 * b + 128)
                q[:, at:at + 4] = f["mlstm_conv_w"][l][:, ch].T
                q[:, at + 4] = f["mlstm_conv_b"][l][ch]
        q[:, Q_ON:Q_ON + 8] = strips(f["mlstm_out_norm"][l])
        q[:, Q_QN:Q_QN + 4] = strips(f["mla_q_norm"][l])
        q[:, Q_KVN:Q_KVN + 2] = strips(f["mla_kv_norm"][l])
        q[64:68, Q_IB] = f["mlstm_i_bias"][l]
        q[96:100, Q_FB] = f["mlstm_f_bias"][l]
    par[:, L * NPAR:] = strips(f["final_norm"])

    arrays = {
        "w": _stream(f["w_in"], f["mla_w_uq"], f["mla_w_ukv"], f["w_branch"], f["w_out"]),
        "xin": np.ascontiguousarray(f["x"][0].T.reshape(DT, P, S).transpose(1, 0, 2)),
        "consts": consts,
        "params": par,
        "table": f["t5_table"],
        "onehot": onehot,
    }
    nc = _bacc.Bacc("TRN2", target_bir_lowering=False, num_devices=1)
    args = [nc.dram_tensor(k, a.shape, F32, kind="ExternalInput").ap() for k, a in arrays.items()]
    args.append(nc.dram_tensor("out_t", (P, DT, S), F32, kind="ExternalOutput").ap())
    build(nc, *args)
    got = _run(nc, [arrays], core_ids=[0]).results[0]["out_t"]
    return np.ascontiguousarray(got.transpose(2, 1, 0).reshape(1, S, D))
```
